# Optimizing a Trainium2 kernel written in Bass

```python
import math
import jax, jax.numpy as jnp
from jax import lax
import numpy as np

D_MODEL = 1024
BATCH = 1
SEQ = 256
DEPTH = 2

RET_HEADS = 4
RET_DK = 256
RET_DV = 512
RET_CHUNK = 128
MLA_HEADS = 8
MLA_NOPE = 128
MLA_ROPE = 64
MLA_V = 128
MLA_Q_RANK = 256
MLA_KV_RANK = 256
ATTN_Q_BLOCK = 128
MOBA_HEADS = 16
MOBA_DH = D_MODEL // MOBA_HEADS
MOBA_BLOCK = 256
MOBA_TOPK = 3
MOBA_Q_CHUNK = 32

ROPE_THETA = 10000.0
LN_EPS = 1e-5
RMS_EPS = 1e-6
NEG = -1e30
DN_ALPHA = (2.0 * DEPTH) ** 0.25
DN_BETA = (8.0 * DEPTH) ** -0.25
N_EVEN = (DEPTH + 1) // 2
N_ODD = DEPTH // 2

RET_W = RET_HEADS * RET_DV
MLA_W = MLA_HEADS * MLA_V
MOBA_W = MOBA_HEADS * MOBA_DH
EVEN_SPLITS = (RET_HEADS * RET_DK, RET_HEADS * RET_DK, RET_W, RET_W,
               MLA_Q_RANK, MLA_KV_RANK, MLA_ROPE, MLA_W)
EVEN_IN = sum(EVEN_SPLITS)
ODD_SPLITS = (MOBA_W, MOBA_W, MOBA_W, MOBA_W)
ODD_IN = sum(ODD_SPLITS)


def _split(h, sizes):
    offs = np.cumsum(sizes)[:-1].tolist()
    return jnp.split(h, offs, axis=-1)

def _heads(t, n):
    B, S, W = t.shape
    return t.reshape(B, S, n, W // n).transpose(0, 2, 1, 3)

def _merge(t):
    B, H, S, d = t.shape
    return t.transpose(0, 2, 1, 3).reshape(B, S, H * d)

def layer_norm(x, g, b):
    xf = x.astype(jnp.float32)
    mu = jnp.mean(xf, -1, keepdims=True)
    xc = xf - mu
    var = jnp.mean(xc * xc, -1, keepdims=True)
    return (xc * lax.rsqrt(var + LN_EPS) * g + b).astype(x.dtype)

def rms_norm(x, g):
    xf = x.astype(jnp.float32)
    return (xf * lax.rsqrt(jnp.mean(xf * xf, -1, keepdims=True) + RMS_EPS) * g).astype(x.dtype)

def rope(x, pos):
    d = x.shape[-1]
    inv = 1.0 / (ROPE_THETA ** (jnp.arange(0, d, 2, dtype=jnp.float32) / d))
    ang = pos.astype(jnp.float32)[:, None, :, None] * inv
    cos, sin = jnp.cos(ang), jnp.sin(ang)
    x1, x2 = x[..., : d // 2], x[..., d // 2:]
    return jnp.concatenate([x1 * cos - x2 * sin, x1 * sin + x2 * cos], -1).astype(x.dtype)

def retnet_rotate(x, pos):
    d = x.shape[-1]
    inv = 1.0 / (ROPE_THETA ** jnp.linspace(0.0, 1.0, d // 2, dtype=jnp.float32))
    ang = pos.astype(jnp.float32)[:, None, :, None] * inv
    cos, sin = jnp.cos(ang), jnp.sin(ang)
    x1, x2 = x[..., 0::2], x[..., 1::2]
    out = jnp.stack([x1 * cos - x2 * sin, x2 * cos + x1 * sin], -1)
    return out.reshape(x.shape).astype(x.dtype)

def retention_chunkwise(q, k, v):
    B, H, S, dk = q.shape
    dv = v.shape[-1]
    C = RET_CHUNK
    n = S // C
    q = q.astype(jnp.float32)
    k = k.astype(jnp.float32) * (dk ** -0.5)
    v = v.astype(jnp.float32)
    log_g = jnp.log(1.0 - 2.0 ** (-5.0 - jnp.arange(H, dtype=jnp.float32)))
    qc = q.reshape(B, H, n, C, dk)
    kc = k.reshape(B, H, n, C, dk)
    vc = v.reshape(B, H, n, C, dv)
    idx = jnp.arange(C, dtype=jnp.float32)
    rel = idx[:, None] - idx[None, :]
    decay = jnp.where(rel >= 0, jnp.exp(log_g[:, None, None] * jnp.maximum(rel, 0.0)), 0.0)
    inner = jnp.einsum('bhncd,bhnkd->bhnck', qc, kc) * decay[None, :, None]
    o_inner = jnp.einsum('bhnck,bhnkv->bhncv', inner, vc)
    zeta = jnp.exp(log_g[:, None] * (C - 1.0 - idx))
    kv_chunk = jnp.einsum('bhnkd,bhnkv->bhndv', kc * zeta[None, :, None, :, None], vc)
    g_chunk = jnp.exp(log_g * C)[None, :, None, None]

    def step(R, kv):
        return R * g_chunk + kv, R

    _, r_prev = lax.scan(step, jnp.zeros((B, H, dk, dv), jnp.float32), jnp.moveaxis(kv_chunk, 2, 0))
    r_prev = jnp.moveaxis(r_prev, 0, 2)
    xi = jnp.exp(log_g[:, None] * (idx + 1.0))
    o_cross = jnp.einsum('bhncd,bhndv->bhncv', qc, r_prev) * xi[None, :, None, :, None]
    return (o_inner + o_cross).reshape(B, H, S, dv)

def head_group_norm(o):
    of = o.astype(jnp.float32)
    mu = jnp.mean(of, -1, keepdims=True)
    oc = of - mu
    var = jnp.mean(oc * oc, -1, keepdims=True)
    return oc * lax.rsqrt(var + LN_EPS)

def causal_attention(q, k, v, scale):
    B, H, S, d = q.shape
    dv = v.shape[-1]
    nq = S // ATTN_Q_BLOCK
    qb = q.reshape(B, H, nq, ATTN_Q_BLOCK, d).transpose(2, 0, 1, 3, 4)
    kpos = jnp.arange(S)

    def one(args):
        qi, i = args
        s = jnp.einsum('bhqd,bhkd->bhqk', qi, k).astype(jnp.float32) * scale
        qpos = i * ATTN_Q_BLOCK + jnp.arange(ATTN_Q_BLOCK)
        s = jnp.where(kpos[None, :] <= qpos[:, None], s, NEG)
        p = jax.nn.softmax(s, axis=-1).astype(v.dtype)
        return jnp.einsum('bhqk,bhkd->bhqd', p, v)

    out = lax.map(one, (qb, jnp.arange(nq)))
    return out.transpose(1, 2, 0, 3, 4).reshape(B, H, S, dv)

def moba_attention(q, k, v):
    B, H, S, dh = q.shape
    L = MOBA_BLOCK
    nb = -(-S // L)
    pad = nb * L - S
    kp = jnp.pad(k, ((0, 0), (0, 0), (0, pad), (0, 0)))
    vp = jnp.pad(v, ((0, 0), (0, 0), (0, pad), (0, 0)))
    kb = kp.reshape(B, H, nb, L, dh)
    vb = vp.reshape(B, H, nb, L, dh)
    kmean = jnp.mean(kb.astype(jnp.float32), axis=3)
    qblk = jnp.arange(S) // L
    gate = jnp.einsum('bhsd,bhnd->bhsn', q.astype(jnp.float32), kmean)
    past = jnp.arange(nb)[None, :] < qblk[:, None]
    gate = jnp.where(past, gate, NEG)
    k_sel = min(MOBA_TOPK, nb)
    _, sel = lax.top_k(gate, k_sel)
    valid = jnp.arange(k_sel)[None, :] < qblk[:, None]
    scale = dh ** -0.5
    Qc = MOBA_Q_CHUNK
    nc = S // Qc
    qch = jnp.moveaxis(q.reshape(B, H, nc, Qc, dh), 2, 0)
    selch = jnp.moveaxis(sel.reshape(B, H, nc, Qc, k_sel), 2, 0)
    validch = valid.reshape(nc, Qc, k_sel)
    bi = jnp.arange(B)[:, None, None, None]
    hi = jnp.arange(H)[None, :, None, None]

    def one(args):
        qi, si, vi, c = args
        q0 = c * Qc
        qpos = q0 + jnp.arange(Qc)
        own = q0 // L
        kg = kb[bi, hi, si]
        vg = vb[bi, hi, si]
        s_g = jnp.einsum('bhqd,bhqnld->bhqnl', qi, kg).astype(jnp.float32) * scale
        s_g = jnp.where(vi[None, None, :, :, None], s_g, NEG)
        ko = lax.dynamic_slice_in_dim(kp, own * L, L, axis=2)
        vo = lax.dynamic_slice_in_dim(vp, own * L, L, axis=2)
        s_o = jnp.einsum('bhqd,bhld->bhql', qi, ko).astype(jnp.float32) * scale
        kpos = own * L + jnp.arange(L)
        s_o = jnp.where(kpos[None, :] <= qpos[:, None], s_o, NEG)
        s = jnp.concatenate([s_g.reshape(B, H, Qc, k_sel * L), s_o], axis=-1)
        p = jax.nn.softmax(s, axis=-1).astype(v.dtype)
        p_g = p[..., : k_sel * L].reshape(B, H, Qc, k_sel, L)
        p_o = p[..., k_sel * L:]
        return (jnp.einsum('bhqnl,bhqnld->bhqd', p_g, vg)
                + jnp.einsum('bhql,bhld->bhqd', p_o, vo))

    out = lax.map(one, (qch, selch, validch, jnp.arange(nc)))
    return jnp.moveaxis(out, 0, 2).reshape(B, H, S, dh)

def retention_mla_layer(x, pos, w_in, q_norm_g, w_uq, kv_norm_g, w_ukv, w_out):
    B, S, _ = x.shape
    h = x @ w_in
    rq, rk, rv, rg, mq, mkv, mkr, mg = _split(h, EVEN_SPLITS)
    q_r = retnet_rotate(_heads(rq, RET_HEADS), pos)
    k_r = retnet_rotate(_heads(rk, RET_HEADS), pos)
    o_r = head_group_norm(retention_chunkwise(q_r, k_r, _heads(rv, RET_HEADS)))
    ret_out = (_merge(o_r) * jax.nn.silu(rg.astype(jnp.float32))).astype(x.dtype)
    q_m = (rms_norm(mq, q_norm_g) @ w_uq).reshape(B, S, MLA_HEADS, MLA_NOPE + MLA_ROPE).transpose(0, 2, 1, 3)
    q_nope, q_pe = q_m[..., :MLA_NOPE], rope(q_m[..., MLA_NOPE:], pos)
    kv = (rms_norm(mkv, kv_norm_g) @ w_ukv).reshape(B, S, MLA_HEADS, MLA_NOPE + MLA_V).transpose(0, 2, 1, 3)
    k_nope, v_m = kv[..., :MLA_NOPE], kv[..., MLA_NOPE:]
    k_pe = rope(mkr[:, None], pos)
    q_full = jnp.concatenate([q_nope, q_pe], -1)
    k_full = jnp.concatenate([k_nope, jnp.broadcast_to(k_pe, (B, MLA_HEADS, S, MLA_ROPE))], -1)
    o_m = causal_attention(q_full, k_full, v_m, (MLA_NOPE + MLA_ROPE) ** -0.5)
    mla_out = (_merge(o_m) * jax.nn.silu(mg)).astype(x.dtype)
    return jnp.concatenate([ret_out, mla_out], axis=-1) @ w_out

def moba_layer(x, pos, w_in, w_out):
    h = x @ w_in
    q, k, v, g = _split(h, ODD_SPLITS)
    q = rope(_heads(q, MOBA_HEADS), pos)
    k = rope(_heads(k, MOBA_HEADS), pos)
    o = moba_attention(q, k, _heads(v, MOBA_HEADS))
    return (_merge(o) * jax.nn.silu(g)) @ w_out

def first_inputs(seed: int = 0) -> dict:
    key = jax.random.key(seed)
    ks = jax.random.split(key, 16)
    f32 = jnp.float32
    nrm = lambda k, shape, fan_in, gain=1.0: jax.random.normal(k, shape, f32) * (gain * fan_in ** -0.5)
    x = jax.random.normal(ks[0], (BATCH, SEQ, D_MODEL), f32)
    offs = jax.random.randint(ks[1], (BATCH, 1), 0, 1024, dtype=jnp.int32)
    positions = (offs + jnp.arange(SEQ, dtype=jnp.int32)[None, :]).astype(jnp.int32)
    return {
        "x": x,
        "positions": positions,
        "w_in_even": nrm(ks[2], (N_EVEN, D_MODEL, EVEN_IN), D_MODEL),
        "q_norm_even": 1.0 + 0.02 * jax.random.normal(ks[3], (N_EVEN, MLA_Q_RANK), f32),
        "w_uq_even": nrm(ks[4], (N_EVEN, MLA_Q_RANK, MLA_HEADS * (MLA_NOPE + MLA_ROPE)), MLA_Q_RANK),
        "kv_norm_even": 1.0 + 0.02 * jax.random.normal(ks[5], (N_EVEN, MLA_KV_RANK), f32),
        "w_ukv_even": nrm(ks[6], (N_EVEN, MLA_KV_RANK, MLA_HEADS * (MLA_NOPE + MLA_V)), MLA_KV_RANK),
        "w_out_even": nrm(ks[7], (N_EVEN, RET_W + MLA_W, D_MODEL), RET_W + MLA_W, DN_BETA),
        "w_in_odd": nrm(ks[8], (N_ODD, D_MODEL, ODD_IN), D_MODEL),
        "w_out_odd": nrm(ks[9], (N_ODD, MOBA_W, D_MODEL), MOBA_W, DN_BETA),
        "ln_g": 1.0 + 0.02 * jax.random.normal(ks[10], (DEPTH, D_MODEL), f32),
        "ln_b": 0.02 * jax.random.normal(ks[11], (DEPTH, D_MODEL), f32),
    }

def first_block(x, positions, w_in_even, q_norm_even, w_uq_even, kv_norm_even, w_ukv_even,
              w_out_even, w_in_odd, w_out_odd, ln_g, ln_b):
    for i in range(DEPTH):
        j = i // 2
        if i % 2 == 0:
            y = retention_mla_layer(x, positions, w_in_even[j], q_norm_even[j], w_uq_even[j],
                                    kv_norm_even[j], w_ukv_even[j], w_out_even[j])
        else:
            y = moba_layer(x, positions, w_in_odd[j], w_out_odd[j])
        x = layer_norm(DN_ALPHA * x + y, ln_g[i], ln_b[i])
    return x


DEPTH_2 = 1

CHUNK = 64
ATT_HEADS = 8
ATT_HEAD_DIM = 64
ATT_WIDTH = ATT_HEADS * ATT_HEAD_DIM
N_PREV_CHUNKS = 8
BAND_CHUNKS = N_PREV_CHUNKS + 1
REL_CLIP = 256
SSD_HEAD_DIM = 64
SSD_WIDTH = D_MODEL
SSD_HEADS = SSD_WIDTH // SSD_HEAD_DIM
SSD_GROUPS = 2
SSD_STATE = 128
SSD_CONV = 4
SSD_CHUNK = CHUNK
CONV_DIM = SSD_WIDTH + 2 * SSD_GROUPS * SSD_STATE
MIX_WIDTH = ATT_WIDTH + SSD_WIDTH
IN_PROJ = 3 * ATT_WIDTH + SSD_WIDTH + CONV_DIM + SSD_HEADS
SPLITS = [ATT_WIDTH, 2 * ATT_WIDTH, 3 * ATT_WIDTH,
          3 * ATT_WIDTH + SSD_WIDTH,
          3 * ATT_WIDTH + SSD_WIDTH + CONV_DIM]
D_FF = 4 * D_MODEL
EPS = 1e-5


def rmsnorm(x, w):
    xf = x.astype(jnp.float32)
    y = xf * lax.rsqrt(jnp.mean(xf * xf, axis=-1, keepdims=True) + EPS)
    return (y * w.astype(jnp.float32)).astype(x.dtype)

def chunk_band_attention(q, k, v, rel_bias):
    bsz, seq = q.shape[0], q.shape[1]
    nc = seq // CHUNK
    shp = (bsz, nc, CHUNK, ATT_HEADS, ATT_HEAD_DIM)
    q = q.reshape(shp)
    k = k.reshape(shp)
    v = v.reshape(shp)
    pad = ((0, 0), (N_PREV_CHUNKS, 0), (0, 0), (0, 0), (0, 0))
    kp = jnp.pad(k, pad)
    vp = jnp.pad(v, pad)
    kb = jnp.concatenate([kp[:, j:j + nc] for j in range(BAND_CHUNKS)], axis=2)
    vb = jnp.concatenate([vp[:, j:j + nc] for j in range(BAND_CHUNKS)], axis=2)
    scale = ATT_HEAD_DIM ** -0.5
    scores = jnp.einsum('bcqhd,bckhd->bhcqk', q, kb).astype(jnp.float32) * scale
    qi = jnp.arange(CHUNK)[:, None]
    kj = jnp.arange(BAND_CHUNKS * CHUNK)[None, :]
    rel = N_PREV_CHUNKS * CHUNK + qi - kj
    idx = jnp.clip(rel, -REL_CLIP, REL_CLIP) + REL_CLIP
    bias = jnp.transpose(rel_bias.astype(jnp.float32)[idx], (2, 0, 1))
    key_chunk = jnp.arange(nc)[:, None] - N_PREV_CHUNKS + jnp.arange(BAND_CHUNKS)[None, :]
    valid = jnp.repeat(key_chunk >= 0, CHUNK, axis=1)
    scores = scores + bias[None, :, None]
    scores = jnp.where(valid[None, None, :, None, :], scores, -1e30)
    probs = jax.nn.softmax(scores, axis=-1).astype(v.dtype)
    out = jnp.einsum('bhcqk,bckhd->bcqhd', probs, vb)
    return out.reshape(bsz, seq, ATT_WIDTH)

def causal_depthwise_conv(u, w, b):
    out = lax.conv_general_dilated(
        u, w[:, None, :].astype(u.dtype), window_strides=(1,),
        padding=[(SSD_CONV - 1, 0)], dimension_numbers=('NWC', 'WIO', 'NWC'),
        feature_group_count=u.shape[-1])
    return out + b.astype(u.dtype)

def ssd_scan(x, dt, A, Bm, Cm):
    bsz, seq = x.shape[0], x.shape[1]
    nc = seq // SSD_CHUNK
    L = SSD_CHUNK
    r = SSD_HEADS // SSD_GROUPS
    X = (x * dt[..., None]).reshape(bsz, nc, L, SSD_GROUPS, r, SSD_HEAD_DIM)
    a = jnp.moveaxis((dt * A).reshape(bsz, nc, L, SSD_GROUPS, r), 2, -1)
    a_cum = jnp.cumsum(a, axis=-1)
    Bc = Bm.reshape(bsz, nc, L, SSD_GROUPS, SSD_STATE)
    Cc = Cm.reshape(bsz, nc, L, SSD_GROUPS, SSD_STATE)
    tril = jnp.tril(jnp.ones((L, L), dtype=bool))
    seg = a_cum[..., :, None] - a_cum[..., None, :]
    decay_in = jnp.exp(jnp.where(tril, seg, -jnp.inf))
    cb = jnp.einsum('bclgn,bcsgn->bcgls', Cc, Bc)
    y_diag = jnp.einsum('bcgls,bcgrls,bcsgrp->bclgrp', cb, decay_in, X)
    decay_out = jnp.exp(a_cum[..., -1:] - a_cum)
    states = jnp.einsum('bcsgn,bcgrs,bcsgrp->bcgrpn', Bc, decay_out, X)
    chunk_decay = jnp.exp(a_cum[..., -1])

    def step(carry, inp):
        st, dec = inp
        return carry * dec[..., None, None] + st, carry

    init = jnp.zeros_like(states[:, 0])
    _, prev = lax.scan(step, init, (jnp.moveaxis(states, 1, 0), jnp.moveaxis(chunk_decay, 1, 0)))
    prev = jnp.moveaxis(prev, 0, 1)
    y_off = jnp.einsum('bclgn,bcgrpn,bcgrl->bclgrp', Cc, prev, jnp.exp(a_cum))
    return (y_diag + y_off).reshape(bsz, seq, SSD_HEADS, SSD_HEAD_DIM)

def ssd_mixer(z, xbc, dt_raw, conv_w, conv_b, dt_bias, a_log, d_skip, norm_w):
    bsz, seq = z.shape[0], z.shape[1]
    xbc = jax.nn.silu(causal_depthwise_conv(xbc, conv_w, conv_b)).astype(jnp.float32)
    xs = xbc[..., :SSD_WIDTH]
    Bm = xbc[..., SSD_WIDTH:SSD_WIDTH + SSD_GROUPS * SSD_STATE].reshape(bsz, seq, SSD_GROUPS, SSD_STATE)
    Cm = xbc[..., SSD_WIDTH + SSD_GROUPS * SSD_STATE:].reshape(bsz, seq, SSD_GROUPS, SSD_STATE)
    dt = jax.nn.softplus(dt_raw.astype(jnp.float32) + dt_bias.astype(jnp.float32))
    A = -jnp.exp(a_log.astype(jnp.float32))
    xh = xs.reshape(bsz, seq, SSD_HEADS, SSD_HEAD_DIM)
    y = ssd_scan(xh, dt, A, Bm, Cm) + d_skip.astype(jnp.float32)[:, None] * xh
    y = y.reshape(bsz, seq, SSD_WIDTH) * jax.nn.silu(z.astype(jnp.float32))
    yg = y.reshape(bsz, seq, SSD_GROUPS, SSD_WIDTH // SSD_GROUPS)
    yg = yg * lax.rsqrt(jnp.mean(yg * yg, axis=-1, keepdims=True) + EPS)
    y = yg.reshape(bsz, seq, SSD_WIDTH) * norm_w.astype(jnp.float32)
    return y.astype(z.dtype)

def second_inputs(seed: int = 0) -> dict:
    key = jax.random.key(seed)
    ks = jax.random.split(key, 16)
    f32 = jnp.float32
    x = jax.random.normal(ks[0], (BATCH, SEQ, D_MODEL), f32)
    norm_mix_w = 1.0 + 0.05 * jax.random.normal(ks[1], (DEPTH_2, D_MODEL), f32)
    w_in = jax.random.normal(ks[2], (DEPTH_2, D_MODEL, IN_PROJ), f32) * D_MODEL ** -0.5
    rel_bias = 0.1 * jax.random.normal(ks[3], (DEPTH_2, 2 * REL_CLIP + 1, ATT_HEADS), f32)
    conv_w = jax.random.normal(ks[4], (DEPTH_2, SSD_CONV, CONV_DIM), f32) * SSD_CONV ** -0.5
    conv_b = 0.01 * jax.random.normal(ks[5], (DEPTH_2, CONV_DIM), f32)
    dt0 = jnp.exp(jax.random.uniform(ks[6], (DEPTH_2, SSD_HEADS), f32,
                                     minval=np.log(1e-3), maxval=np.log(1e-1)))
    dt_bias = dt0 + jnp.log(-jnp.expm1(-dt0))
    a_log = jnp.log(jax.random.uniform(ks[7], (DEPTH_2, SSD_HEADS), f32, minval=1.0, maxval=16.0))
    d_skip = 1.0 + 0.1 * jax.random.normal(ks[8], (DEPTH_2, SSD_HEADS), f32)
    ssd_norm_w = 1.0 + 0.05 * jax.random.normal(ks[9], (DEPTH_2, SSD_WIDTH), f32)
    w_out = jax.random.normal(ks[10], (DEPTH_2, MIX_WIDTH, D_MODEL), f32) * MIX_WIDTH ** -0.5
    norm_mlp_w = 1.0 + 0.05 * jax.random.normal(ks[11], (DEPTH_2, D_MODEL), f32)
    w_ff1 = jax.random.normal(ks[12], (DEPTH_2, D_MODEL, D_FF), f32) * D_MODEL ** -0.5
    w_ff2 = jax.random.normal(ks[13], (DEPTH_2, D_FF, D_MODEL), f32) * D_FF ** -0.5
    norm_final_w = 1.0 + 0.05 * jax.random.normal(ks[14], (D_MODEL,), f32)
    return {"x": x, "norm_mix_w": norm_mix_w, "w_in": w_in, "rel_bias": rel_bias,
            "conv_w": conv_w, "conv_b": conv_b, "dt_bias": dt_bias, "a_log": a_log,
            "d_skip": d_skip, "ssd_norm_w": ssd_norm_w, "w_out": w_out,
            "norm_mlp_w": norm_mlp_w, "w_ff1": w_ff1, "w_ff2": w_ff2,
            "norm_final_w": norm_final_w}

def second_block(x, norm_mix_w, w_in, rel_bias, conv_w, conv_b, dt_bias, a_log, d_skip,
              ssd_norm_w, w_out, norm_mlp_w, w_ff1, w_ff2, norm_final_w):
    h = x
    for i in range(DEPTH_2):
        hn = rmsnorm(h, norm_mix_w[i])
        proj = hn @ w_in[i]
        q, k, v, z, xbc, dt_raw = jnp.split(proj, SPLITS, axis=-1)
        att = chunk_band_attention(q, k, v, rel_bias[i])
        ssd = ssd_mixer(z, xbc, dt_raw, conv_w[i], conv_b[i], dt_bias[i],
                        a_log[i], d_skip[i], ssd_norm_w[i])
        h = h + jnp.concatenate([att, ssd], axis=-1) @ w_out[i]
        hn = rmsnorm(h, norm_mlp_w[i])
        h = h + jnp.square(jax.nn.relu(hn @ w_ff1[i])) @ w_ff2[i]
    return rmsnorm(h, norm_final_w)


def setup_inputs(seed=0):
    out = dict(first_inputs(seed))
    for name, value in second_inputs(seed + 1).items():
        if name != "x":
            out[name + "_2"] = value
    return out


def reference(
    x, positions, w_in_even, q_norm_even, w_uq_even, kv_norm_even, w_ukv_even, w_out_even,
    w_in_odd, w_out_odd, ln_g, ln_b, norm_mix_w_2, w_in_2, rel_bias_2, conv_w_2, conv_b_2,
    dt_bias_2, a_log_2, d_skip_2, ssd_norm_w_2, w_out_2, norm_mlp_w_2, w_ff1_2, w_ff2_2,
    norm_final_w_2,
):
    x = first_block(
        x, positions, w_in_even, q_norm_even, w_uq_even, kv_norm_even, w_ukv_even, w_out_even,
        w_in_odd, w_out_odd, ln_g, ln_b,
    )
    return second_block(
        x, norm_mix_w_2, w_in_2, rel_bias_2, conv_w_2, conv_b_2, dt_bias_2, a_log_2, d_skip_2,
        ssd_norm_w_2, w_out_2, norm_mlp_w_2, w_ff1_2, w_ff2_2, norm_final_w_2,
    )


_drawn_inputs = setup_inputs


def setup_inputs(seed=0):
    import zlib

    import numpy as np

    out = dict(_drawn_inputs(seed))
    spreads = {}
    factors = {'q_norm_even': 8.0, 'kv_norm_even': 8.0, 'rel_bias_2': 8.0, 'conv_b_2': 6.454}
    for name, (base, spread) in spreads.items():
        noise = np.random.default_rng([zlib.crc32(name.encode()), seed]).standard_normal(out[name].shape)
        drawn = base * np.exp(spread * noise) if base else spread * noise
        out[name] = __import__('jax').numpy.asarray(drawn.astype(out[name].dtype))
    for name, factor in factors.items():
        out[name] = (out[name] * factor).astype(out[name].dtype)
    return out
```

```python
from contextlib import ExitStack

import numpy as np

import concourse.bass as bass
from concourse import mybir

F32 = mybir.dt.float32
F32R = mybir.dt.float32r
I32 = mybir.dt.int32
ALU = mybir.AluOpType
ACT = mybir.ActivationFunctionType
AX = mybir.AxisListType.X

P = 128
S = 256
D = 1024
T = S // P
KD = D // P
NCOL = 512
NEG = -1e30
LN_EPS = 1e-5
RMS_EPS = 1e-6
DN_ALPHA = 4.0 ** 0.25

RET_HEADS, RET_DK, RET_DV = 4, 256, 512
MLA_HEADS, NOPE, ROPE = 8, 128, 64
MOBA_HEADS, DH = 16, 64
BAND_HEADS = 8
SSD_HEADS, SSD_P, SSD_N, SSD_G = 16, 64, 128, 2
CONV_DIM = 1536
CONV_TILES = CONV_DIM // P
TAPS = 4
REL_CLIP = 256
D_FF = 4096
FF_CHUNKS = D_FF // NCOL

RQ, RK, RV, RG, MQ, MKR, MG = 0, 1024, 2048, 4096, 6144, 6656, 6720
SQ, SK, SV, SZ, SX, SDT = 0, 512, 1024, 1536, 2560, 4096

C_ID, C_TRI, C_ONES, C_MASK, C_FRET, C_FROPE = 0, 128, 256, 384, 768, 769
C_END = 770
RAW_SLOTS = 3
TWO_PI = 2.0 * np.pi
PI_SAFE = 3.1415925


def shape_tables():
    i = np.arange(P)
    table = np.zeros((P, C_END), np.float32)
    table[:, C_ID:C_ID + P] = np.eye(P)
    table[:, C_TRI:C_TRI + P] = i[:, None] <= i[None, :]
    table[:, C_ONES:C_ONES + P] = 1.0
    causal = np.where(i[None, :] <= i[:, None], 0.0, NEG)
    table[:, C_MASK:C_MASK + P] = causal
    table[:, C_MASK + 2 * P:C_MASK + 3 * P] = causal
    line = np.linspace(0.0, 1.0, P, dtype=np.float32)
    table[:, C_FRET] = np.float32(1.0) / np.power(np.float32(10000.0), line)
    half = np.arange(0, ROPE, 2, dtype=np.float32) / np.float32(ROPE)
    table[:, C_FROPE] = np.tile(np.float32(1.0) / np.power(np.float32(10000.0), half), P // (ROPE // 2))
    decay = np.zeros((P, RET_HEADS, 3, P), np.float32)
    for h in range(RET_HEADS):
        log_g = np.log(1.0 - 2.0 ** (-5.0 - h))
        rel = i[None, :] - i[:, None]
        diag = np.where(rel >= 0, np.exp(log_g * np.maximum(rel, 0)), 0.0)
        decay[:, h, 0] = diag
        decay[:, h, 1] = np.exp(log_g * (rel + P))
        decay[:, h, 2] = diag
    decay *= RET_DK ** -0.5
    return table, decay.reshape(P, -1)


class Piece:

    def __init__(self, chunk, src, nk, k0, cols, order=None, rows=0):
        self.chunk, self.src, self.nk, self.k0, self.cols = chunk, src, nk, k0, cols
        self.order = order
        self.raw = nk * (rows or cols)
        self.size = nk * cols


class Chunk:

    def __init__(self, number, layout, acts, width, epilogue, **info):
        self.n, self.layout, self.acts, self.width, self.epilogue = number, layout, acts, width, epilogue
        self.info = info
        self.pieces = []
        self.banks = None


def plan(w):
    chunks, pieces, steps = [], [], []

    def chunk(layout, acts, width, epilogue, **info):
        c = Chunk(len(chunks), layout, acts, width, epilogue, **info)
        chunks.append(c)
        return c

    def rows(ap, k0, nk, c0, cols):
        return ap[k0 * P:(k0 + nk) * P, c0:c0 + cols].rearrange("(k p) n -> p k n", p=P)

    def load(c, ap, k0, nk, c0, cols=NCOL, order=None, acts_k0=None, src=None, width=None):
        p = Piece(c, src if src is not None else rows(ap, k0, nk, c0, cols), nk,
                  k0 if acts_k0 is None else acts_k0, width or cols, order, cols)
        p.n = len(pieces)
        pieces.append(p)
        c.pieces.append(p)
        steps.append(("piece", p))

    def whole(c, ap, c0, order=None):
        for k0 in range(0, KD, 4):
            load(c, ap, k0, 4, c0, order=order)

    def step(*s):
        steps.append(s)

    step("trig", 0)
    step("turn_x", 0)
    for n, c0 in enumerate((RQ, RQ + NCOL, RK, RK + NCOL)):
        c = chunk("feat", "x", NCOL, "rotate", rot=n, table=0, dst=4 * n)
        whole(c, w["w_in_even"], c0, order="pairs")
        step("epi", c)
    for n in range(4):
        c = chunk("tok", "x", NCOL, "copy_tok", dst=("R1", 2048, n * NCOL))
        whole(c, w["w_in_even"], RV + n * NCOL)
        step("epi", c)
    for h in range(RET_HEADS):
        c = chunk("tok", "x", NCOL, "silu_tok", dst=("R2", 2048, h * NCOL))
        load(c, w["w_in_even"], 0, 4, RG + h * NCOL)
        step("ret_scores", h)
        load(c, w["w_in_even"], 4, 4, RG + h * NCOL)
        step("epi", c)
        if h:
            step("ret_turn", h - 1)
        step("ret_values", h)
    c = chunk("feat", "x", NCOL, "norm_ranks")
    load(c, w["w_in_even"], 0, 4, MQ)
    load(c, w["w_in_even"], 4, 4, MQ)
    step("ret_turn", RET_HEADS - 1)
    step("epi", c)
    ck = chunk("feat", "x", NCOL, "rotate", rot=None, table=1, dst=None)
    load(ck, w["w_in_even"], 0, 8, MKR, ROPE, order="spread", width=2 * P)
    ck.width = 2 * P
    step("epi", ck)
    for n in range(2):
        c = chunk("feat", "x", NCOL, "silu_feat", dst=("R1", n * 1024))
        whole(c, w["w_in_even"], MG + n * NCOL)
        step("epi", c)
    uq = w["w_uq_even"].rearrange("(k p) (h n) -> p k h n", p=P, n=NOPE + ROPE)
    ukv = w["w_ukv_even"].rearrange("(k p) (h n) -> p k h n", p=P, n=2 * NOPE)
    for n in range(2):
        c = chunk("feat", "ranks", NCOL, "copy_feat", dst=("R3", n * 1024))
        load(c, None, 0, 2, 0, src=[uq[:, k, 4 * n:4 * n + 4, 0:NOPE] for k in range(2)], acts_k0=0)
        step("epi", c)
    c = chunk("feat", "ranks", NCOL, "rotate", rot=None, table=1, dst=None)
    load(c, None, 0, 2, 0, src=[uq[:, k, :, NOPE:NOPE + ROPE] for k in range(2)], acts_k0=0, order="halves")
    step("epi", c)
    for n in range(2):
        c = chunk("feat", "ranks", NCOL, "copy_feat", dst=("R3", 2048 + n * 1024))
        load(c, None, 0, 2, 0, src=[ukv[:, k, 4 * n:4 * n + 4, 0:NOPE] for k in range(2)], acts_k0=2)
        step("epi", c)
    for n in range(2):
        c = chunk("tok", "ranks", NCOL, "copy_tok", dst=("R1", 1024, 2048 + n * NCOL))
        load(c, None, 0, 2, 0, src=[ukv[:, k, 4 * n:4 * n + 4, NOPE:] for k in range(2)], acts_k0=2)
        step("epi", c)

    def pipeline(first, count, per_unit, between):
        a0 = first
        for n in range(count + 3):
            if n < count:
                step("scores", a0 + n)
            for f in between.get(n, ()):
                f()
            if 1 <= n <= count:
                step("turn", a0 + n - 1)
            if 2 <= n <= count + 1:
                a = a0 + n - 2
                step("values", a)
                if (a - a0) % per_unit == per_unit - 1:
                    step("gate", UNIT[a])
            if n >= 3 and (n - 3) % per_unit == per_unit - 1:
                step("low", UNIT[a0 + n - 3])

    ys = [chunk("tok", "cat", NCOL, "residual", n=n) for n in range(2)]
    order = [(k0, n) for k0 in range(0, 24, 4) for n in range(2)]
    out_piece = [lambda k0=k0, n=n: load(ys[n], w["w_out_even"], k0, 4, n * NCOL) for k0, n in order]
    pipeline(0, MLA_HEADS, 1, {n: [out_piece[n]] for n in range(8)})
    for f in out_piece[8:]:
        f()
    for c in ys:
        step("epi", c)
    step("layer_norm", 0)
    for n in range(4):
        c = chunk("feat", "x", NCOL, "rotate", rot=n, table=1, dst=4 * n)
        whole(c, w["w_in_odd"], n * NCOL, order="halves")
        step("epi", c)
    for n in range(2):
        c = chunk("tok", "x", NCOL, "copy_tok", dst=("R1", 1024, n * NCOL))
        whole(c, w["w_in_odd"], 2048 + n * NCOL)
        step("epi", c)
    gs = []

    def gate_piece(n, k0):
        if k0 == 0:
            gs.append(chunk("feat", "x", NCOL, "silu_feat", dst=("R1", 2048 + n * 1024)))
        load(gs[n], w["w_in_odd"], k0, 4, 3072 + n * NCOL)
        if k0:
            step("epi", gs[n])

    ys2 = []

    def moba_out(k0, n):
        if len(ys2) <= n:
            ys2.append(chunk("tok", "cat2", NCOL, "residual", n=n))
        load(ys2[n], w["w_out_odd"], k0, 4, n * NCOL)

    gate_piece(0, 0)
    gate_piece(0, 4)
    between = {0: [lambda: gate_piece(1, 0)], 2: [lambda: gate_piece(1, 4)],
               12: [lambda: moba_out(0, 0)], 15: [lambda: moba_out(0, 1)]}
    pipeline(8, MOBA_HEADS, 2, between)
    moba_out(4, 0)
    moba_out(4, 1)
    for c in ys2:
        step("epi", c)
    step("layer_norm", 1)
    step("rms_norm", 0)
    c = chunk("tok", "x", SSD_HEADS, "copy_dt")
    load(c, w["w_in_2"], 0, 8, SDT, SSD_HEADS)
    step("epi", c)
    for n in range(3):
        c = chunk("feat", "x", NCOL, "conv_in", dst=4 * n)
        whole(c, w["w_in_2"], SX + n * NCOL)
        step("epi", c)
        step("conv", n)
    for n in range(2):
        c = chunk("feat", "x", NCOL, "copy_feat", dst=("R3", n * 1024))
        whole(c, w["w_in_2"], SQ + n * NCOL)
        step("epi", c)
    c = chunk("tok", "x", NCOL, "copy_tok", dst=("R3", NCOL, 2048))
    whole(c, w["w_in_2"], SV)
    step("epi", c)
    zs = []

    def z_piece(n, k0):
        if k0 == 0:
            zs.append(chunk("tok", "x", NCOL, "silu_tok", dst=("zb", 1024, n * NCOL)))
        load(zs[n], w["w_in_2"], k0, 4, SZ + n * NCOL)
        if k0:
            step("epi", zs[n])

    pipeline(24, BAND_HEADS, 2, {1: [lambda: z_piece(0, 0)], 3: [lambda: z_piece(0, 4)],
                                 5: [lambda: z_piece(1, 0)], 7: [lambda: z_piece(1, 4)]})
    step("ssd", 0)
    ys3 = [chunk("tok", "cat2", NCOL, "add", n=n) for n in range(2)]
    for k0 in range(0, 12, 4):
        for n in range(2):
            load(ys3[n], w["w_out_2"], k0, 4, n * NCOL)
    for c in ys3:
        step("epi", c)
    step("rms_norm", 1)
    down = [chunk("tok", "ff", NCOL, "add", n=n) for n in range(2)]
    for c in range(FF_CHUNKS + 1):
        if c < FF_CHUNKS:
            u = chunk("feat", "x", NCOL, "relu2", dst=c)
            whole(u, w["w_ff1_2"], c * NCOL)
            step("epi", u)
        if c:
            for n in range(2):
                load(down[n], w["w_ff2_2"], 4 * (c - 1), 4, n * NCOL)
    for c in down:
        step("epi", c)
    step("final", 0)
    return chunks, pieces, steps


UNIT = {a: a if a < 8 else (8 + (a - 8) // 2 if a < 24 else 16 + (a - 24) // 2) for a in range(32)}
LAST_OF_UNIT = {u: max(a for a in UNIT if UNIT[a] == u) for u in range(20)}


def cat_place(u):
    return ("cat", 16 + u) if u < 8 else ("cat2", u - 8 if u < 16 else u - 16)


def build(nc, w, out):
    chunks, pieces, steps = plan(w)
    order = {}
    for s in steps:
        if s[0] == "piece" and s[1].chunk.n not in order:
            order[s[1].chunk.n] = len(order)
    down = [c for c in chunks if c.acts == "ff"]
    turn = 0
    for c in sorted(chunks, key=lambda c: order[c.n]):
        if c in down:
            c.pair, c.turn = 2 + down.index(c), None
        else:
            c.pair, c.turn = turn % 2, turn
            turn += 1
    by_turn = {c.turn: c for c in chunks if c.turn is not None}
    READER = {"copy_tok": "act", "copy_feat": "act", "conv_in": "act", "copy_dt": "dve"}
    reads = {"act": 0, "dve": 0}
    for s in steps:
        if s[0] == "epi":
            c = s[1]
            c.reader = READER.get(c.epilogue, "dve")
            reads[c.reader] += 1
            c.read_count = reads[c.reader]

    with ExitStack() as ctx:
        def sb(name, shape, dt=F32):
            return ctx.enter_context(nc.sbuf_tensor(name, shape, dt))

        def sem(name):
            return ctx.enter_context(nc.semaphore(name))

        cst = sb("cst", [P, C_END])
        raw = sb("raw", [P, RAW_SLOTS, 2048])
        w_hi = sb("w_hi", [P, 2, 2048], F32R)
        w_lo = sb("w_lo", [P, 2, 2048], F32R)
        res = sb("res", [P, T, D])
        x_hi = sb("x_hi", [P, KD, S], F32R)
        x_lo = sb("x_lo", [P, KD, S], F32R)
        R1 = sb("R1", [P, 4096])
        R2 = sb("R2", [P, 4096])
        R3 = sb("R3", [P, 4096])
        tmp = sb("tmp", [P, 2048])
        trig = sb("trig", [P, 2, 2, S])
        probs = sb("probs", [P, 2, 3 * P])
        turned = sb("turned", [P, 2, 3 * P])
        gated = sb("gated", [P, 2, S])
        cols = sb("cols", [P, 64])
        ssd_c = sb("ssd_c", [P, 10, 2 * SSD_HEADS])
        conv_c = sb("conv_c", [P, 5, CONV_TILES])
        stats = sb("stats", [P, 64])
        with nc.sbuf_tensor("cat_hi", [P, 24, S], F32R) as cat_hi, nc.sbuf_tensor("cat_lo", [P, 24, S], F32R) as cat_lo:
            pass
        cat2_hi = sb("cat2_hi", [P, 16, S], F32R)
        cat2_lo = sb("cat2_lo", [P, 16, S], F32R)
        zb = sb("zb", [P, 4096])
        acc = ctx.enter_context(nc.psum_tensor("acc", [P, 4, 2, 512], F32))
        aux = acc[:, 2:4].rearrange("p a b n -> p (a b) n")

        ident = cst[:, C_ID:C_ID + P]
        tri = cst[:, C_TRI:C_TRI + P]
        ones = cst[:, C_ONES:C_ONES + P]
        causal = cst[:, C_MASK:C_MASK + 3 * P]
        decay = tmp[:, 0:RET_HEADS * 3 * P].rearrange("p (h n) -> p h n", h=RET_HEADS)
        region = {"R1": R1, "R2": R2, "R3": R3, "zb": zb}
        qn_col, kvn_col = cols[:, 0:2], cols[:, 2:4]
        ln_g_col, ln_b_col = cols[:, 4:20], cols[:, 20:36]
        mix_col, mlp_col = cols[:, 36:44], cols[:, 44:52]
        ssdn_col = cols[:, 52:60]
        half_neg = cols[:, 60:61]
        acts = {"x": (x_hi, x_lo), "ranks": (cat_hi[:, 20:24], cat_lo[:, 20:24]), "cat": (cat_hi, cat_lo),
                "cat2": (cat2_hi, cat2_lo), "ff": (cat2_hi, cat2_lo)}
        q_pe = R2[:, 0:1024].rearrange("p (g t s) -> p g t s", g=2, t=2)
        k_pe = R2[:, 1024:1536].rearrange("p (t s) -> p t s", t=2)
        bias = zb[:, 2048:4096].rearrange("p (h n) -> p h n", h=BAND_HEADS)
        conv_in = R2[:, 0:CONV_TILES * (S + 3)].rearrange("p (c s) -> p c s", c=CONV_TILES)
        conv_out = R1[:, 0:CONV_TILES * S].rearrange("p (c s) -> p c s", c=CONV_TILES)
        b_T, c_T = conv_out[:, 8:10], conv_out[:, 10:12]
        x_dt = R2[:, 0:2048].rearrange("p (b h n) -> p b h n", b=2, h=SSD_HEADS)
        y_ssd = R2[:, 2048:4096].rearrange("p (b h n) -> p b h n", b=2, h=SSD_HEADS)
        x_far = R1[:, 0:1024].rearrange("p (h n) -> p h n", h=SSD_HEADS)
        y_far = R1[:, 1024:2048].rearrange("p (h n) -> p h n", h=SSD_HEADS)
        cb = R1[:, 3072:3840].rearrange("p (b g n) -> p b g n", b=3, g=2)
        seg = R3[:, :].rearrange("p (b h n) -> p b h n", b=2, h=SSD_HEADS)
        row_a = tmp[:, :].rearrange("p (h n) -> p h n", h=SSD_HEADS)

        raw_landed = [sem(f"raw_landed{i}") for i in range(RAW_SLOTS)]
        names = ("tables_landed", "decay_landed", "x_landed", "pos_landed", "cols_landed", "dt_landed", "conv_landed", "gb_landed", "bias_landed",
                 "out_landed", "hi_ready", "lo_ready", "lo_ready_pool", "piece_used", "acc_read_act",
                 "acc_read_dve", "angles_ready", "trig_ready", "x_turned", "x_hi_ready", "x_lo_ready", "rot_products",
                 "rot_ready", "tanh_ready", "ret_scored", "ret_decayed", "ret_summed", "ret_centred", "ret_var",
                 "ret_rstd", "ret_scaled", "ret_turned", "ret_hi", "ret_lo", "squares_ready", "squares_summed",
                 "mean_square", "rank_rstd", "ranks_scaled", "ranks_hi", "ranks_lo", "scores_ready", "scores_read",
                 "negmax_ready", "exp_ready", "probs_ready", "probs_turned", "turned_copied", "values_ready",
                 "out_read", "cat_hi_ready", "cat_lo_ready", "var_ready", "rstd_ready", "normed_ready", "normed_turned",
                 "scaled_ready", "normed_hi", "normed_lo", "res_ready", "pool_own", "dve_own", "act_own", "pe_own",
                 "conv_read", "conv_tanh", "dt_exp_in", "dt_exp", "dt_ln_in", "dt_ln", "a_ready", "rows_ready", "cums_ready",
                 "seg_rows", "seg_ready", "seg_exp", "m_ready", "cb_ready", "cb_read", "xs_turned", "xs_read", "y_near",
                 "y_far_ready", "y_read", "edge_ready", "edge_exp", "y_gated", "y_sq", "y_rstd", "relu_ready", "ff_hi", "ff_lo",
                 "half_ready", "cols_set", "pad_ready", "final_ready")
        sems = {n: sem(n) for n in names}

        def due(name, value):
            return sems[name], value

        block = ctx.enter_context(nc.Block())

        class Own:

            def __init__(self, eng, name):
                self.eng, self.name, self.counts, self.last = eng, name, {}, None

            def __call__(self, ins, name=None):
                name = name or self.name
                self.counts[name] = self.counts.get(name, 0) + 1
                self.last = (name, self.counts[name])
                ins.then_inc(sems[name], 1)

            def wait(self):
                self.eng.wait_ge(sems[self.last[0]], self.last[1])

        def backwards(h, n):
            return bass.AP(zb, 2048 + h * S + n - 1, [[4096, P], [-1, n]])

        def split_views(p, k0, k1):
            slot = p.n % 2
            r = raw[:, p.n % RAW_SLOTS, k0 * p.raw // p.nk:k1 * p.raw // p.nk]
            parts = [b[:, slot, k0 * p.cols:k1 * p.cols] for b in (w_hi, w_lo)]
            if p.order == "pairs":
                return [(r.rearrange("p (k f t) -> p k t f", t=2, f=P),
                         *[v.rearrange("p (k t f) -> p k t f", t=2, f=P) for v in parts])]
            if p.order == "halves":
                r = r.rearrange("p (g t s) -> p t g s", t=2, s=ROPE // 2)
                parts = [v.rearrange("p (k t h s) -> p t k h s", h=4, t=2, s=ROPE // 2) for v in parts]
                return [(r[:, t], parts[0][:, t], parts[1][:, t]) for t in range(2)]
            if p.order == "spread":
                r = r.rearrange("p (k t s) -> p k t s", k=p.nk, t=2)
                parts = [v.rearrange("p (k t r s) -> p k t r s", k=p.nk, t=2, r=4) for v in parts]
                return [(r, parts[0][:, :, :, c, :], parts[1][:, :, :, c, :]) for c in range(4)]
            return [(r, *parts)]

        def pool_share(p):
            return p.nk == 4

        n_pool = {}
        count = 0
        for p in pieces:
            count += pool_share(p)
            n_pool[p.n] = count
        n_spread = [p.n for p in pieces if p.order == "spread"]

        def hi_prep(eng, own, n):
            p = pieces[n]
            eng.wait_ge(raw_landed[n % RAW_SLOTS], 16 * p.loads)
            if n >= 2:
                eng.wait_ge(*due("piece_used", n - 1))
            for r, hi, _ in split_views(p, 0, p.nk):
                ins = eng.activation(hi, r, ACT.Copy)
            own(ins, "hi_ready")

        def lo_prep(eng, own, n, k0, k1, signal):
            p = pieces[n]
            eng.wait_ge(*due("hi_ready", n + 1))
            eng.wait_ge(raw_landed[n % RAW_SLOTS], 16 * p.loads)
            if n >= 2:
                eng.wait_ge(*due("piece_used", n - 1))
            for r, hi, lo in split_views(p, k0, k1):
                ins = eng.tensor_tensor(lo, r, hi.bitcast(F32), ALU.subtract)
            own(ins, signal)

        loads = [0] * RAW_SLOTS
        for p in pieces:
            srcs = p.src if isinstance(p.src, list) else [p.src]
            loads[p.n % RAW_SLOTS] += len(srcs)
            p.loads = loads[p.n % RAW_SLOTS]
            p.srcs = srcs

        MLA_COPIES = 4 + 2 + 2 + 2
        NORM = {("layer_norm", 0): 0, ("rms_norm", 0): 1, ("rms_norm", 1): 2}
        TURNS = {("layer_norm", 0): 0, ("rms_norm", 0): 4, ("ssd", 0): 8, ("rms_norm", 1): 12}
        Z_READS = max(c.read_count for c in chunks if c.epilogue == "silu_tok")
        tanh_n = {}
        for s in steps:
            if s[0] == "epi" and s[1].epilogue.startswith("silu"):
                tanh_n[s[1].n] = len(tanh_n) + 1
        rot_n = {}
        for s in steps:
            if s[0] == "epi" and s[1].epilogue == "rotate":
                rot_n[s[1].n] = len(rot_n)

        Y_READS = [max(c.read_count for c in chunks if c.epilogue == "residual" and c.acts == a) for a in ("cat", "cat2")]
        ff2_used = {c: max(p.n for p in pieces if p.chunk.acts == "ff" and p.k0 == 4 * c) + 1 for c in range(FF_CHUNKS)}

        def rot_products(n):
            base = 2048 * (n % 2)
            if 4 <= n < 6:
                return tmp[:, :].rearrange("p (q m s) -> p q m s", q=4, m=2)
            return R2[:, base:base + 2048].rearrange("p (q m s) -> p q m s", q=4, m=2)

        def rot_dst(c, n):
            if c.info["dst"] is not None:
                i = c.info["dst"]
                return R3[:, i * S:(i + 4) * S].rearrange("p (m t s) -> p m t s", m=2, t=2)
            return k_pe.rearrange("p (m t) s -> p m t s", m=1) if c.width == 2 * P else q_pe

        by = lambda e, f=None: [c.read_count for c in chunks if c.epilogue == e and (f is None or f(c))]
        GATE_READS = by("silu_feat", lambda c: True)
        GATE_READS = [GATE_READS[1], GATE_READS[2], GATE_READS[3]]
        SSD_READS = max(by("add", lambda c: c.acts == "cat2"))
        FINAL_READS = max(by("add", lambda c: c.acts == "ff"))
        CONV_READS = by("conv_in")

        def epi_dst(c):
            i = c.info["dst"]
            if c.layout == "tok":
                r, width, c0 = i
                if r == "R1" and width == 2048:
                    return R1[:, :].rearrange("p (t n) -> p t n", t=T)[:, :, c0:c0 + NCOL]
                if width == 2048:
                    return region[r][:, :].rearrange("p (t n) -> p t n", t=T)[:, :, c0:c0 + NCOL]
                base = (c0 // 2048) * 2048 if width == 1024 else 2048
                v = region[r][:, base:base + T * width].rearrange("p (t n) -> p t n", t=T)
                return v[:, :, c0 - base:c0 - base + NCOL]
            r, c0 = i
            return region[r][:, c0:c0 + 1024].rearrange("p (b n) -> p b n", b=2)

        @block.sync
        def _(sp):
            sp.dma_start(res[:, :, :], w["x"].rearrange("(t p) n -> p t n", p=P)).then_inc(sems["x_landed"], 16)
            sp.dma_start(cst[:, :], w["tables"]).then_inc(sems["tables_landed"], 16)
            for p in pieces:
                n = p.n
                if n >= RAW_SLOTS:
                    sp.wait_ge(*due("hi_ready", n - RAW_SLOTS + 1))
                    sp.wait_ge(*due("lo_ready", n - RAW_SLOTS + 1))
                    if n_pool[n - RAW_SLOTS]:
                        sp.wait_ge(*due("lo_ready_pool", n_pool[n - RAW_SLOTS]))
                per = p.raw // len(p.srcs)
                for i, src in enumerate(p.srcs):
                    dst = raw[:, n % RAW_SLOTS, i * per:(i + 1) * per]
                    if len(src.shape) == 3:
                        dst = dst.rearrange("p (a b) -> p a b", a=src.shape[1])
                    sp.dma_start(dst, src).then_inc(raw_landed[n % RAW_SLOTS], 16)
            sp.wait_ge(*due("final_ready", 1))
            sp.dma_start(out.rearrange("(t p) n -> p t n", p=P), tmp[:, :].rearrange("p (t n) -> p t n", t=T)).then_inc(sems["out_landed"], 16)
            sp.wait_ge(*due("out_landed", 16))

        @block.tensor
        def _(pe):
            own = Own(pe, "pe_own")

            def ready_acts(c):
                if c.acts == "x":
                    pe.wait_ge(*due("x_hi_ready", state["x"]))
                    pe.wait_ge(*due("x_lo_ready", state["x"]))
                if c.acts == "ranks":
                    pe.wait_ge(*due("ranks_hi", 1))
                    pe.wait_ge(*due("ranks_lo", 1))

            state = {"x": 4}

            def product(p):
                c = p.chunk
                slot = p.n % 2
                hi, lo = acts[c.acts]
                if p is c.pieces[0]:
                    ready_acts(c)
                    if c.turn is not None and c.turn >= 2:
                        before = by_turn[c.turn - 2]
                        pe.wait_ge(*due("acc_read_" + before.reader, before.read_count))
                k_last = p.k0 + p.nk
                if c.acts == "cat":
                    if p.k0 < 16:
                        pe.wait_ge(*due("ret_hi", 8))
                        pe.wait_ge(*due("ret_lo", 8))
                    else:
                        pe.wait_ge(*due("cat_hi_ready", k_last - 16))
                        pe.wait_ge(*due("cat_lo_ready", k_last - 16))
                if c.acts == "cat2":
                    if c.epilogue == "residual":
                        pe.wait_ge(*due("cat_hi_ready", 8 + k_last))
                        pe.wait_ge(*due("cat_lo_ready", 8 + k_last))
                    elif p.k0 == 0:
                        pe.wait_ge(*due("cat_hi_ready", 20))
                        pe.wait_ge(*due("cat_lo_ready", 20))
                    else:
                        pe.wait_ge(*due("normed_hi", 4))
                        pe.wait_ge(*due("normed_lo", 4))
                k_acts = p.k0
                if c.acts == "ff":
                    pe.wait_ge(*due("ff_hi", p.k0 // 4 + 1))
                    pe.wait_ge(*due("ff_lo", p.k0 // 4 + 1))
                    k_acts = p.k0 % 16
                pe.wait_ge(*due("hi_ready", p.n + 1))
                pe.wait_ge(*due("lo_ready", p.n + 1))
                if n_pool[p.n]:
                    pe.wait_ge(*due("lo_ready_pool", n_pool[p.n]))
                wh = w_hi[:, slot, 0:p.size].rearrange("p (k n) -> p k n", k=p.nk)
                wl = w_lo[:, slot, 0:p.size].rearrange("p (k n) -> p k n", k=p.nk)
                first, last = p is c.pieces[0], p is c.pieces[-1]
                for k in range(p.nk):
                    start, stop = first and k == 0, last and k == p.nk - 1
                    ka = k_acts + k
                    if c.layout == "tok":
                        for t in range(T):
                            o = acc[:, c.pair, t, 0:p.cols]
                            xh, xl = hi[:, ka, t * P:(t + 1) * P], lo[:, ka, t * P:(t + 1) * P]
                            pe.matmul(o, xh, wh[:, k, :], start=start, stop=False)
                            pe.matmul(o, xh, wl[:, k, :], start=False, stop=False)
                            ins = pe.matmul(o, xl, wh[:, k, :], start=False, stop=stop)
                    else:
                        for f in range(p.cols // P):
                            o = acc[:, c.pair, f // 2, (f % 2) * S:(f % 2 + 1) * S]
                            fs = slice(f * P, (f + 1) * P)
                            pe.matmul(o, wh[:, k, fs], hi[:, ka, :], start=start and f % 2 == 0, stop=False, skip_group_check=True)
                            pe.matmul(o, wh[:, k, fs], lo[:, ka, :], start=False, stop=False, skip_group_check=True)
                            ins = pe.matmul(o, wl[:, k, fs], hi[:, ka, :], start=False, stop=stop, skip_group_check=True)
                own(ins, "piece_used")

            def turn_tokens(src, per_bank_signal, wait_reads=None):
                for f in range(KD):
                    for t in range(T):
                        ins = pe.transpose(aux[:, f // 2, (f % 2) * S + t * P:(f % 2) * S + (t + 1) * P],
                                           src[:, t, f * P:(f + 1) * P], ident)
                    if f % 2:
                        ins.then_inc(sems[per_bank_signal], 1)

            normed = tmp[:, :].rearrange("p (t n) -> p t n", t=T)
            v_ret = R1[:, :].rearrange("p (t n) -> p t n", t=T)
            norms = [0]
            for s in steps:
                kind, i = s
                if kind == "piece":
                    product(i)
                elif kind == "turn_x":
                    pe.wait_ge(*due("x_landed", 16))
                    pe.wait_ge(*due("tables_landed", 16))
                    turn_tokens(res, "x_turned")
                elif kind == "ret_scores":
                    h = i
                    if h == 0:
                        pe.wait_ge(*due("rot_ready", 4))
                        pe.wait_ge(*due("x_lo_ready", 4))
                    else:
                        pe.wait_ge(*due("ret_decayed", h))
                    q = R3[:, 0:2048].rearrange("p (f s) -> p f s", f=8)
                    k = R3[:, 2048:4096].rearrange("p (f s) -> p f s", f=8)
                    for j, (o0, i0, n) in enumerate(((0, 0, S), (S, P, P))):
                        for t in range(2):
                            ins = pe.matmul(aux[:, 0, o0:o0 + n], k[:, 2 * h + t, j * P:(j + 1) * P],
                                            q[:, 2 * h + t, i0:i0 + n], start=(t == 0), stop=(t == 1))
                    own(ins, "ret_scored")
                elif kind == "ret_values":
                    h = i
                    pe.wait_ge(*due("ret_decayed", h + 1))
                    pe.wait_ge(*due("acc_read_act", 4))
                    if h:
                        pe.wait_ge(*due("ret_centred", h))
                    pr = probs[:, h % 2, :]
                    vs = slice(h * RET_DV, (h + 1) * RET_DV)
                    pe.matmul(aux[:, 2, :], pr[:, 0:P], v_ret[:, 0, vs], start=True, stop=True)
                    pe.matmul(aux[:, 3, :], pr[:, P:2 * P], v_ret[:, 0, vs], start=True, stop=False)
                    pe.matmul(aux[:, 3, :], pr[:, 2 * P:3 * P], v_ret[:, 1, vs], start=False, stop=True).then_inc(sems["ret_summed"], 1)
                elif kind == "ret_turn":
                    h = i
                    gate = R2[:, :].rearrange("p (t n) -> p t n", t=T)
                    pe.wait_ge(*due("ret_scaled", h + 1))
                    for half in range(2):
                        n = 2 * h + half
                        if n:
                            pe.wait_ge(*due("ret_lo", n))
                            pe.wait_ge(*due("ret_hi", n))
                        for f in range(2):
                            for t in range(T):
                                c0 = h * RET_DV + (2 * half + f) * P
                                ins = pe.transpose(aux[:, 1, f * S + t * P:f * S + (t + 1) * P], gate[:, t, c0:c0 + P], ident)
                        own(ins, "ret_turned")
                elif kind == "scores":
                    a = i
                    if a == 0:
                        pe.wait_ge(*due("ret_lo", 8))
                        pe.wait_ge(*due("acc_read_act", MLA_COPIES))
                        pe.wait_ge(*due("rot_ready", 6))
                    if a == 8:
                        pe.wait_ge(*due("rot_ready", 10))
                        pe.wait_ge(*due("acc_read_act", MLA_COPIES + 2))
                    if a == 24:
                        pe.wait_ge(*due("acc_read_act", MLA_COPIES + 2 + 3 + 3))
                    if a >= 2:
                        pe.wait_ge(*due("scores_read", a - 1))
                    bank = aux[:, 3 * (a % 2), :]
                    for o0, q0, n in ((0, 0, P), (P, P, S)):
                        o = bank[:, o0:o0 + n]
                        if a < 8:
                            g, r = a // 4, 32 * (a % 4)
                            qn = R3[:, a * S:(a + 1) * S]
                            kn = R3[:, 2048 + a * S:2048 + (a + 1) * S]
                            pe.matmul(o, qn[:, q0:q0 + P], kn[:, 0:n], start=True, stop=False)
                            for t in range(2):
                                ins = pe.matmul(o, q_pe[r:r + 32, g, t, q0:q0 + P], k_pe[r:r + 32, t, 0:n],
                                                start=False, stop=(t == 1), tile_position=(r, 0))
                        elif a < 24:
                            g, r = (a - 8) // 4, 32 * (a % 4)
                            qk = R3[:, :].rearrange("p (q g t s) -> p q g t s", q=2, g=4, t=2)
                            for t in range(2):
                                ins = pe.matmul(o, qk[r:r + 32, 0, g, t, q0:q0 + P], qk[r:r + 32, 1, g, t, 0:n],
                                                start=(t == 0), stop=(t == 1), tile_position=(r, 0))
                        else:
                            g, r = (a - 24) // 2, 64 * (a % 2)
                            qk = R3[:, 0:2048].rearrange("p (q g s) -> p q g s", q=2, g=4)
                            ins = pe.matmul(o, qk[r:r + 64, 0, g, q0:q0 + P], qk[r:r + 64, 1, g, 0:n],
                                            start=True, stop=True, tile_position=(r, 0))
                    own(ins, "scores_ready")
                elif kind == "turn":
                    a = i
                    pe.wait_ge(*due("probs_ready", a + 1))
                    if a:
                        pe.wait_ge(*due("turned_copied", a))
                    pr = probs[:, a % 2, :]
                    for o0, c0 in ((0, 0), (P, P), (2 * P, 2 * P)):
                        ins = pe.transpose(aux[:, 1, o0:o0 + P], pr[:, c0:c0 + P], ident)
                    own(ins, "probs_turned")
                elif kind == "values":
                    a = i
                    u = UNIT[a]
                    pe.wait_ge(*due("turned_copied", a + 1))
                    if u:
                        pe.wait_ge(*due("out_read", u))
                    tp = turned[:, a % 2, :]
                    if a < 8:
                        v, vs, rows = R1[:, 2048:4096].rearrange("p (t n) -> p t n", t=T), slice(a * P, (a + 1) * P), slice(0, P)
                    elif a < 24:
                        h, r = a - 8, 64 * (a % 2)
                        v, vs, rows = R1[:, 0:2048].rearrange("p (t n) -> p t n", t=T), slice(h * DH, (h + 1) * DH), slice(r, r + 64)
                    else:
                        h, r = a - 24, 64 * (a % 2)
                        v, vs, rows = R3[:, 2048:3072].rearrange("p (t n) -> p t n", t=T), slice(h * DH, (h + 1) * DH), slice(r, r + 64)
                    o = aux[rows, 2, (u % 2) * S:(u % 2 + 1) * S]
                    pe.matmul(o, v[:, 0, vs], tp[:, 0:S], start=True, stop=False, skip_group_check=True)
                    pe.matmul(o[:, P:S], v[:, 1, vs], tp[:, S:3 * P], start=False, stop=True,
                              skip_group_check=True).then_inc(sems["values_ready"], 1)
                elif kind == "layer_norm" or kind == "rms_norm":
                    if kind == "layer_norm" and i == 1:
                        continue
                    pe.wait_ge(*due("normed_ready", NORM[kind, i] + 1))
                    turn_tokens(normed, "normed_turned")
                    state["x"] += 4
                elif kind == "epi" and i.epilogue == "norm_ranks":
                    pe.wait_ge(*due("squares_ready", 1))
                    sq = R3[:, 0:1024].rearrange("p (k s) -> p k s", k=4)
                    for r in range(2):
                        for k in range(2):
                            ins = pe.matmul(aux[:, 0, r * S:(r + 1) * S], ones, sq[:, 2 * r + k, :], start=(k == 0), stop=(k == 1))
                    own(ins, "squares_summed")
                elif kind == "ssd":
                    pe.wait_ge(*due("a_ready", 1))
                    pe.wait_ge(*due("cat_lo_ready", 20))
                    pe.wait_ge(*due("cat_hi_ready", 20))
                    a = ssd_c[:, 2, :]
                    pe.matmul(aux[:, 0, 0:32], tri, a, start=True, stop=True)
                    pe.matmul(aux[:, 0, 32:64], ones, a, start=True, stop=True).then_inc(sems["cums_ready"], 1)
                    pe.wait_ge(*due("acc_read_dve", Z_READS))
                    for b, (s0, l0) in enumerate(((0, 0), (P, P), (0, P))):
                        for g in range(2):
                            n = 2 * b + g
                            ins = pe.matmul(acc[:, 0, n // 4, (n % 4) * P:(n % 4 + 1) * P], b_T[:, g, s0:s0 + P],
                                            c_T[:, g, l0:l0 + P], start=True, stop=True)
                    own(ins, "cb_ready")
                    for b in range(2):
                        if b:
                            pe.wait_ge(*due("xs_read", 1))
                        for f in range(8):
                            ins = pe.transpose(acc[:, 1, f // 4, (f % 4) * P:(f % 4 + 1) * P], conv_out[:, f, b * P:(b + 1) * P], ident)
                        own(ins, "xs_turned")
                    for b in range(2):
                        pe.wait_ge(*due("rows_ready", b + 1))
                        for q in range(4):
                            n = 4 * b + q
                            if n == 0:
                                pe.wait_ge(*due("edge_ready", 1))
                            if n >= 2:
                                pe.wait_ge(*due("seg_rows", n - 1))
                            pe.matmul(aux[:, n % 2, :], ones, tmp[:, q * 512:(q + 1) * 512], start=True, stop=True).then_inc(sems["cums_ready"], 1)
                    for b in range(2):
                        pe.wait_ge(*due("m_ready", b + 1))
                        if b:
                            pe.wait_ge(*due("y_read", 1))
                        for h in range(SSD_HEADS):
                            ins = pe.matmul(aux[:, 2 + h // 8, (h % 8) * SSD_P:(h % 8 + 1) * SSD_P], seg[:, b, h, :],
                                            x_dt[:, b, h, :], start=True, stop=True)
                        own(ins, "y_near")
                    pe.wait_ge(*due("edge_ready", 2))
                    pe.wait_ge(*due("xs_read", 2))
                    for g in range(2):
                        ins = pe.matmul(acc[:, 1, g, :], cb[:, 2, g, :],
                                        x_far[:, 8 * g:8 * g + 8, :].rearrange("p h n -> p (h n)"), start=True, stop=True)
                    own(ins, "y_far_ready")
                    pe.wait_ge(*due("y_gated", 1))
                    turn_tokens(R2[:, 2048:4096].rearrange("p (t n) -> p t n", t=T), "normed_turned")
                elif kind == "final":
                    pass

        @block.scalar
        def _(act):
            own = Own(act, "act_own")
            act.dma_start(cols[:, 0:2], w["q_norm_even"].rearrange("a (k p) -> p (a k)", p=P), allow_slow_non_contiguous=True).then_inc(sems["cols_landed"], 16)
            act.dma_start(cols[:, 2:4], w["kv_norm_even"].rearrange("a (k p) -> p (a k)", p=P), allow_slow_non_contiguous=True).then_inc(sems["cols_landed"], 16)
            for l in range(2):
                act.dma_start(cols[:, 4 + 8 * l:12 + 8 * l], w["ln_g"][l:l + 1].rearrange("a (k p) -> p (a k)", p=P), allow_slow_non_contiguous=True).then_inc(sems["cols_landed"], 16)
                act.dma_start(cols[:, 20 + 8 * l:28 + 8 * l], w["ln_b"][l:l + 1].rearrange("a (k p) -> p (a k)", p=P), allow_slow_non_contiguous=True).then_inc(sems["cols_landed"], 16)
            for c0, name in ((36, "norm_mix_w_2"), (44, "norm_mlp_w_2"), (52, "ssd_norm_w_2")):
                act.dma_start(cols[:, c0:c0 + 8], w[name].rearrange("a (k p) -> p (a k)", p=P), allow_slow_non_contiguous=True).then_inc(sems["cols_landed"], 16)
            for n in range(2):
                act.wait_ge(*due("angles_ready", n + 1))
                own(act.activation(trig[:, n, :, :], trig[:, n, :, :], ACT.Sin), "trig_ready")
            for n in range(2):
                hi_prep(act, own, n)
            for s in steps:
                kind, i = s
                if kind == "piece":
                    if i.n + 2 < len(pieces):
                        hi_prep(act, own, i.n + 2)
                elif kind == "turn_x":
                    for b in range(4):
                        act.wait_ge(*due("x_turned", b + 1))
                        own(act.activation(x_hi[:, 2 * b:2 * b + 2, :], aux[:, b, :].rearrange("p (f s) -> p f s", f=2),
                                       ACT.Copy), "x_hi_ready")
                elif kind == "epi":
                    c = i
                    a2 = acc[:, c.pair, :, :]
                    if c.epilogue in ("copy_tok", "copy_feat"):
                        act.wait_ge(*due("piece_used", c.pieces[-1].n + 1))
                        own(act.activation(epi_dst(c), a2, ACT.Copy), "acc_read_act")
                    elif c.epilogue.startswith("silu"):
                        act.wait_ge(*due("piece_used", c.pieces[-1].n + 1))
                        own(act.activation(epi_dst(c), a2, ACT.Tanh, scale=0.5), "tanh_ready")
                    elif c.epilogue == "norm_ranks":
                        act.wait_ge(*due("piece_used", c.pieces[-1].n + 1))
                        own(act.activation(R3[:, 0:1024].rearrange("p (b n) -> p b n", b=2), a2, ACT.Square), "squares_ready")
                        act.wait_ge(*due("acc_read_dve", c.read_count))
                        own(act.activation(cat_hi[:, 20:24, :].rearrange("p k s -> p (k s)"), R3[:, 2048:3072], ACT.Copy), "ranks_hi")
                    elif c.epilogue == "conv_in":
                        act.wait_ge(*due("piece_used", c.pieces[-1].n + 1))
                        act.wait_ge(*due("pad_ready", 1))
                        for b in range(2):
                            f = c.info["dst"] + 2 * b
                            ins = act.activation(conv_in[:, f:f + 2, 3:], a2[:, b, :].rearrange("p (f s) -> p f s", f=2), ACT.Copy)
                        own(ins, "acc_read_act")
                    elif c.epilogue == "relu2":
                        n = c.info["dst"]
                        act.wait_ge(*due("piece_used", c.pieces[-1].n + 1))
                        if n:
                            act.wait_ge(*due("acc_read_dve", c.read_count - 1))
                        own(act.activation(tmp[:, 0:1024].rearrange("p (b n) -> p b n", b=2), a2, ACT.Relu), "relu_ready")
                        act.wait_ge(*due("acc_read_dve", c.read_count))
                        if n >= 4:
                            act.wait_ge(*due("piece_used", ff2_used[n - 4]))
                        own(act.activation(cat2_hi[:, 4 * (n % 4):4 * (n % 4) + 4, :].rearrange("p k s -> p (k s)"), tmp[:, 1024:2048],
                                       ACT.Copy), "ff_hi")
                elif kind == "ret_values":
                    h = i
                    gate = R2[:, :].rearrange("p (t n) -> p t n", t=T)
                    act.wait_ge(*due("ret_centred", h + 1))
                    act.wait_ge(*due("ret_rstd", h + 1))
                    for t in range(T):
                        v = gate[:, t, h * RET_DV:(h + 1) * RET_DV]
                        ins = act.activation(v, v, ACT.Copy, scale=stats[:, 40 + 2 * (h % 2) + t:41 + 2 * (h % 2) + t])
                    own(ins, "ret_scaled")
                elif kind == "ret_turn":
                    for half in range(2):
                        n = 2 * i + half
                        act.wait_ge(*due("ret_turned", n + 1))
                        own(act.activation(cat_hi[:, 2 * n:2 * n + 2, :], aux[:, 1, :].rearrange("p (f s) -> p f s", f=2),
                                       ACT.Copy), "ret_hi")
                elif kind == "scores":
                    a = i
                    act.wait_ge(*due("negmax_ready", a + 1))
                    pr = probs[:, a % 2, :]
                    nm = stats[:, 2 * (a % 2):2 * (a % 2) + 2]
                    sm = stats[:, 4 + 2 * (a % 2):6 + 2 * (a % 2)]
                    act.activation(pr[:, 0:P], pr[:, 0:P], ACT.Exp, bias=nm[:, 0:1], accum_out=sm[:, 0:1])
                    own(act.activation(pr[:, P:], pr[:, P:], ACT.Exp, bias=nm[:, 1:2], accum_out=sm[:, 1:2]), "exp_ready")
                elif kind == "turn":
                    a = i
                    act.wait_ge(*due("probs_turned", a + 1))
                    if a >= 2:
                        act.wait_ge(*due("values_ready", a - 1))
                    own(act.activation(turned[:, a % 2, :], aux[:, 1, 0:3 * P], ACT.Copy), "turned_copied")
                elif kind == "gate":
                    u = i
                    act.wait_ge(*due("out_read", u + 1))
                    b, tile = cat_place(u)
                    if u == 8:
                        act.wait_ge(*due("acc_read_dve", Y_READS[0]))
                    if u == 16:
                        act.wait_ge(*due("acc_read_dve", Y_READS[1]))
                    own(act.activation(acts[b][0][:, tile, :], gated[:, u % 2, :], ACT.Copy), "cat_hi_ready")
                elif kind in ("layer_norm", "rms_norm") and (kind, i) in NORM:
                    t0 = TURNS[kind, i]
                    for b in range(4):
                        act.wait_ge(*due("scaled_ready", t0 + b + 1))
                        own(act.activation(x_hi[:, 2 * b:2 * b + 2, :], R1[:, b * 512:(b + 1) * 512].rearrange("p (f s) -> p f s", f=2),
                                       ACT.Copy), "x_hi_ready")
                elif kind == "conv":
                    n = i
                    act.wait_ge(*due("conv_read", n + 1))
                    own(act.activation(conv_in[:, 4 * n:4 * n + 4, 0:S], conv_out[:, 4 * n:4 * n + 4, :], ACT.Tanh), "conv_tanh")
                    if n == 2:
                        act.wait_ge(*due("dt_exp_in", 1))
                        act.wait_ge(*due("dt_landed", 48))
                        act.activation(ssd_c[:, 3, :], ssd_c[:, 3, :], ACT.Exp)
                        own(act.activation(ssd_c[:, 5, 0:16], ssd_c[:, 5, 0:16], ACT.Exp), "dt_exp")
                        act.wait_ge(*due("dt_ln_in", 1))
                        own(act.activation(ssd_c[:, 6, :], ssd_c[:, 4, :], ACT.Ln), "dt_ln")
                elif kind == "ssd":
                    act.wait_ge(*due("edge_ready", 1))
                    act.activation(ssd_c[:, 7, :], ssd_c[:, 7, :], ACT.Exp)
                    own(act.activation(ssd_c[:, 8, :], ssd_c[:, 8, :], ACT.Exp), "edge_exp")
                    for b in range(2):
                        act.wait_ge(*due("seg_ready", b + 1))
                        own(act.activation(seg[:, b], seg[:, b], ACT.Exp), "seg_exp")
                    t0 = TURNS["ssd", 0]
                    for b in range(4):
                        act.wait_ge(*due("scaled_ready", t0 + b + 1))
                        own(act.activation(cat2_hi[:, 4 + 2 * b:6 + 2 * b, :], tmp[:, b * 512:(b + 1) * 512].rearrange("p (f s) -> p f s", f=2),
                                       ACT.Copy), "normed_hi")

        @block.vector
        def _(dve):
            own = Own(dve, "dve_own")
            rot = [0]

            def low_prep(n):
                p = pieces[n]
                lo_prep(dve, own, n, 0, 3 if pool_share(p) else p.nk, "lo_ready")

            own(dve.memset(stats[:, :], 0.0))
            dve.wait_ge(*due("pos_landed", 16))
            dve.wait_ge(*due("tables_landed", 16))
            pos = R1[:, 256:512]
            own(dve.tensor_copy(pos, R1[:, 0:256].bitcast(I32)))
            n_turn, ang = R1[:, 512:768], R1[:, 768:1024]
            c1 = 6.28125
            c2 = float(np.float32(np.floor((TWO_PI - c1) * 2 ** 20) / 2 ** 20))
            c3 = float(np.float32(TWO_PI - c1 - c2))
            magic = 1.5 * 2 ** 23
            for n, col in ((0, C_FRET), (1, C_FROPE)):
                own.wait()
                own(dve.tensor_scalar(ang, pos, cst[:, col:col + 1], None, ALU.mult))
                own.wait()
                own(dve.tensor_scalar(n_turn, ang, 1.0 / TWO_PI, magic, ALU.mult, ALU.add))
                own.wait()
                own(dve.tensor_scalar(n_turn, n_turn, magic, None, ALU.subtract))
                for c in (c1, c2, c3):
                    own.wait()
                    own(dve.scalar_tensor_tensor(ang, n_turn, -c, ang, ALU.mult, ALU.add))
                own.wait()
                own(dve.tensor_scalar(trig[:, n, 0, :], ang, PI_SAFE, -PI_SAFE, ALU.min, ALU.max))
                own(dve.tensor_scalar(ang, ang, 0.5 * np.pi, None, ALU.add))
                own.wait()
                own(dve.tensor_scalar(n_turn, ang, np.pi, -TWO_PI, ALU.is_gt, ALU.mult))
                own.wait()
                own(dve.tensor_tensor(ang, ang, n_turn, ALU.add))
                own.wait()
                own(dve.tensor_scalar(trig[:, n, 1, :], ang, PI_SAFE, -PI_SAFE, ALU.min, ALU.max), "angles_ready")

            def row_stats(src, count, at, slot):
                st = stats[:, 8:8 + 12 * 1] if False else stats[:, at:at + 6 * count]
                for m in range(count):
                    own(dve.bn_stats(st[:, 6 * m:6 * m + 6], src[:, m * 512:(m + 1) * 512]))
                own.wait()
                own(dve.bn_aggr(slot, st))

            def full_norm(kind, i):
                n = NORM_ALL[kind, i]
                own.wait()
                mv = stats[:, 32:36].rearrange("p (t n) -> p t n", t=T)
                for t in range(T):
                    row_stats(res[:, t, :], 2, 8 + 12 * t, mv[:, t, :])
                own.wait()
                if kind == "layer_norm":
                    own(dve.tensor_scalar(stats[:, 36:38], mv[:, :, 1], LN_EPS, None, ALU.add), "var_ready")
                else:
                    own(dve.tensor_tensor(stats[:, 38:40], mv[:, :, 0], mv[:, :, 0], ALU.mult))
                    own.wait()
                    own(dve.scalar_tensor_tensor(stats[:, 36:38], stats[:, 38:40], LN_EPS, mv[:, :, 1], ALU.add, ALU.add), "var_ready")
                dve.wait_ge(*due("rstd_ready", n + 1))
                for t in range(T):
                    o = tmp[:, t * D:(t + 1) * D]
                    signal = "normed_ready" if t == T - 1 and (kind, i) in NORM else None
                    if kind == "layer_norm":
                        own(dve.tensor_scalar(o, res[:, t, :], mv[:, t, 0:1], stats[:, 44 + t:45 + t], ALU.subtract, ALU.mult), signal)
                    else:
                        own(dve.tensor_scalar(o, res[:, t, :], stats[:, 44 + t:45 + t], None, ALU.mult), signal)

            NORM_ALL = {("layer_norm", 0): 0, ("layer_norm", 1): 1, ("rms_norm", 0): 2, ("rms_norm", 1): 3, ("final", 0): 4}

            def scaled_split(t0, gain, offset, dst, hi, lo, hi_name, hi_base, lo_name):
                for b in range(4):
                    dve.wait_ge(*due("normed_turned", t0 + b + 1))
                    for f in range(2):
                        k = 2 * b + f
                        src = aux[:, b, f * S:(f + 1) * S]
                        o = dst[:, k * S:(k + 1) * S]
                        if offset is None:
                            own(dve.tensor_scalar(o, src, gain[:, k:k + 1], None, ALU.mult), "scaled_ready" if f else None)
                        else:
                            own(dve.tensor_scalar(o, src, gain[:, k:k + 1], offset[:, k:k + 1], ALU.mult, ALU.add), "scaled_ready" if f else None)
                for b in range(4):
                    dve.wait_ge(*due(hi_name, hi_base + b + 1))
                    ks = slice(2 * b, 2 * b + 2)
                    own(dve.tensor_tensor(lo[:, ks, :], dst[:, b * 512:(b + 1) * 512].rearrange("p (f s) -> p f s", f=2),
                                      hi[:, ks, :].bitcast(F32), ALU.subtract), lo_name)

            low_prep(0)
            low_prep(1)
            for s in steps:
                kind, i = s
                if kind == "piece":
                    if i.n + 2 < len(pieces):
                        low_prep(i.n + 2)
                elif kind == "turn_x":
                    for b in range(4):
                        dve.wait_ge(*due("x_hi_ready", b + 1))
                        dve.wait_ge(*due("x_turned", b + 1))
                        ks = slice(2 * b, 2 * b + 2)
                        own(dve.tensor_tensor(x_lo[:, ks, :], aux[:, b, :].rearrange("p (f s) -> p f s", f=2),
                                          x_hi[:, ks, :].bitcast(F32), ALU.subtract), "x_lo_ready")
                elif kind == "epi":
                    c = i
                    a2 = acc[:, c.pair, :, :]
                    if c.epilogue == "rotate":
                        n = rot_n[c.n]
                        dve.wait_ge(*due("piece_used", c.pieces[-1].n + 1))
                        dve.wait_ge(*due("trig_ready", 2))
                        if n >= 2:
                            dve.wait_ge(*due("rot_ready", n if n in (4, 5) else n - 1))
                        if n == 6:
                            dve.wait_ge(*due("res_ready", 1))
                        m = 1 if c.width == 2 * P else 2
                        pr = rot_products(n)
                        sin = trig[:, c.info["table"], 0:1, :].to_broadcast([P, m, S])
                        cos = trig[:, c.info["table"], 1:2, :].to_broadcast([P, m, S])
                        first, second = a2[:, 0:m, 0:S], a2[:, 0:m, S:2 * S]
                        for q, (part, f) in enumerate(((first, cos), (second, sin), (second, cos), (first, sin))):
                            ins = dve.tensor_tensor(pr[:, q, 0:m, :], part, f, ALU.mult)
                            if q < 3:
                                own(ins)
                        own(ins, "acc_read_dve")
                    elif c.epilogue.startswith("silu"):
                        dve.wait_ge(*due("piece_used", c.pieces[-1].n + 1))
                        dve.wait_ge(*due("tanh_ready", tanh_n[c.n]))
                        o = epi_dst(c)
                        own(dve.scalar_tensor_tensor(o, o, 1.0, a2, ALU.add, ALU.mult), "acc_read_dve")
                    elif c.epilogue == "norm_ranks":
                        dve.wait_ge(*due("squares_summed", 1))
                        own(dve.tensor_scalar(R3[:, 1024:1536], aux[:, 0, :], 1.0 / 256, RMS_EPS, ALU.mult, ALU.add), "mean_square")
                        dve.wait_ge(*due("rank_rstd", 1))
                        dve.wait_ge(*due("cols_landed", 16 * 9))
                        dve.wait_ge(*due("piece_used", c.pieces[-1].n + 1))
                        for k in range(4):
                            gain = cols[:, k:k + 1]
                            ins = dve.scalar_tensor_tensor(R3[:, 2048 + k * S:2048 + (k + 1) * S], a2[:, k // 2, (k % 2) * S:(k % 2 + 1) * S],
                                                           gain, R3[:, 1024 + (k // 2) * S:1024 + (k // 2 + 1) * S], ALU.mult, ALU.mult)
                            if k < 3:
                                own(ins)
                        own(ins, "acc_read_dve")
                        dve.wait_ge(*due("ranks_hi", 1))
                        own(dve.tensor_tensor(cat_lo[:, 20:24, :].rearrange("p k s -> p (k s)"), R3[:, 2048:3072],
                                          cat_hi[:, 20:24, :].rearrange("p k s -> p (k s)").bitcast(F32), ALU.subtract), "ranks_lo")
                    elif c.epilogue in ("residual", "add"):
                        dve.wait_ge(*due("piece_used", c.pieces[-1].n + 1))
                        r = res[:, :, c.info["n"] * NCOL:(c.info["n"] + 1) * NCOL]
                        if c.acts == "cat2" and c.epilogue == "residual":
                            dve.wait_ge(*due("res_ready", 1))
                        scale = DN_ALPHA if c.epilogue == "residual" else 1.0
                        own(dve.scalar_tensor_tensor(r, r, scale, a2, ALU.mult, ALU.add), "acc_read_dve")
                    elif c.epilogue == "copy_dt":
                        dve.wait_ge(*due("piece_used", c.pieces[-1].n + 1))
                        dve.wait_ge(*due("dt_landed", 48))
                        v = ssd_c[:, 0, :].rearrange("p (t n) -> p t n", t=T)
                        own(dve.tensor_tensor(v, a2[:, :, 0:16], ssd_c[:, 9, 0:16].rearrange("p (a n) -> p a n", a=1).to_broadcast([P, T, 16]),
                                          ALU.add), "acc_read_dve")
                        dve.wait_ge(*due("acc_read_dve", c.read_count))
                        own(dve.scalar_tensor_tensor(ssd_c[:, 3, :], ssd_c[:, 0, :], -1.0, ssd_c[:, 0, :], ALU.mult, ALU.min), "dt_exp_in")
                    elif c.epilogue == "relu2":
                        n = c.info["dst"]
                        dve.wait_ge(*due("piece_used", c.pieces[-1].n + 1))
                        dve.wait_ge(*due("relu_ready", n + 1))
                        if n:
                            dve.wait_ge(*due("ff_hi", n))
                            dve.wait_ge(*due("ff_lo", n))
                        own(dve.scalar_tensor_tensor(tmp[:, 1024:2048].rearrange("p (b n) -> p b n", b=2), a2, 0.0,
                                                 tmp[:, 0:1024].rearrange("p (b n) -> p b n", b=2), ALU.max, ALU.mult), "acc_read_dve")
                        dve.wait_ge(*due("ff_hi", n + 1))
                        ks = slice(4 * (n % 4), 4 * (n % 4) + 4)
                        own(dve.tensor_tensor(cat2_lo[:, ks, :].rearrange("p k s -> p (k s)"), tmp[:, 1024:2048],
                                          cat2_hi[:, ks, :].rearrange("p k s -> p (k s)").bitcast(F32), ALU.subtract), "ff_lo")
                elif kind == "ret_scores":
                    h = i
                    dve.wait_ge(*due("ret_scored", h + 1))
                    dve.wait_ge(*due("decay_landed", 16))
                    if h >= 2:
                        dve.wait_ge(*due("ret_summed", h - 1))
                    own(dve.tensor_tensor(probs[:, h % 2, :], aux[:, 0, 0:3 * P], decay[:, h, :], ALU.mult), "ret_decayed")
                elif kind == "ret_values":
                    h = i
                    gate = R2[:, :].rearrange("p (t n) -> p t n", t=T)
                    dve.wait_ge(*due("ret_summed", h + 1))
                    mv = stats[:, 32:36].rearrange("p (t n) -> p t n", t=T)
                    for t in range(T):
                        row_stats(aux[:, 2 + t, :], 1, 8 + 6 * t, mv[:, t, :])
                    own.wait()
                    own(dve.tensor_scalar(stats[:, 36 + 2 * (h % 2):38 + 2 * (h % 2)], mv[:, :, 1], LN_EPS, 4.0, ALU.add, ALU.mult), "ret_var")
                    for t in range(T):
                        v = gate[:, t, h * RET_DV:(h + 1) * RET_DV]
                        ins = dve.scalar_tensor_tensor(v, aux[:, 2 + t, :], mv[:, t, 0:1], v, ALU.subtract, ALU.mult)
                        if t == 0:
                            own(ins)
                    own(ins, "ret_centred")
                    dve.wait_ge(*due("ret_centred", h + 1))
                elif kind == "ret_turn":
                    for half in range(2):
                        n = 2 * i + half
                        dve.wait_ge(*due("ret_hi", n + 1))
                        dve.wait_ge(*due("ret_turned", n + 1))
                        own(dve.tensor_tensor(cat_lo[:, 2 * n:2 * n + 2, :], aux[:, 1, :].rearrange("p (f s) -> p f s", f=2),
                                          cat_hi[:, 2 * n:2 * n + 2, :].bitcast(F32), ALU.subtract), "ret_lo")
                elif kind == "scores":
                    a = i
                    pr = probs[:, a % 2, :]
                    dve.wait_ge(*due("scores_ready", a + 1))
                    if a >= 2:
                        dve.wait_ge(*due("probs_turned", a - 1))
                    nm = stats[:, 2 * (a % 2):2 * (a % 2) + 2]
                    scale = (NOPE + ROPE) ** -0.5 if a < 8 else DH ** -0.5
                    bank = aux[:, 3 * (a % 2), 0:3 * P]
                    if a < 24:
                        own(dve.scalar_tensor_tensor(pr, bank, scale, causal, ALU.mult, ALU.add), "scores_read")
                    else:
                        dve.wait_ge(*due("bias_landed", 16 * BAND_HEADS))
                        dve.wait_ge(*due("half_ready", 1))
                        own(dve.scalar_tensor_tensor(pr[:, 0:P], bank[:, 0:P], scale, backwards(a - 24, P), ALU.mult, ALU.add))
                        own.wait()
                        own(dve.scalar_tensor_tensor(pr[:, P:], bank[:, P:], scale, backwards(a - 24, S), ALU.mult, ALU.add), "scores_read")
                    dve.wait_ge(*due("scores_read", a + 1))
                    own(dve.tensor_reduce(nm[:, 0:1], pr[:, 0:P], AX, ALU.max, negate=True))
                    own.wait()
                    own(dve.tensor_reduce(nm[:, 1:2], pr[:, P:], AX, ALU.max, negate=True), "negmax_ready")
                elif kind == "turn":
                    a = i
                    pr = probs[:, a % 2, :]
                    sm = stats[:, 4 + 2 * (a % 2):6 + 2 * (a % 2)]
                    dve.wait_ge(*due("exp_ready", a + 1))
                    own(dve.reciprocal(sm, sm))
                    own.wait()
                    own(dve.tensor_scalar(pr[:, 0:P], pr[:, 0:P], sm[:, 0:1], None, ALU.mult))
                    own.wait()
                    own(dve.tensor_scalar(pr[:, P:], pr[:, P:], sm[:, 1:2], None, ALU.mult), "probs_ready")
                elif kind == "gate":
                    u = i
                    dve.wait_ge(*due("values_ready", LAST_OF_UNIT[u] + 1))
                    if u >= 2:
                        dve.wait_ge(*due("cat_hi_ready", u - 1))
                        dve.wait_ge(*due("cat_lo_ready", u - 1))
                    o = aux[:, 2, (u % 2) * S:(u % 2 + 1) * S]
                    if u < 16:
                        g = R1[:, u * S:(u + 1) * S] if u < 8 else R1[:, 2048 + (u - 8) * S:2048 + (u - 7) * S]
                        if u == 0 or u == 8:
                            dve.wait_ge(*due("acc_read_dve", GATE_READS[u // 8]))
                        if u == 8 + 4:
                            dve.wait_ge(*due("acc_read_dve", GATE_READS[2]))
                        own(dve.scalar_tensor_tensor(gated[:, u % 2, :], o, 0.5, g, ALU.mult, ALU.mult), "out_read")
                    else:
                        own(dve.tensor_copy(gated[:, u % 2, :], o), "out_read")
                elif kind == "low":
                    u = i
                    b, tile = cat_place(u)
                    dve.wait_ge(*due("cat_hi_ready", u + 1))
                    dve.wait_ge(*due("out_read", u + 1))
                    own(dve.tensor_tensor(acts[b][1][:, tile, :], gated[:, u % 2, :], acts[b][0][:, tile, :].bitcast(F32),
                                      ALU.subtract), "cat_lo_ready")
                elif kind == "layer_norm" and i == 0:
                    dve.wait_ge(*due("acc_read_dve", Y_READS[0]))
                    full_norm(kind, i)
                    scaled_split(0, ln_g_col[:, 0:8], ln_b_col[:, 0:8], R1, x_hi, x_lo, "x_hi_ready", 4, "x_lo_ready")
                elif kind == "layer_norm":
                    dve.wait_ge(*due("acc_read_dve", Y_READS[1]))
                    full_norm(kind, i)
                    dve.wait_ge(*due("gb_landed", 64))
                    for op, at in ((ALU.mult, 0), (ALU.add, 1024)):
                        g = R2[:, at:at + 1024].rearrange("p (a n) -> p a n", a=1).to_broadcast([P, T, D])
                        own.wait()
                        if op == ALU.mult:
                            own(dve.tensor_tensor(tmp[:, :].rearrange("p (t n) -> p t n", t=T), tmp[:, :].rearrange("p (t n) -> p t n", t=T), g, op))
                        else:
                            own(dve.tensor_tensor(res[:, :, :], tmp[:, :].rearrange("p (t n) -> p t n", t=T), g, op))
                elif kind == "rms_norm":
                    dve.wait_ge(*due("acc_read_dve", Y_READS[1] if i == 0 else SSD_READS))
                    full_norm(kind, i)
                    scaled_split(TURNS[kind, i], mix_col if i == 0 else mlp_col, None, R1, x_hi, x_lo, "x_hi_ready",
                                 4 * (1 + NORM[kind, i]), "x_lo_ready")
                    if i == 0:
                        own(dve.memset(conv_in[:, :, 0:3], 0.0))
                        dve.wait_ge(*due("conv_landed", 16 * 5))
                        own(dve.tensor_scalar(conv_c[:, :, :], conv_c[:, :, :], 0.5, None, ALU.mult), "pad_ready")
                        dve.wait_ge(*due("bias_landed", 16 * BAND_HEADS))
                        own(dve.memset(bias[0:64, :, 0:64], NEG), "half_ready")
                    else:
                        own.wait()
                elif kind == "conv":
                    n = i
                    dve.wait_ge(*due("acc_read_act", CONV_READS[n]))
                    for f in range(4 * n, 4 * n + 4):
                        own(dve.tensor_scalar(conv_out[:, f, :], conv_in[:, f, 0:S], conv_c[:, 0, f:f + 1], conv_c[:, 4, f:f + 1],
                                              ALU.mult, ALU.add))
                    for tap in range(1, TAPS):
                        own.wait()
                        for f in range(4 * n, 4 * n + 4):
                            own(dve.scalar_tensor_tensor(conv_out[:, f, :], conv_in[:, f, tap:tap + S], conv_c[:, tap, f:f + 1],
                                                         conv_out[:, f, :], ALU.mult, ALU.add), "conv_read" if tap == TAPS - 1 and f == 4 * n + 3 else None)
                    dve.wait_ge(*due("conv_tanh", n + 1))
                    own(dve.scalar_tensor_tensor(conv_out[:, 4 * n:4 * n + 4, :], conv_in[:, 4 * n:4 * n + 4, 0:S], 1.0,
                                                 conv_out[:, 4 * n:4 * n + 4, :], ALU.add, ALU.mult))
                    if n == 2:
                        e, u, t, z = ssd_c[:, 3, :], ssd_c[:, 4, :], ssd_c[:, 1, :], ssd_c[:, 7, :]
                        dve.wait_ge(*due("dt_exp", 1))
                        own(dve.tensor_scalar(u, e, 1.0, None, ALU.add), "dt_ln_in")
                        own.wait()
                        own(dve.tensor_scalar(t, u, 1.0, None, ALU.subtract))
                        own.wait()
                        own(dve.tensor_scalar(z, t, 0.0, None, ALU.is_equal))
                        own.wait()
                        own(dve.tensor_tensor(t, t, z, ALU.add))
                        own.wait()
                        own(dve.reciprocal(t, t))
                        own.wait()
                        own(dve.tensor_tensor(t, t, e, ALU.mult))
                        own(dve.tensor_tensor(z, z, e, ALU.mult))
                        dve.wait_ge(*due("dt_ln", 1))
                        own.wait()
                        own(dve.tensor_tensor(t, t, ssd_c[:, 6, :], ALU.mult))
                        own.wait()
                        own(dve.tensor_tensor(t, t, z, ALU.add))
                        own.wait()
                        own(dve.scalar_tensor_tensor(t, ssd_c[:, 0, :], 0.0, t, ALU.max, ALU.add))
                        own.wait()
                        a_row = ssd_c[:, 5, 0:16].rearrange("p (a n) -> p a n", a=1).to_broadcast([P, T, 16])
                        own(dve.scalar_tensor_tensor(ssd_c[:, 2, :].rearrange("p (t n) -> p t n", t=T), t.rearrange("p (t n) -> p t n", t=T),
                                                 -1.0, a_row, ALU.mult, ALU.mult), "a_ready")
                elif kind == "ssd":
                    own.wait()
                    dt = ssd_c[:, 1, :].rearrange("p (b h) -> p b h", b=2)
                    cum, edge, far = ssd_c[:, 6, :], ssd_c[:, 7, :], ssd_c[:, 8, :]
                    dve.wait_ge(*due("cums_ready", 1))
                    own(dve.tensor_copy(cum, aux[:, 0, 0:32]))
                    own.wait()
                    own(dve.tensor_copy(edge, cum))
                    own(dve.tensor_tensor(far, aux[:, 0, 32:64], cum, ALU.subtract), "edge_ready")
                    dve.wait_ge(*due("cb_ready", 1))
                    own(dve.tensor_tensor(R1[:, 3072:3584].rearrange("p (n l) -> p n l", n=4), acc[:, 0, 0, :].rearrange("p (n l) -> p n l", n=4),
                                          tri.rearrange("p (a l) -> p a l", a=1).to_broadcast([P, 4, P]), ALU.mult))
                    own(dve.tensor_copy(R1[:, 3584:3840], acc[:, 0, 1, 0:256]))
                    for b in range(2):
                        dve.wait_ge(*due("xs_turned", b + 1))
                        xs = acc[:, 1, :, :].rearrange("p c (h n) -> p (c h) n", n=SSD_P)
                        own(dve.tensor_tensor(x_dt[:, b], xs, dt[:, b, :].rearrange("p (h n) -> p h n", n=1).to_broadcast([P, 16, SSD_P]), ALU.mult))
                        own(dve.tensor_tensor(y_ssd[:, b], xs, ssd_c[:, 5, 16:32].rearrange("p (h n) -> p h n", n=1).to_broadcast([P, 16, SSD_P]), ALU.mult), "xs_read")
                    dve.wait_ge(*due("edge_exp", 1))
                    own.wait()
                    own(dve.tensor_tensor(x_far, x_dt[:, 0], far[:, 0:16].rearrange("p (h n) -> p h n", n=1).to_broadcast([P, 16, SSD_P]),
                                      ALU.mult), "edge_ready")
                    for b in range(2):
                        for q in range(4):
                            n = 4 * b + q
                            dve.wait_ge(*due("cums_ready", 2 + n))
                            c4 = cum[:, 16 * b + 4 * q:16 * b + 4 * q + 4].rearrange("p (h n) -> p h n", n=1).to_broadcast([P, 4, P])
                            own(dve.tensor_tensor(seg[:, b, 4 * q:4 * q + 4, :], aux[:, n % 2, :].rearrange("p (h n) -> p h n", h=4), c4,
                                              ALU.subtract), "seg_rows")
                        dve.wait_ge(*due("seg_rows", 4 * (b + 1)))
                        own(dve.tensor_scalar(seg[:, b], seg[:, b], 0.0, None, ALU.min), "seg_ready")
                    for b in range(2):
                        dve.wait_ge(*due("seg_exp", b + 1))
                        own.wait()
                        for g in range(2):
                            m = seg[:, b, 8 * g:8 * g + 8, :]
                            ins = dve.tensor_tensor(m, m, cb[:, b, g:g + 1, :].to_broadcast([P, 8, P]), ALU.mult)
                            if g == 0:
                                own(ins)
                        own(ins, "m_ready")
                    for b in range(2):
                        dve.wait_ge(*due("y_near", b + 1))
                        yb = R2[:, 2048 + b * 1024:2048 + (b + 1) * 1024].rearrange("p (c n) -> p c n", c=2)
                        own(dve.tensor_tensor(yb, yb, aux[:, 2:4, :], ALU.add), "y_read")
                    dve.wait_ge(*due("y_far_ready", 1))
                    own(dve.tensor_tensor(y_far, acc[:, 1, :, :].rearrange("p c (h n) -> p (c h) n", n=SSD_P),
                                          edge[:, 16:32].rearrange("p (h n) -> p h n", n=1).to_broadcast([P, 16, SSD_P]), ALU.mult))
                    own.wait()
                    own(dve.tensor_tensor(y_ssd[:, 1], y_ssd[:, 1], y_far, ALU.add))
                    own.wait()
                    y2 = R2[:, 2048:4096]
                    dve.wait_ge(*due("acc_read_dve", Z_READS))
                    own(dve.tensor_tensor(y2, y2, zb[:, 0:2048], ALU.mult))
                    own.wait()
                    mv = stats[:, 8:40]
                    for n in range(4):
                        st = mv[:, 6 * n:6 * n + 6]
                        own(dve.bn_stats(st, y2[:, n * 512:(n + 1) * 512]))
                    own.wait()
                    ag = ssd_c[:, 3, 0:8].rearrange("p (n v) -> p n v", v=2)
                    for n in range(4):
                        own(dve.bn_aggr(ag[:, n, :], mv[:, 6 * n:6 * n + 6]))
                    own.wait()
                    ms = ssd_c[:, 3, 8:12]
                    own(dve.tensor_tensor(ms, ag[:, :, 0], ag[:, :, 0], ALU.mult))
                    own.wait()
                    own(dve.scalar_tensor_tensor(ms, ms, 4.0 * LN_EPS, ag[:, :, 1], ALU.add, ALU.add), "y_sq")
                    dve.wait_ge(*due("y_rstd", 1))
                    for n in range(4):
                        v = y2[:, n * 512:(n + 1) * 512]
                        own(dve.tensor_scalar(v, v, ssd_c[:, 3, 12 + n:13 + n], None, ALU.mult), "y_gated" if n == 3 else None)
                    scaled_split(TURNS["ssd", 0], ssdn_col, None, tmp, cat2_hi[:, 4:12, :], cat2_lo[:, 4:12, :], "normed_hi", 0, "normed_lo")
                elif kind == "final":
                    dve.wait_ge(*due("acc_read_dve", FINAL_READS))
                    full_norm("final", 0)
                    dve.wait_ge(*due("gb_landed", 80))
                    own.wait()
                    g = R2[:, 0:1024].rearrange("p (a n) -> p a n", a=1).to_broadcast([P, T, D])
                    o = tmp[:, :].rearrange("p (t n) -> p t n", t=T)
                    own(dve.tensor_tensor(o, o, g, ALU.mult), "final_ready")

        @block.gpsimd
        def _(pool):
            own = Own(pool, "pool_own")

            def low_prep(n):
                if pool_share(pieces[n]):
                    lo_prep(pool, own, n, 3, 4, "lo_ready_pool")

            def inverse_root(o, i, signal):
                n = i.shape[1]
                own(pool.tensor_tensor(o, i, half_neg.to_broadcast([P, n]), ALU.pow), signal)

            own(pool.memset(half_neg, -0.5))
            pool.dma_start(R1[:, 0:256].bitcast(I32), w["positions"].to_broadcast([P, S])).then_inc(sems["pos_landed"], 16)
            pool.dma_start(tmp[:, 0:RET_HEADS * 3 * P], w["decay"]).then_inc(sems["decay_landed"], 16)
            for j, name in ((9, "dt_bias_2"), (5, "a_log_2")):
                pool.dma_start(ssd_c[:, j, 0:16], w[name].to_broadcast([P, 16])).then_inc(sems["dt_landed"], 16)
            pool.dma_start(ssd_c[:, 5, 16:32], w["d_skip_2"].to_broadcast([P, 16])).then_inc(sems["dt_landed"], 16)
            for tap in range(TAPS):
                pool.dma_start(conv_c[:, tap, :], w["conv_w_2"][tap:tap + 1, :].rearrange("a (k p) -> p (a k)", p=P), allow_slow_non_contiguous=True).then_inc(sems["conv_landed"], 16)
            pool.dma_start(conv_c[:, 4, :], w["conv_b_2"].rearrange("a (k p) -> p (a k)", p=P), allow_slow_non_contiguous=True).then_inc(sems["conv_landed"], 16)
            own.wait()
            low_prep(0)
            low_prep(1)

            def gains(l):
                pool.dma_start(R2[:, 0:1024], w["ln_g"][l:l + 1].to_broadcast([P, D])).then_inc(sems["gb_landed"], 16)
                pool.dma_start(R2[:, 1024:2048], w["ln_b"][l:l + 1].to_broadcast([P, D])).then_inc(sems["gb_landed"], 16)

            for s in steps:
                kind, i = s
                if kind == "piece":
                    if i.n + 2 < len(pieces):
                        low_prep(i.n + 2)
                elif kind == "epi" and i.epilogue == "rotate":
                    c = i
                    n = rot_n[c.n]
                    m = 1 if c.width == 2 * P else 2
                    pool.wait_ge(*due("acc_read_dve", c.read_count))
                    if n >= 4 and c.info["dst"] is None:
                        pool.wait_ge(*due("ret_turned", 8))
                    pr, o = rot_products(n), rot_dst(c, n)
                    own(pool.tensor_tensor(o[:, :, 0, :], pr[:, 0, 0:m, :], pr[:, 1, 0:m, :], ALU.subtract))
                    own.wait()
                    own(pool.tensor_tensor(o[:, :, 1, :], pr[:, 2, 0:m, :], pr[:, 3, 0:m, :], ALU.add), "rot_ready")
                elif kind == "ret_values":
                    h = i
                    pool.wait_ge(*due("ret_var", h + 1))
                    inverse_root(stats[:, 40 + 2 * (h % 2):42 + 2 * (h % 2)], stats[:, 36 + 2 * (h % 2):38 + 2 * (h % 2)], "ret_rstd")
                elif kind == "epi" and i.epilogue == "norm_ranks":
                    pool.wait_ge(*due("mean_square", 1))
                    inverse_root(R3[:, 1024:1536], R3[:, 1024:1536], "rank_rstd")
                elif kind == "layer_norm" or kind == "rms_norm":
                    n = {("layer_norm", 0): 0, ("layer_norm", 1): 1, ("rms_norm", 0): 2, ("rms_norm", 1): 3}[kind, i]
                    pool.wait_ge(*due("var_ready", n + 1))
                    inverse_root(stats[:, 44:46], stats[:, 36:38], "rstd_ready")
                    if kind == "layer_norm" and i == 0:
                        pool.wait_ge(*due("normed_ready", 1))
                        pool.wait_ge(*due("gb_landed", 32))
                        v = tmp[:, :].rearrange("p (t n) -> p t n", t=T)
                        own(pool.tensor_tensor(res[:, :, :], v, R2[:, 0:1024].rearrange("p (a n) -> p a n", a=1).to_broadcast([P, T, D]), ALU.mult))
                        own.wait()
                        own(pool.tensor_tensor(res[:, :, :], res[:, :, :], R2[:, 1024:2048].rearrange("p (a n) -> p a n", a=1).to_broadcast([P, T, D]), ALU.add), "res_ready")
                    if kind == "rms_norm" and i == 1:
                        pool.wait_ge(*due("normed_turned", 16))
                        pool.dma_start(R2[:, 0:1024], w["norm_final_w_2"].to_broadcast([P, D])).then_inc(sems["gb_landed"], 16)
                elif kind == "low" and i == MLA_HEADS - 1:
                    pool.wait_ge(*due("scores_ready", MLA_HEADS))
                    gains(0)
                elif kind == "low" and i == 15:
                    pool.wait_ge(*due("rot_ready", 10))
                    gains(1)
                elif kind == "low" and i == 8:
                    pool.wait_ge(*due("acc_read_dve", Y_READS[0]))
                    table = w["rel_bias_2"]
                    for h in range(BAND_HEADS):
                        src = bass.AP(table.tensor, h * (2 * REL_CLIP + 1) + REL_CLIP + 1 - P, [[1, P], [1, S]])
                        pool.dma_start(bias[:, h, :], src).then_inc(sems["bias_landed"], 16)
                elif kind == "ssd":
                    for b in range(2):
                        if b:
                            pool.wait_ge(*due("cums_ready", 5))
                        else:
                            pool.wait_ge(*due("a_ready", 1))
                        a = ssd_c[:, 2, 16 * b:16 * b + 16].rearrange("p (h n) -> p h n", n=1).to_broadcast([P, 16, P])
                        own(pool.tensor_tensor(row_a, tri.rearrange("p (a n) -> p a n", a=1).to_broadcast([P, 16, P]), a, ALU.mult), "rows_ready")
                    pool.wait_ge(*due("y_sq", 1))
                    inverse_root(ssd_c[:, 3, 12:16], ssd_c[:, 3, 8:12], "y_rstd")
                elif kind == "final":
                    pool.wait_ge(*due("var_ready", 5))
                    inverse_root(stats[:, 44:46], stats[:, 36:38], "rstd_ready")


_NAMES = ("w_in_even", "w_uq_even", "w_ukv_even", "w_out_even", "w_in_odd", "w_out_odd", "w_in_2", "w_out_2", "w_ff1_2", "w_ff2_2")
_ROWS = ("q_norm_even", "kv_norm_even", "ln_g", "ln_b", "norm_mix_w_2", "norm_mlp_w_2", "ssd_norm_w_2", "norm_final_w_2",
         "conv_b_2", "dt_bias_2", "a_log_2", "d_skip_2", "positions")


def kernel(**inputs):
    import concourse.bacc as _bacc
    from concourse.bass_utils import run_bass_kernel_spmd as _run

    arrays = {}
    arrays["x"] = np.ascontiguousarray(inputs["x"]).reshape(S, D)
    for name in _NAMES:
        a = np.ascontiguousarray(inputs[name])
        arrays[name] = a.reshape(a.shape[-2:])
    for name in _ROWS:
        a = np.ascontiguousarray(inputs[name])
        arrays[name] = a.reshape(-1, a.shape[-1])
    arrays["conv_w_2"] = np.ascontiguousarray(inputs["conv_w_2"]).reshape(TAPS, CONV_DIM)
    arrays["rel_bias_2"] = np.ascontiguousarray(np.asarray(inputs["rel_bias_2"])[0].T)
    arrays["tables"], arrays["decay"] = shape_tables()
    nc = _bacc.Bacc("TRN2", target_bir_lowering=False, num_devices=1)
    feed, w = {}, {}
    for name, a in arrays.items():
        feed[f"in_{name}"] = a
        w[name] = nc.dram_tensor(f"in_{name}", a.shape, mybir.dt.from_np(a.dtype), kind="ExternalInput").ap()
    out = nc.dram_tensor("out", (S, D), F32, kind="ExternalOutput").ap()
    build(nc, w, out)
    r = _run(nc, [feed], core_ids=[0])
    return r.results[0]["out"].reshape(1, S, D)
```

```python
from contextlib import ExitStack

import numpy as np

import concourse.bass as bass
from concourse import mybir

F32 = mybir.dt.float32
F32R = mybir.dt.float32r
I32 = mybir.dt.int32
ALU = mybir.AluOpType
ACT = mybir.ActivationFunctionType
AX = mybir.AxisListType.X

P = 128
S = 256
D = 1024
T = S // P
KD = D // P
NCOL = 512
NEG = -1e30
LN_EPS = 1e-5
RMS_EPS = 1e-6
DN_ALPHA = 4.0 ** 0.25

RET_HEADS, RET_DK, RET_DV = 4, 256, 512
MLA_HEADS, NOPE, ROPE = 8, 128, 64
MOBA_HEADS, DH = 16, 64
BAND_HEADS = 8
SSD_HEADS, SSD_P, SSD_N, SSD_G = 16, 64, 128, 2
CONV_DIM = 1536
CONV_TILES = CONV_DIM // P
TAPS = 4
REL_CLIP = 256
D_FF = 4096
FF_CHUNKS = D_FF // NCOL

RQ, RK, RV, RG, MQ, MKR, MG = 0, 1024, 2048, 4096, 6144, 6656, 6720
SQ, SK, SV, SZ, SX, SDT = 0, 512, 1024, 1536, 2560, 4096

C_ID, C_TRI, C_ONES, C_MASK, C_FRET, C_FROPE = 0, 128, 256, 384, 768, 769
C_END = 770
RAW_SLOTS = 3
PROBS = 4
TWO_PI = 2.0 * np.pi
PI_SAFE = 3.1415925


def shape_tables():
    i = np.arange(P)
    table = np.zeros((P, C_END), np.float32)
    table[:, C_ID:C_ID + P] = np.eye(P)
    table[:, C_TRI:C_TRI + P] = i[:, None] <= i[None, :]
    table[:, C_ONES:C_ONES + P] = 1.0
    causal = np.where(i[None, :] <= i[:, None], 0.0, NEG)
    table[:, C_MASK:C_MASK + P] = causal
    table[:, C_MASK + 2 * P:C_MASK + 3 * P] = causal
    line = np.linspace(0.0, 1.0, P, dtype=np.float32)
    table[:, C_FRET] = np.float32(1.0) / np.power(np.float32(10000.0), line)
    half = np.arange(0, ROPE, 2, dtype=np.float32) / np.float32(ROPE)
    table[:, C_FROPE] = np.tile(np.float32(1.0) / np.power(np.float32(10000.0), half), P // (ROPE // 2))
    decay = np.zeros((P, RET_HEADS, 3, P), np.float32)
    for h in range(RET_HEADS):
        log_g = np.log(1.0 - 2.0 ** (-5.0 - h))
        rel = i[None, :] - i[:, None]
        diag = np.where(rel >= 0, np.exp(log_g * np.maximum(rel, 0)), 0.0)
        decay[:, h, 0] = diag
        decay[:, h, 1] = np.exp(log_g * (rel + P))
        decay[:, h, 2] = diag
    decay *= RET_DK ** -0.5
    return table, decay.reshape(P, -1)


class Piece:

    def __init__(self, chunk, src, nk, k0, cols, order=None, rows=0):
        self.chunk, self.src, self.nk, self.k0, self.cols = chunk, src, nk, k0, cols
        self.order = order
        self.raw = nk * (rows or cols)
        self.size = nk * cols


class Chunk:

    def __init__(self, number, layout, acts, width, epilogue, **info):
        self.n, self.layout, self.acts, self.width, self.epilogue = number, layout, acts, width, epilogue
        self.info = info
        self.pieces = []
        self.banks = None


def plan(w):
    chunks, pieces, steps = [], [], []

    def chunk(layout, acts, width, epilogue, **info):
        c = Chunk(len(chunks), layout, acts, width, epilogue, **info)
        chunks.append(c)
        return c

    def rows(ap, k0, nk, c0, cols):
        return ap[k0 * P:(k0 + nk) * P, c0:c0 + cols].rearrange("(k p) n -> p k n", p=P)

    def load(c, ap, k0, nk, c0, cols=NCOL, order=None, acts_k0=None, src=None, width=None):
        p = Piece(c, src if src is not None else rows(ap, k0, nk, c0, cols), nk,
                  k0 if acts_k0 is None else acts_k0, width or cols, order, cols)
        p.n = len(pieces)
        pieces.append(p)
        c.pieces.append(p)
        steps.append(("piece", p))

    def whole(c, ap, c0, order=None):
        for k0 in range(0, KD, 4):
            load(c, ap, k0, 4, c0, order=order)

    def step(*s):
        steps.append(s)

    step("turn_x", 0)
    for n, c0 in enumerate((RQ, RQ + NCOL, RK, RK + NCOL)):
        c = chunk("feat", "x", NCOL, "rotate", rot=n, table=0, dst=4 * n)
        whole(c, w["w_in_even"], c0, order="pairs")
        step("epi", c)
    for n in range(4):
        c = chunk("tok", "x", NCOL, "copy_tok", dst=("R1", 2048, n * NCOL))
        whole(c, w["w_in_even"], RV + n * NCOL)
        step("epi", c)
    for h in range(RET_HEADS):
        c = chunk("tok", "x", NCOL, "silu_tok", dst=("R2", 2048, h * NCOL))
        load(c, w["w_in_even"], 0, 4, RG + h * NCOL)
        step("ret_scores", h)
        load(c, w["w_in_even"], 4, 4, RG + h * NCOL)
        step("epi", c)
        if h:
            step("ret_turn", h - 1)
        step("ret_values", h)
    c = chunk("feat", "x", NCOL, "keep_ranks")
    load(c, w["w_in_even"], 0, 4, MQ)
    load(c, w["w_in_even"], 4, 4, MQ)
    step("epi", c)
    step("ret_turn", RET_HEADS - 1)
    ck = chunk("feat", "x", NCOL, "rotate", rot=None, table=1, dst=None)
    load(ck, w["w_in_even"], 0, 8, MKR, ROPE, order="spread", width=2 * P)
    ck.width = 2 * P
    step("rank_sums", 0)
    step("epi", ck)
    for n in range(2):
        c = chunk("feat", "x", NCOL, "silu_feat", dst=("R1", n * 1024))
        load(c, w["w_in_even"], 0, 4, MG + n * NCOL)
        if n == 0:
            step("rank_spread", 0)
        load(c, w["w_in_even"], 4, 4, MG + n * NCOL)
        step("epi", c)
    uq = w["w_uq_even"].rearrange("(k p) (h n) -> p k h n", p=P, n=NOPE + ROPE)
    ukv = w["w_ukv_even"].rearrange("(k p) (h n) -> p k h n", p=P, n=2 * NOPE)
    for n in range(2):
        c = chunk("feat", "ranks", NCOL, "copy_feat", dst=("R3", n * 1024))
        load(c, None, 0, 2, 0, src=[uq[:, k, 4 * n:4 * n + 4, 0:NOPE] for k in range(2)], acts_k0=0)
        step("epi", c)
    c = chunk("feat", "ranks", NCOL, "rotate", rot=None, table=1, dst=None)
    load(c, None, 0, 2, 0, src=[uq[:, k, :, NOPE:NOPE + ROPE] for k in range(2)], acts_k0=0, order="halves")
    step("epi", c)
    for n in range(2):
        c = chunk("feat", "ranks", NCOL, "copy_feat", dst=("R3", 2048 + n * 1024))
        load(c, None, 0, 2, 0, src=[ukv[:, k, 4 * n:4 * n + 4, 0:NOPE] for k in range(2)], acts_k0=2)
        step("epi", c)
    for n in range(2):
        c = chunk("tok", "ranks", NCOL, "copy_tok", dst=("R1", 1024, 2048 + n * NCOL))
        load(c, None, 0, 2, 0, src=[ukv[:, k, 4 * n:4 * n + 4, NOPE:] for k in range(2)], acts_k0=2)
        step("epi", c)

    def pipeline(first, count, per_unit, between):
        for n in range(count + 4):
            if n < count:
                step("scores", first + n)
            if 1 <= n <= count:
                step("normalise", first + n - 1)
            for f in between.get(n, ()):
                f()
            if 2 <= n <= count + 1:
                step("turn", first + n - 2)
            m = n - 3
            if 0 <= m < count:
                step("values", first + m)
                if m % per_unit == per_unit - 1:
                    step("gate", UNIT[first + m])
            m = n - 4
            if m >= 0 and m % per_unit == per_unit - 1:
                step("low", UNIT[first + m])

    ys = [chunk("tok", "cat", NCOL, "residual", n=n) for n in range(2)]
    order = [(k0, n) for k0 in range(0, 24, 4) for n in range(2)]
    out_piece = [lambda k0=k0, n=n: load(ys[n], w["w_out_even"], k0, 4, n * NCOL) for k0, n in order]
    between = {n: [out_piece[n]] for n in range(8)}
    between[9] = [out_piece[8]]
    between[10] = [out_piece[9]]
    pipeline(0, MLA_HEADS, 1, between)
    out_piece[10]()
    step("epi", ys[0])
    out_piece[11]()
    step("epi", ys[1])
    step("layer_norm", 0)
    def halves_of(make, ap, c0, order=None):
        made = []

        def half(k0):
            if k0 == 0:
                made.append(make())
            load(made[0], ap, k0, 4, c0, order=order)
            if k0:
                step("epi", made[0])
        return [lambda: half(0), lambda: half(4)]

    def moba_part(part, n):
        c0 = 1024 * part + n * NCOL
        if part < 2:
            return halves_of(lambda: chunk("feat", "x", NCOL, "rotate", rot=part, table=1, dst=8 * part + 4 * n),
                             w["w_in_odd"], c0, order="halves")
        if part == 2:
            return halves_of(lambda: chunk("tok", "x", NCOL, "copy_tok", dst=("R1", 1024, n * NCOL)), w["w_in_odd"], c0)
        return halves_of(lambda: chunk("feat", "x", NCOL, "silu_feat", dst=("R1", 2048 + n * 1024)), w["w_in_odd"], c0)

    for part in range(3):
        for f in moba_part(part, 0):
            f()

    ys2 = []

    def moba_out(k0, n):
        if len(ys2) <= n:
            ys2.append(chunk("tok", "cat2", NCOL, "residual", n=n))
        load(ys2[n], w["w_out_odd"], k0, 2, n * NCOL)

    rest = moba_part(3, 0) + moba_part(0, 1) + moba_part(1, 1) + moba_part(2, 1) + moba_part(3, 1)
    between = {n: [f] for n, f in zip((0, 1, 2, 3, 4, 6, 7, 8, 10, 11), rest)}
    between.update({n: [lambda k0=k0, m=m: moba_out(k0, m)] for n, k0, m in ((12, 0, 0), (13, 0, 1), (14, 2, 0), (15, 2, 1), (17, 4, 0), (18, 4, 1))})
    pipeline(8, MOBA_HEADS, 2, between)
    moba_out(6, 0)
    step("epi", ys2[0])
    moba_out(6, 1)
    step("epi", ys2[1])
    step("layer_norm", 1)
    step("rms_norm", 0)
    c = chunk("tok", "x", SSD_HEADS, "copy_dt")
    load(c, w["w_in_2"], 0, 8, SDT, SSD_HEADS)
    step("epi", c)
    for n in range(3):
        c = chunk("feat", "x", NCOL, "conv_in", dst=4 * n)
        load(c, w["w_in_2"], 0, 4, SX + n * NCOL)
        step("conv", n - 1) if n else step("softplus", 0)
        load(c, w["w_in_2"], 4, 4, SX + n * NCOL)
        step("epi", c)
    between = [[("conv", 2)], [("ssd_cums", 0), ("ssd_cb", 0)], [("ssd_xs", 0)], [("ssd_xs", 1)], [("ssd_rows", 0)], [("ssd_rows", 1)],
               [("ssd_rows", 2)], [("ssd_rows", 3)], [("ssd_last", 0), ("ssd_gate", 0)], [("ssd_turn", 0)]]
    parts = []
    for n in range(2):
        parts += halves_of(lambda n=n: chunk("tok", "x", NCOL, "silu_tok", dst=("zb", 1024, n * NCOL)), w["w_in_2"], SZ + n * NCOL)
    for n in range(2):
        parts += halves_of(lambda n=n: chunk("feat", "x", NCOL, "copy_feat", dst=("R3", n * 1024)), w["w_in_2"], SQ + n * NCOL)
    parts += halves_of(lambda: chunk("tok", "x", NCOL, "copy_tok", dst=("R3", NCOL, 2048)), w["w_in_2"], SV)
    for f, sts in zip(parts, between):
        f()
        for st in sts:
            step(*st)
    ys3 = []

    def second_out(k0, n, nk=4):
        if len(ys3) <= n:
            ys3.append(chunk("tok", "cat2", NCOL, "add", n=n))
        load(ys3[n], w["w_out_2"], k0, nk, n * NCOL)

    pipeline(24, BAND_HEADS, 2, {n: [lambda k0=k0, m=m, nk=nk: second_out(k0, m, nk)] for n, k0, m, nk in
                                 ((1, 4, 0, 4), (3, 4, 1, 4), (5, 8, 0, 4), (7, 8, 1, 4), (9, 0, 0, 2), (10, 0, 1, 2))})
    second_out(2, 0, 2)
    step("epi", ys3[0])
    second_out(2, 1, 2)
    step("epi", ys3[1])
    step("rms_norm", 1)
    down = [chunk("tok", "ff", NCOL, "add", n=n) for n in range(2)]
    for c in range(FF_CHUNKS + 1):
        if c < FF_CHUNKS:
            u = chunk("feat", "x", NCOL, "relu2", dst=c)
            whole(u, w["w_ff1_2"], c * NCOL)
            step("epi", u)
        if c:
            for n in range(2):
                load(down[n], w["w_ff2_2"], 4 * (c - 1), 4, n * NCOL)
                if c == FF_CHUNKS:
                    step("epi", down[n])
    step("final", 0)
    return chunks, pieces, steps


UNIT = {a: a if a < 8 else (8 + (a - 8) // 2 if a < 24 else 16 + (a - 24) // 2) for a in range(32)}
LAST_OF_UNIT = {u: max(a for a in UNIT if UNIT[a] == u) for u in range(20)}


def cat_place(u):
    return ("cat", 16 + u) if u < 8 else ("cat2", u - 8 if u < 16 else u - 16)


def build(nc, w, out):
    chunks, pieces, steps = plan(w)
    order = {}
    for s in steps:
        if s[0] == "piece" and s[1].chunk.n not in order:
            order[s[1].chunk.n] = len(order)
    down = [c for c in chunks if c.acts == "ff"]
    turn = 0
    for c in sorted(chunks, key=lambda c: order[c.n]):
        if c in down:
            c.pair, c.turn = 2 + down.index(c), None
        else:
            c.pair, c.turn = turn % 2, turn
            turn += 1
    by_turn = {c.turn: c for c in chunks if c.turn is not None}
    READER = {"keep_ranks": "act", "copy_tok": "act", "copy_feat": "act", "conv_in": "act", "copy_dt": "dve"}
    reads = {"act": 0, "dve": 0}
    for s in steps:
        if s[0] == "epi":
            c = s[1]
            c.reader = READER.get(c.epilogue, "dve")
            reads[c.reader] += 1
            c.read_count = reads[c.reader]

    with ExitStack() as ctx:
        def sb(name, shape, dt=F32):
            return ctx.enter_context(nc.sbuf_tensor(name, shape, dt))

        def sem(name):
            return ctx.enter_context(nc.semaphore(name))

        cst = sb("cst", [P, C_END])
        raw = sb("raw", [P, RAW_SLOTS, 2048])
        w_hi = sb("w_hi", [P, 2, 2048], F32R)
        w_lo = sb("w_lo", [P, 2, 2048], F32R)
        res = sb("res", [P, T, D])
        x_hi = sb("x_hi", [P, KD, S], F32R)
        x_lo = sb("x_lo", [P, KD, S], F32R)
        R1 = sb("R1", [P, 4096])
        R2 = sb("R2", [P, 4096])
        R3 = sb("R3", [P, 4096])
        tmp = sb("tmp", [P, 2048])
        trig = sb("trig", [P, 2, 2, S])
        probs = sb("probs", [P, PROBS, 3 * P])
        turned = sb("turned", [P, 2, 3 * P])
        gated = sb("gated", [P, 2, S])
        cols = sb("cols", [P, 64])
        ssd_c = sb("ssd_c", [P, 10, 2 * SSD_HEADS])
        conv_c = sb("conv_c", [P, 5, CONV_TILES])
        stats = sb("stats", [P, 64])
        soft = sb("soft", [P, PROBS, 2, 2])
        with nc.sbuf_tensor("cat_hi", [P, 24, S], F32R) as cat_hi, nc.sbuf_tensor("cat_lo", [P, 24, S], F32R) as cat_lo:
            pass
        cat2_hi = sb("cat2_hi", [P, 16, S], F32R)
        cat2_lo = sb("cat2_lo", [P, 16, S], F32R)
        zb = sb("zb", [P, 4096])
        acc = ctx.enter_context(nc.psum_tensor("acc", [P, 4, 2, 512], F32))
        aux = acc[:, 2:4].rearrange("p a b n -> p (a b) n")

        ident = cst[:, C_ID:C_ID + P]
        tri = cst[:, C_TRI:C_TRI + P]
        ones = cst[:, C_ONES:C_ONES + P]
        causal = cst[:, C_MASK:C_MASK + 3 * P]
        decay = tmp[:, 0:RET_HEADS * 3 * P].rearrange("p (h n) -> p h n", h=RET_HEADS)
        region = {"R1": R1, "R2": R2, "R3": R3, "zb": zb}
        qn_col, kvn_col = cols[:, 0:2], cols[:, 2:4]
        ln_g_col, ln_b_col = cols[:, 4:20], cols[:, 20:36]
        mix_col, mlp_col = cols[:, 36:44], cols[:, 44:52]
        ssdn_col = cols[:, 52:60]
        half_neg = cols[:, 60:61]
        acts = {"x": (x_hi, x_lo), "ranks": (cat_hi[:, 20:24], cat_lo[:, 20:24]), "cat": (cat_hi, cat_lo),
                "cat2": (cat2_hi, cat2_lo), "ff": (cat2_hi, cat2_lo)}
        q_pe = R2[:, 0:1024].rearrange("p (g t s) -> p g t s", g=2, t=2)
        k_pe = R2[:, 1024:1536].rearrange("p (t s) -> p t s", t=2)
        bias = zb[:, 2048:4096].rearrange("p (h n) -> p h n", h=BAND_HEADS)
        conv_in = R2[:, 0:CONV_TILES * (S + 3)].rearrange("p (c s) -> p c s", c=CONV_TILES)
        conv_out = R1[:, 0:CONV_TILES * S].rearrange("p (c s) -> p c s", c=CONV_TILES)
        b_T, c_T = conv_out[:, 8:10], conv_out[:, 10:12]
        x_dt = R2[:, 0:2048].rearrange("p (b h n) -> p b h n", b=2, h=SSD_HEADS)
        y_ssd = R2[:, 2048:4096].rearrange("p (b h n) -> p b h n", b=2, h=SSD_HEADS)
        x_far = R3[:, 3072:4096].rearrange("p (h n) -> p h n", h=SSD_HEADS)
        y_far = tmp[:, 1024:2048].rearrange("p (h n) -> p h n", h=SSD_HEADS)
        cb = R1[:, 3072:3840].rearrange("p (b g n) -> p b g n", b=3, g=2)
        seg = R1[:, 0:2048].rearrange("p (i h n) -> p i h n", i=2, h=8)
        row_a = tmp[:, 0:1024].rearrange("p (h n) -> p h n", h=8)

        raw_landed = [sem(f"raw_landed{i}") for i in range(RAW_SLOTS)]
        names = ("tables_landed", "decay_landed", "x_landed", "pos_landed", "cols_landed", "dt_landed", "conv_landed", "gb_landed", "bias_landed",
                 "out_landed", "hi_ready", "lo_ready", "lo_ready_pool", "piece_used", "acc_read_act",
                 "acc_read_dve", "angles_ready", "trig_ready", "x_turned", "x_hi_ready", "x_lo_ready", "x_lo_odd", "x_lo_pool", "normed_lo_pool", "rot_products",
                 "rot_ready", "tanh_ready", "ret_scored", "ret_decayed", "ret_summed", "ret_centred", "ret_var",
                 "ret_rstd", "ret_scaled", "ret_turned", "ret_hi", "ret_lo", "squares_ready", "squares_summed",
                 "mean_square", "rank_rstd", "diag_ready", "ranks_spread", "ranks_scaled", "ranks_hi", "ranks_lo", "scores_ready", "scores_read",
                 "negmax_ready", "exp_ready", "probs_ready", "probs_turned", "turned_copied", "values_ready",
                 "out_read", "cat_hi_ready", "cat_lo_ready", "var_ready", "rstd_ready", "normed_ready", "normed_turned",
                 "scaled_ready", "normed_hi", "normed_lo", "res_ready", "pool_own", "dve_own", "act_own", "pe_own",
                 "conv_read", "conv_tanh", "dt_exp_in", "dt_exp", "dt_ln_in", "dt_ln", "a_ready", "rows_ready", "cums_ready",
                 "seg_rows", "seg_ready", "seg_exp", "m_ready", "silu_ready", "far_ready", "far_read", "cb_ready", "cb_read", "xs_turned", "xs_read", "y_near",
                 "y_far_ready", "y_read", "edge_ready", "edge_exp", "y_gated", "y_sq", "y_rstd", "relu_ready", "ff_hi", "ff_lo",
                 "half_ready", "cols_set", "pad_ready", "final_ready")
        sems = {n: sem(n) for n in names}

        def due(name, value):
            return sems[name], value

        block = ctx.enter_context(nc.Block())

        class Own:

            def __init__(self, eng, name):
                self.eng, self.name, self.counts, self.last = eng, name, {}, None

            def __call__(self, ins, name=None):
                name = name or self.name
                self.counts[name] = self.counts.get(name, 0) + 1
                self.last = (name, self.counts[name])
                ins.then_inc(sems[name], 1)

            def wait(self):
                self.eng.wait_ge(sems[self.last[0]], self.last[1])

        def backwards(h, n):
            return bass.AP(zb, 2048 + h * S + n - 1, [[4096, P], [-1, n]])

        def split_views(p, k0, k1):
            slot = p.n % 2
            r = raw[:, p.n % RAW_SLOTS, k0 * p.raw // p.nk:k1 * p.raw // p.nk]
            parts = [b[:, slot, k0 * p.cols:k1 * p.cols] for b in (w_hi, w_lo)]
            if p.order == "pairs":
                return [(r.rearrange("p (k f t) -> p k t f", t=2, f=P),
                         *[v.rearrange("p (k t f) -> p k t f", t=2, f=P) for v in parts])]
            if p.order == "halves":
                r = r.rearrange("p (g t s) -> p t g s", t=2, s=ROPE // 2)
                parts = [v.rearrange("p (k t h s) -> p t k h s", h=4, t=2, s=ROPE // 2) for v in parts]
                return [(r[:, t], parts[0][:, t], parts[1][:, t]) for t in range(2)]
            if p.order == "spread":
                r = r.rearrange("p (k t s) -> p k t s", k=p.nk, t=2)
                parts = [v.rearrange("p (k t r s) -> p k t r s", k=p.nk, t=2, r=4) for v in parts]
                return [(r, parts[0][:, :, :, c, :], parts[1][:, :, :, c, :]) for c in range(4)]
            return [(r, *parts)]

        def pool_share(p):
            return p.nk == 4

        n_pool = {}
        count = 0
        for p in pieces:
            count += pool_share(p)
            n_pool[p.n] = count
        n_spread = [p.n for p in pieces if p.order == "spread"]

        def hi_prep(eng, own, n):
            p = pieces[n]
            eng.wait_ge(raw_landed[n % RAW_SLOTS], 16 * p.loads)
            if n >= 2:
                eng.wait_ge(*due("piece_used", n - 1))
            for r, hi, _ in split_views(p, 0, p.nk):
                ins = eng.activation(hi, r, ACT.Copy)
            own(ins, "hi_ready")

        def lo_prep(eng, own, n, k0, k1, signal):
            p = pieces[n]
            eng.wait_ge(*due("hi_ready", n + 1))
            eng.wait_ge(raw_landed[n % RAW_SLOTS], 16 * p.loads)
            if n >= 2:
                eng.wait_ge(*due("piece_used", n - 1))
            for r, hi, lo in split_views(p, k0, k1):
                ins = eng.tensor_tensor(lo, r, hi.bitcast(F32), ALU.subtract)
            own(ins, signal)

        loads = [0] * RAW_SLOTS
        for p in pieces:
            srcs = p.src if isinstance(p.src, list) else [p.src]
            loads[p.n % RAW_SLOTS] += len(srcs)
            p.loads = loads[p.n % RAW_SLOTS]
            p.srcs = srcs

        MLA_COPIES = 4 + 1 + 2 + 2 + 2
        late = set()
        for s0, s1, s2 in zip(steps, steps[1:], steps[2:]):
            if s0[0] == "piece" and s1[0] == "epi" and s2[0] in ("layer_norm", "rms_norm"):
                late.add(s0[1].n)
        NORM = {("layer_norm", 0): 0, ("rms_norm", 0): 1, ("rms_norm", 1): 2}
        TURNS = {("layer_norm", 0): 0, ("rms_norm", 0): 4, ("ssd", 0): 8, ("rms_norm", 1): 12}
        Z_READS = max(c.read_count for c in chunks if c.epilogue == "silu_tok")
        tanh_n = {}
        for s in steps:
            if s[0] == "epi" and s[1].epilogue.startswith("silu"):
                tanh_n[s[1].n] = len(tanh_n) + 1
        rot_n = {}
        for s in steps:
            if s[0] == "epi" and s[1].epilogue == "rotate":
                rot_n[s[1].n] = len(rot_n)

        Y_READS = [max(c.read_count for c in chunks if c.epilogue == "residual" and c.acts == a) for a in ("cat", "cat2")]
        ff2_used = {c: max(p.n for p in pieces if p.chunk.acts == "ff" and p.k0 == 4 * c) + 1 for c in range(FF_CHUNKS)}

        def rot_products(n):
            base = 2048 * (n % 2)
            if 4 <= n < 6:
                return tmp[:, :].rearrange("p (q m s) -> p q m s", q=4, m=2)
            return R2[:, base:base + 2048].rearrange("p (q m s) -> p q m s", q=4, m=2)

        def rot_dst(c, n):
            if c.info["dst"] is not None:
                i = c.info["dst"]
                return R3[:, i * S:(i + 4) * S].rearrange("p (m t s) -> p m t s", m=2, t=2)
            return k_pe.rearrange("p (m t) s -> p m t s", m=1) if c.width == 2 * P else q_pe

        by = lambda e, f=None: [c.read_count for c in chunks if c.epilogue == e and (f is None or f(c))]
        GATE_READS = by("silu_feat", lambda c: True)
        GATE_READS = [GATE_READS[1], GATE_READS[2], GATE_READS[3]]
        SSD_READS = max(by("add", lambda c: c.acts == "cat2"))
        FINAL_READS = max(by("add", lambda c: c.acts == "ff"))
        CONV_READS = by("conv_in")

        def epi_dst(c):
            i = c.info["dst"]
            if c.layout == "tok":
                r, width, c0 = i
                if r == "R1" and width == 2048:
                    return R1[:, :].rearrange("p (t n) -> p t n", t=T)[:, :, c0:c0 + NCOL]
                if width == 2048:
                    return region[r][:, :].rearrange("p (t n) -> p t n", t=T)[:, :, c0:c0 + NCOL]
                base = (c0 // 2048) * 2048 if width == 1024 else 2048
                v = region[r][:, base:base + T * width].rearrange("p (t n) -> p t n", t=T)
                return v[:, :, c0 - base:c0 - base + NCOL]
            r, c0 = i
            return region[r][:, c0:c0 + 1024].rearrange("p (b n) -> p b n", b=2)

        @block.sync
        def _(sp):
            sp.dma_start(res[:, :, :], w["x"].rearrange("(t p) n -> p t n", p=P)).then_inc(sems["x_landed"], 16)
            sp.dma_start(cst[:, :], w["tables"]).then_inc(sems["tables_landed"], 16)
            for p in pieces:
                n = p.n
                if n >= RAW_SLOTS:
                    sp.wait_ge(*due("hi_ready", n - RAW_SLOTS + 1))
                    sp.wait_ge(*due("lo_ready", n - RAW_SLOTS + 1))
                    if n_pool[n - RAW_SLOTS]:
                        sp.wait_ge(*due("lo_ready_pool", n_pool[n - RAW_SLOTS]))
                per = p.raw // len(p.srcs)
                for i, src in enumerate(p.srcs):
                    dst = raw[:, n % RAW_SLOTS, i * per:(i + 1) * per]
                    if len(src.shape) == 3:
                        dst = dst.rearrange("p (a b) -> p a b", a=src.shape[1])
                    sp.dma_start(dst, src).then_inc(raw_landed[n % RAW_SLOTS], 16)
            for t in range(T):
                sp.wait_ge(*due("final_ready", t + 1))
                sp.dma_start(out[t * P:(t + 1) * P, :], tmp[:, t * D:(t + 1) * D]).then_inc(sems["out_landed"], 16)
            sp.wait_ge(*due("out_landed", 32))

        @block.tensor
        def _(pe):
            own = Own(pe, "pe_own")

            def ready_acts(c):
                if c.acts == "ranks":
                    pe.wait_ge(*due("ranks_hi", 1))
                    pe.wait_ge(*due("ranks_lo", 1))

            state = {"x": 0}

            def x_ready(tiles):
                n = state["x"]
                if n == 0:
                    pe.wait_ge(*due("x_hi_ready", tiles // 2))
                    pe.wait_ge(*due("x_lo_ready", tiles // 4))
                    pe.wait_ge(*due("x_lo_odd", tiles // 4))
                    return
                pe.wait_ge(*due("x_hi_ready", 4 * n + tiles // 2))
                pe.wait_ge(*due("x_lo_ready", 2 * n + tiles // 4))
                pe.wait_ge(*due("x_lo_pool", 2 * (n - 1) + tiles // 4))

            def product(p):
                c = p.chunk
                slot = p.n % 2
                hi, lo = acts[c.acts]
                if p is c.pieces[0]:
                    ready_acts(c)
                    if c.turn is not None and c.turn >= 2:
                        before = by_turn[c.turn - 2]
                        pe.wait_ge(*due("acc_read_" + before.reader, before.read_count))
                k_last = p.k0 + p.nk
                if c.acts == "x":
                    x_ready(k_last)
                if c.acts == "cat":
                    if p.k0 < 16:
                        pe.wait_ge(*due("ret_hi", 8))
                        pe.wait_ge(*due("ret_lo", 8))
                    else:
                        pe.wait_ge(*due("cat_hi_ready", k_last - 16))
                        pe.wait_ge(*due("cat_lo_ready", k_last - 16))
                if c.acts == "cat2":
                    if c.epilogue == "residual":
                        pe.wait_ge(*due("cat_hi_ready", 8 + k_last))
                        pe.wait_ge(*due("cat_lo_ready", 8 + k_last))
                    elif p.k0 < 4:
                        pe.wait_ge(*due("cat_hi_ready", 16 + k_last))
                        pe.wait_ge(*due("cat_lo_ready", 16 + k_last))
                    else:
                        pe.wait_ge(*due("normed_hi", 4))
                        pe.wait_ge(*due("normed_lo", 2))
                        pe.wait_ge(*due("normed_lo_pool", 2))
                k_acts = p.k0
                if c.acts == "ff":
                    pe.wait_ge(*due("ff_hi", p.k0 // 4 + 1))
                    pe.wait_ge(*due("ff_lo", p.k0 // 4 + 1))
                    k_acts = p.k0 % 16
                pe.wait_ge(*due("hi_ready", p.n + 1))
                pe.wait_ge(*due("lo_ready", p.n + 1))
                if n_pool[p.n]:
                    pe.wait_ge(*due("lo_ready_pool", n_pool[p.n]))
                wh = w_hi[:, slot, 0:p.size].rearrange("p (k n) -> p k n", k=p.nk)
                wl = w_lo[:, slot, 0:p.size].rearrange("p (k n) -> p k n", k=p.nk)
                first, last = p is c.pieces[0], p is c.pieces[-1]
                for k in range(p.nk):
                    start, stop = first and k == 0, last and k == p.nk - 1
                    ka = k_acts + k
                    if c.layout == "tok":
                        for t in range(T):
                            o = acc[:, c.pair, t, 0:p.cols]
                            xh, xl = hi[:, ka, t * P:(t + 1) * P], lo[:, ka, t * P:(t + 1) * P]
                            pe.matmul(o, xh, wh[:, k, :], start=start, stop=False)
                            pe.matmul(o, xh, wl[:, k, :], start=False, stop=False)
                            ins = pe.matmul(o, xl, wh[:, k, :], start=False, stop=stop)
                    else:
                        for f in range(p.cols // P):
                            o = acc[:, c.pair, f // 2, (f % 2) * S:(f % 2 + 1) * S]
                            fs = slice(f * P, (f + 1) * P)
                            pe.matmul(o, wh[:, k, fs], hi[:, ka, :], start=start and f % 2 == 0, stop=False, skip_group_check=True)
                            pe.matmul(o, wh[:, k, fs], lo[:, ka, :], start=False, stop=False, skip_group_check=True)
                            ins = pe.matmul(o, wl[:, k, fs], hi[:, ka, :], start=False, stop=stop, skip_group_check=True)
                own(ins, "piece_used")

            def turn_tokens(src, per_bank_signal, wait_reads=None):
                for f in range(KD):
                    for t in range(T):
                        ins = pe.transpose(aux[:, f // 2, (f % 2) * S + t * P:(f % 2) * S + (t + 1) * P],
                                           src[:, t, f * P:(f + 1) * P], ident)
                    if f % 2:
                        ins.then_inc(sems[per_bank_signal], 1)

            def near(i):
                b, g = i // 2, i % 2
                pe.wait_ge(*due("m_ready", i + 1))
                if i >= 2:
                    pe.wait_ge(*due("y_read", i - 1))
                if i == 0:
                    pe.wait_ge(*due("far_read", 1))
                for h in range(8):
                    ins = pe.matmul(aux[:, 2 + g, h * SSD_P:(h + 1) * SSD_P], seg[:, i % 2, h, :],
                                    x_dt[:, b, 8 * g + h, :], start=True, stop=True)
                own(ins, "y_near")

            normed = tmp[:, :].rearrange("p (t n) -> p t n", t=T)
            v_ret = R1[:, :].rearrange("p (t n) -> p t n", t=T)
            norms = [0]
            for s in steps:
                kind, i = s
                if kind == "piece":
                    product(i)
                elif kind == "turn_x":
                    pe.wait_ge(*due("x_landed", 16))
                    pe.wait_ge(*due("tables_landed", 16))
                    turn_tokens(res, "x_turned")
                elif kind == "ret_scores":
                    h = i
                    if h == 0:
                        pe.wait_ge(*due("rot_ready", 4))
                        x_ready(8)
                    else:
                        pe.wait_ge(*due("ret_decayed", h))
                    if h >= 2:
                        pe.wait_ge(*due("ret_lo", 2 * h - 2))
                    q = R3[:, 0:2048].rearrange("p (f s) -> p f s", f=8)
                    k = R3[:, 2048:4096].rearrange("p (f s) -> p f s", f=8)
                    for j, (o0, i0, n) in enumerate(((0, 0, S), (S, P, P))):
                        for t in range(2):
                            ins = pe.matmul(aux[:, 0, o0:o0 + n], k[:, 2 * h + t, j * P:(j + 1) * P],
                                            q[:, 2 * h + t, i0:i0 + n], start=(t == 0), stop=(t == 1))
                    own(ins, "ret_scored")
                elif kind == "ret_values":
                    h = i
                    pe.wait_ge(*due("ret_decayed", h + 1))
                    pe.wait_ge(*due("acc_read_act", 4))
                    if h:
                        pe.wait_ge(*due("ret_centred", h))
                    pr = probs[:, h % 2, :]
                    vs = slice(h * RET_DV, (h + 1) * RET_DV)
                    pe.matmul(aux[:, 2, :], pr[:, 0:P], v_ret[:, 0, vs], start=True, stop=True)
                    pe.matmul(aux[:, 3, :], pr[:, P:2 * P], v_ret[:, 0, vs], start=True, stop=False)
                    pe.matmul(aux[:, 3, :], pr[:, 2 * P:3 * P], v_ret[:, 1, vs], start=False, stop=True).then_inc(sems["ret_summed"], 1)
                elif kind == "ret_turn":
                    h = i
                    gate = R2[:, :].rearrange("p (t n) -> p t n", t=T)
                    pe.wait_ge(*due("ret_scaled", h + 1))
                    for half in range(2):
                        n = 2 * h + half
                        if n >= 2:
                            pe.wait_ge(*due("ret_lo", n - 1))
                        if half:
                            pe.wait_ge(*due("ret_decayed", min(h + 2, RET_HEADS)))
                        for f in range(2):
                            for t in range(T):
                                c0 = h * RET_DV + (2 * half + f) * P
                                ins = pe.transpose(aux[:, 1 - half, f * S + t * P:f * S + (t + 1) * P], gate[:, t, c0:c0 + P], ident)
                        own(ins, "ret_turned")
                elif kind == "scores":
                    a = i
                    if a == 0:
                        pe.wait_ge(*due("ret_lo", 8))
                        pe.wait_ge(*due("acc_read_act", MLA_COPIES))
                        pe.wait_ge(*due("rot_ready", 6))
                    if a == 8:
                        pe.wait_ge(*due("rot_ready", 8))
                    if a == 16:
                        pe.wait_ge(*due("rot_ready", 10))
                    if a == 24:
                        pe.wait_ge(*due("acc_read_act", MLA_COPIES + 2 + 3 + 3))
                        pe.wait_ge(*due("normed_lo", 2))
                    if a >= 2:
                        pe.wait_ge(*due("scores_read", a - 1))
                    bank = aux[:, 3 * (a % 2), :]
                    for o0, q0, n in ((0, 0, P), (P, P, S)):
                        o = bank[:, o0:o0 + n]
                        if a < 8:
                            g, r = a // 4, 32 * (a % 4)
                            qn = R3[:, a * S:(a + 1) * S]
                            kn = R3[:, 2048 + a * S:2048 + (a + 1) * S]
                            pe.matmul(o, qn[:, q0:q0 + P], kn[:, 0:n], start=True, stop=False)
                            for t in range(2):
                                ins = pe.matmul(o, q_pe[r:r + 32, g, t, q0:q0 + P], k_pe[r:r + 32, t, 0:n],
                                                start=False, stop=(t == 1), tile_position=(r, 0))
                        elif a < 24:
                            g, r = (a - 8) // 4, 32 * (a % 4)
                            qk = R3[:, :].rearrange("p (q g t s) -> p q g t s", q=2, g=4, t=2)
                            for t in range(2):
                                ins = pe.matmul(o, qk[r:r + 32, 0, g, t, q0:q0 + P], qk[r:r + 32, 1, g, t, 0:n],
                                                start=(t == 0), stop=(t == 1), tile_position=(r, 0))
                        else:
                            g, r = (a - 24) // 2, 64 * (a % 2)
                            qk = R3[:, 0:2048].rearrange("p (q g s) -> p q g s", q=2, g=4)
                            ins = pe.matmul(o, qk[r:r + 64, 0, g, q0:q0 + P], qk[r:r + 64, 1, g, 0:n],
                                            start=True, stop=True, tile_position=(r, 0))
                    own(ins, "scores_ready")
                elif kind == "turn":
                    a = i
                    pe.wait_ge(*due("probs_ready", a + 1))
                    if a:
                        pe.wait_ge(*due("turned_copied", a))
                    pr = probs[:, a % PROBS, :]
                    for o0, c0 in ((0, 0), (P, P), (2 * P, 2 * P)):
                        ins = pe.transpose(aux[:, 1, o0:o0 + P], pr[:, c0:c0 + P], ident)
                    own(ins, "probs_turned")
                elif kind == "values":
                    a = i
                    u = UNIT[a]
                    pe.wait_ge(*due("turned_copied", a + 1))
                    if u:
                        pe.wait_ge(*due("out_read", u))
                    if a in (8, 16):
                        pe.wait_ge(*due("acc_read_act", MLA_COPIES + a // 8))
                    tp = turned[:, a % 2, :]
                    if a < 8:
                        v, vs, rows = R1[:, 2048:4096].rearrange("p (t n) -> p t n", t=T), slice(a * P, (a + 1) * P), slice(0, P)
                    elif a < 24:
                        h, r = a - 8, 64 * (a % 2)
                        v, vs, rows = R1[:, 0:2048].rearrange("p (t n) -> p t n", t=T), slice(h * DH, (h + 1) * DH), slice(r, r + 64)
                    else:
                        h, r = a - 24, 64 * (a % 2)
                        v, vs, rows = R3[:, 2048:3072].rearrange("p (t n) -> p t n", t=T), slice(h * DH, (h + 1) * DH), slice(r, r + 64)
                    o = aux[rows, 2, (u % 2) * S:(u % 2 + 1) * S]
                    pe.matmul(o, v[:, 0, vs], tp[:, 0:S], start=True, stop=False, skip_group_check=True)
                    pe.matmul(o[:, P:S], v[:, 1, vs], tp[:, S:3 * P], start=False, stop=True,
                              skip_group_check=True).then_inc(sems["values_ready"], 1)
                elif kind == "layer_norm" or kind == "rms_norm":
                    if kind == "layer_norm" and i == 1:
                        continue
                    pe.wait_ge(*due("normed_ready", NORM[kind, i] + 1))
                    turn_tokens(normed, "normed_turned")
                    state["x"] += 1
                elif kind == "rank_sums":
                    pe.wait_ge(*due("squares_ready", 1))
                    pe.wait_ge(*due("ret_lo", 8))
                    sq = R3[:, 0:1024].rearrange("p (k s) -> p k s", k=4)
                    for r in range(2):
                        for t in range(T):
                            for k in range(2):
                                ins = pe.matmul(aux[:, 0, 2 * r + t:2 * r + t + 1], sq[:, 2 * r + k, t * P:(t + 1) * P],
                                                ones[:, 0:1], start=(k == 0), stop=(k == 1))
                    own(ins, "squares_summed")
                elif kind == "rank_spread":
                    pe.wait_ge(*due("diag_ready", 1))
                    own(pe.matmul(aux[:, 3, :], ones, R3[:, 1024:1536], start=True, stop=True), "ranks_spread")
                elif kind == "ssd_cums":
                    pe.wait_ge(*due("a_ready", 1))
                    a = ssd_c[:, 2, :]
                    pe.matmul(aux[:, 0, 0:32], tri, a, start=True, stop=True)
                    own(pe.matmul(aux[:, 0, 32:64], ones, a, start=True, stop=True), "cums_ready")
                elif kind == "ssd_cb":
                    pe.wait_ge(*due("silu_ready", 3))
                    for b, (s0, l0) in enumerate(((0, 0), (P, P), (0, P))):
                        for g in range(2):
                            n = 2 * b + g
                            ins = pe.matmul(aux[:, 2 + n // 4, (n % 4) * P:(n % 4 + 1) * P], b_T[:, g, s0:s0 + P],
                                            c_T[:, g, l0:l0 + P], start=True, stop=True)
                    own(ins, "cb_ready")
                elif kind == "ssd_xs":
                    pe.wait_ge(*due("edge_ready", 1) if i == 0 else due("cb_read", 1))
                    for f in range(8):
                        ins = pe.transpose(aux[:, 2 * i + f // 4, (f % 4) * P:(f % 4 + 1) * P], conv_out[:, f, i * P:(i + 1) * P], ident)
                    own(ins, "xs_turned")
                elif kind == "ssd_rows":
                    if i:
                        near(i - 1)
                    pe.wait_ge(*due("rows_ready", i + 1))
                    if i == 0:
                        pe.wait_ge(*due("xs_read", 1))
                    for q in range(2):
                        n = 2 * i + q
                        if n >= 2:
                            pe.wait_ge(*due("seg_rows", n - 1))
                        own(pe.matmul(aux[:, q, :], ones, tmp[:, q * 512:(q + 1) * 512], start=True, stop=True), "cums_ready")
                    if i == 0:
                        pe.wait_ge(*due("far_ready", 1))
                        for g in range(2):
                            ins = pe.matmul(aux[:, 2 + g, :], cb[:, 2, g, :],
                                            x_far[:, 8 * g:8 * g + 8, :].rearrange("p h n -> p (h n)"), start=True, stop=True)
                        own(ins, "y_far_ready")
                elif kind == "ssd_last":
                    near(3)
                elif kind == "ssd_turn":
                    pe.wait_ge(*due("y_gated", 1))
                    turn_tokens(R2[:, 2048:4096].rearrange("p (t n) -> p t n", t=T), "normed_turned")
                elif kind == "final":
                    pass

        def low_share(eng, own, b, src, hi, lo, hi_name, hi_base, lo_name):
            eng.wait_ge(*due(hi_name, hi_base + b + 1))
            ks = slice(2 * b, 2 * b + 2)
            own(eng.tensor_tensor(lo[:, ks, :], src[:, b * 512:(b + 1) * 512].rearrange("p (f s) -> p f s", f=2),
                                  hi[:, ks, :].bitcast(F32), ALU.subtract), lo_name)

        @block.scalar
        def _(act):
            own = Own(act, "act_own")
            act.dma_start(cols[:, 0:2], w["q_norm_even"].rearrange("a (k p) -> p (a k)", p=P), allow_slow_non_contiguous=True).then_inc(sems["cols_landed"], 16)
            act.dma_start(cols[:, 2:4], w["kv_norm_even"].rearrange("a (k p) -> p (a k)", p=P), allow_slow_non_contiguous=True).then_inc(sems["cols_landed"], 16)
            for l in range(2):
                act.dma_start(cols[:, 4 + 8 * l:12 + 8 * l], w["ln_g"][l:l + 1].rearrange("a (k p) -> p (a k)", p=P), allow_slow_non_contiguous=True).then_inc(sems["cols_landed"], 16)
                act.dma_start(cols[:, 20 + 8 * l:28 + 8 * l], w["ln_b"][l:l + 1].rearrange("a (k p) -> p (a k)", p=P), allow_slow_non_contiguous=True).then_inc(sems["cols_landed"], 16)
            for c0, name in ((36, "norm_mix_w_2"), (44, "norm_mlp_w_2"), (52, "ssd_norm_w_2")):
                act.dma_start(cols[:, c0:c0 + 8], w[name].rearrange("a (k p) -> p (a k)", p=P), allow_slow_non_contiguous=True).then_inc(sems["cols_landed"], 16)
            for s in steps:
                kind, i = s
                if kind == "piece":
                    if i.n + 2 < len(pieces):
                        hi_prep(act, own, i.n + 2)
                elif kind == "turn_x":
                    for b in range(4):
                        act.wait_ge(*due("x_turned", b + 1))
                        own(act.activation(x_hi[:, 2 * b:2 * b + 2, :], aux[:, b, :].rearrange("p (f s) -> p f s", f=2),
                                       ACT.Copy), "x_hi_ready")
                    for n in range(2):
                        hi_prep(act, own, n)
                    for n in range(2):
                        act.wait_ge(*due("angles_ready", n + 1))
                        own(act.activation(trig[:, n, :, :], trig[:, n, :, :], ACT.Sin), "trig_ready")
                elif kind == "epi":
                    c = i
                    a2 = acc[:, c.pair, :, :]
                    if c.epilogue in ("copy_tok", "copy_feat"):
                        act.wait_ge(*due("piece_used", c.pieces[-1].n + 1))
                        own(act.activation(epi_dst(c), a2, ACT.Copy), "acc_read_act")
                    elif c.epilogue.startswith("silu"):
                        act.wait_ge(*due("piece_used", c.pieces[-1].n + 1))
                        own(act.activation(epi_dst(c), a2, ACT.Tanh, scale=0.5), "tanh_ready")
                    elif c.epilogue == "keep_ranks":
                        act.wait_ge(*due("piece_used", c.pieces[-1].n + 1))
                        own(act.activation(R3[:, 0:1024].rearrange("p (b n) -> p b n", b=2), a2, ACT.Square), "squares_ready")
                        own(act.activation(R3[:, 2048:3072].rearrange("p (b n) -> p b n", b=2), a2, ACT.Copy), "acc_read_act")
                    elif c.epilogue == "conv_in":
                        act.wait_ge(*due("piece_used", c.pieces[-1].n + 1))
                        act.wait_ge(*due("pad_ready", 1))
                        for b in range(2):
                            f = c.info["dst"] + 2 * b
                            ins = act.activation(conv_in[:, f:f + 2, 3:], a2[:, b, :].rearrange("p (f s) -> p f s", f=2), ACT.Copy)
                        own(ins, "acc_read_act")
                    elif c.epilogue == "relu2":
                        n = c.info["dst"]
                        act.wait_ge(*due("piece_used", c.pieces[-1].n + 1))
                        if n:
                            act.wait_ge(*due("acc_read_dve", c.read_count - 1))
                        own(act.activation(tmp[:, 0:1024].rearrange("p (b n) -> p b n", b=2), a2, ACT.Relu), "relu_ready")
                        act.wait_ge(*due("acc_read_dve", c.read_count))
                        if n >= 4:
                            act.wait_ge(*due("piece_used", ff2_used[n - 4]))
                        own(act.activation(cat2_hi[:, 4 * (n % 4):4 * (n % 4) + 4, :].rearrange("p k s -> p (k s)"), tmp[:, 1024:2048],
                                       ACT.Copy), "ff_hi")
                elif kind == "rank_spread":
                    act.wait_ge(*due("ranks_scaled", 1))
                    own(act.activation(cat_hi[:, 20:24, :].rearrange("p k s -> p (k s)"), R3[:, 2048:3072], ACT.Copy), "ranks_hi")
                elif kind == "ret_values":
                    h = i
                    gate = R2[:, :].rearrange("p (t n) -> p t n", t=T)
                    act.wait_ge(*due("ret_centred", h + 1))
                    act.wait_ge(*due("ret_rstd", h + 1))
                    for t in range(T):
                        v = gate[:, t, h * RET_DV:(h + 1) * RET_DV]
                        ins = act.activation(v, v, ACT.Copy, scale=stats[:, 40 + 2 * (h % 2) + t:41 + 2 * (h % 2) + t])
                    own(ins, "ret_scaled")
                elif kind == "ret_turn":
                    for half in range(2):
                        n = 2 * i + half
                        act.wait_ge(*due("ret_turned", n + 1))
                        own(act.activation(cat_hi[:, 2 * n:2 * n + 2, :], aux[:, 1 - half, :].rearrange("p (f s) -> p f s", f=2),
                                       ACT.Copy), "ret_hi")
                elif kind == "scores":
                    a = i
                    act.wait_ge(*due("negmax_ready", a + 1))
                    pr = probs[:, a % PROBS, :]
                    nm, sm = soft[:, a % PROBS, 0, :], soft[:, a % PROBS, 1, :]
                    act.activation(pr[:, 0:P], pr[:, 0:P], ACT.Exp, bias=nm[:, 0:1], accum_out=sm[:, 0:1])
                    own(act.activation(pr[:, P:], pr[:, P:], ACT.Exp, bias=nm[:, 1:2], accum_out=sm[:, 1:2]), "exp_ready")
                elif kind == "turn":
                    a = i
                    act.wait_ge(*due("probs_turned", a + 1))
                    if a >= 2:
                        act.wait_ge(*due("values_ready", a - 1))
                    own(act.activation(turned[:, a % 2, :], aux[:, 1, 0:3 * P], ACT.Copy), "turned_copied")
                elif kind == "gate":
                    u = i
                    act.wait_ge(*due("out_read", u + 1))
                    b, tile = cat_place(u)
                    if u == 8:
                        act.wait_ge(*due("acc_read_dve", Y_READS[0]))
                    if u == 16:
                        act.wait_ge(*due("acc_read_dve", Y_READS[1]))
                    own(act.activation(acts[b][0][:, tile, :], gated[:, u % 2, :], ACT.Copy), "cat_hi_ready")
                elif kind in ("layer_norm", "rms_norm") and (kind, i) in NORM:
                    t0 = TURNS[kind, i]
                    for b in range(4):
                        act.wait_ge(*due("scaled_ready", t0 + b + 1))
                        own(act.activation(x_hi[:, 2 * b:2 * b + 2, :], R1[:, b * 512:(b + 1) * 512].rearrange("p (f s) -> p f s", f=2),
                                       ACT.Copy), "x_hi_ready")
                elif kind == "conv":
                    n = i
                    act.wait_ge(*due("conv_read", n + 1))
                    own(act.activation(conv_in[:, 4 * n:4 * n + 4, 0:S], conv_out[:, 4 * n:4 * n + 4, :], ACT.Tanh), "conv_tanh")
                elif kind == "softplus":
                    act.wait_ge(*due("dt_exp_in", 1))
                    act.wait_ge(*due("dt_landed", 48))
                    act.activation(ssd_c[:, 3, :], ssd_c[:, 3, :], ACT.Exp)
                    own(act.activation(ssd_c[:, 5, 0:16], ssd_c[:, 5, 0:16], ACT.Exp), "dt_exp")
                    act.wait_ge(*due("dt_ln_in", 1))
                    own(act.activation(ssd_c[:, 6, :], ssd_c[:, 4, :], ACT.Ln), "dt_ln")
                elif kind == "ssd_cums":
                    act.wait_ge(*due("edge_ready", 1))
                    act.activation(ssd_c[:, 7, :], ssd_c[:, 7, :], ACT.Exp)
                    own(act.activation(ssd_c[:, 8, :], ssd_c[:, 8, :], ACT.Exp), "edge_exp")
                elif kind == "ssd_rows":
                    act.wait_ge(*due("seg_ready", i + 1))
                    own(act.activation(seg[:, i % 2], seg[:, i % 2], ACT.Exp), "seg_exp")
                elif kind == "ssd_turn":
                    t0 = TURNS["ssd", 0]
                    for b in range(4):
                        act.wait_ge(*due("scaled_ready", t0 + b + 1))
                        own(act.activation(cat2_hi[:, 4 + 2 * b:6 + 2 * b, :], tmp[:, b * 512:(b + 1) * 512].rearrange("p (f s) -> p f s", f=2),
                                       ACT.Copy), "normed_hi")

        @block.vector
        def _(dve):
            own = Own(dve, "dve_own")
            rot = [0]

            def low_prep(n):
                p = pieces[n]
                lo_prep(dve, own, n, 0, 3 if pool_share(p) else p.nk, "lo_ready")

            def angles():
                dve.wait_ge(*due("pos_landed", 16))
                dve.wait_ge(*due("tables_landed", 16))
                pos = R1[:, 256:512]
                own(dve.tensor_copy(pos, R1[:, 0:256].bitcast(I32)))
                n_turn, ang = R1[:, 512:768], R1[:, 768:1024]
                c1 = 6.28125
                c2 = float(np.float32(np.floor((TWO_PI - c1) * 2 ** 20) / 2 ** 20))
                c3 = float(np.float32(TWO_PI - c1 - c2))
                magic = 1.5 * 2 ** 23
                for n, col in ((0, C_FRET), (1, C_FROPE)):
                    own.wait()
                    own(dve.tensor_scalar(ang, pos, cst[:, col:col + 1], None, ALU.mult))
                    own.wait()
                    own(dve.tensor_scalar(n_turn, ang, 1.0 / TWO_PI, magic, ALU.mult, ALU.add))
                    own.wait()
                    own(dve.tensor_scalar(n_turn, n_turn, magic, None, ALU.subtract))
                    for c in (c1, c2, c3):
                        own.wait()
                        own(dve.scalar_tensor_tensor(ang, n_turn, -c, ang, ALU.mult, ALU.add))
                    own.wait()
                    own(dve.tensor_scalar(trig[:, n, 0, :], ang, PI_SAFE, -PI_SAFE, ALU.min, ALU.max))
                    own(dve.tensor_scalar(ang, ang, 0.5 * np.pi, None, ALU.add))
                    own.wait()
                    own(dve.tensor_scalar(n_turn, ang, np.pi, -TWO_PI, ALU.is_gt, ALU.mult))
                    own.wait()
                    own(dve.tensor_tensor(ang, ang, n_turn, ALU.add))
                    own.wait()
                    own(dve.tensor_scalar(trig[:, n, 1, :], ang, PI_SAFE, -PI_SAFE, ALU.min, ALU.max), "angles_ready")

            def row_stats(src, count, at, slot):
                st = stats[:, at:at + 6 * count]
                for m in range(count):
                    own(dve.bn_stats(st[:, 6 * m:6 * m + 6], src[:, m * 512:(m + 1) * 512]))
                own.wait()
                own(dve.bn_aggr(slot, st))

            def half_stats(half):
                for t in range(T):
                    own(dve.bn_stats(stats[:, 8 + 12 * t + 6 * half:14 + 12 * t + 6 * half], res[:, t, half * 512:(half + 1) * 512]))

            def row_rstd(kind, i):
                n = NORM_ALL[kind, i]
                mv = stats[:, 32:36].rearrange("p (t n) -> p t n", t=T)
                if kind == "rms_norm" and i == 0:
                    own.wait()
                    for half in range(2):
                        half_stats(half)
                own.wait()
                for t in range(T):
                    own(dve.bn_aggr(mv[:, t, :], stats[:, 8 + 12 * t:20 + 12 * t]))
                own.wait()
                if kind == "layer_norm":
                    own(dve.tensor_scalar(stats[:, 36:38], mv[:, :, 1], LN_EPS, None, ALU.add), "var_ready")
                else:
                    own(dve.tensor_tensor(stats[:, 38:40], mv[:, :, 0], mv[:, :, 0], ALU.mult))
                    own.wait()
                    own(dve.scalar_tensor_tensor(stats[:, 36:38], stats[:, 38:40], LN_EPS, mv[:, :, 1], ALU.add, ALU.add), "var_ready")
                dve.wait_ge(*due("rstd_ready", n + 1))
                return mv

            def full_norm(kind, i):
                mv = row_rstd(kind, i)
                for t in range(T):
                    o = tmp[:, t * D:(t + 1) * D]
                    signal = "normed_ready" if t == T - 1 and (kind, i) in NORM else None
                    if kind == "layer_norm":
                        own(dve.tensor_scalar(o, res[:, t, :], mv[:, t, 0:1], stats[:, 44 + t:45 + t], ALU.subtract, ALU.mult), signal)
                    else:
                        own(dve.tensor_scalar(o, res[:, t, :], stats[:, 44 + t:45 + t], None, ALU.mult), signal)

            NORM_ALL = {("layer_norm", 0): 0, ("layer_norm", 1): 1, ("rms_norm", 0): 2, ("rms_norm", 1): 3, ("final", 0): 4}

            def scaled_split(t0, gain, offset, dst, hi, lo, hi_name, hi_base, lo_name):
                for b in range(4):
                    dve.wait_ge(*due("normed_turned", t0 + b + 1))
                    for f in range(2):
                        k = 2 * b + f
                        src = aux[:, b, f * S:(f + 1) * S]
                        o = dst[:, k * S:(k + 1) * S]
                        if offset is None:
                            own(dve.tensor_scalar(o, src, gain[:, k:k + 1], None, ALU.mult), "scaled_ready" if f else None)
                        else:
                            own(dve.tensor_scalar(o, src, gain[:, k:k + 1], offset[:, k:k + 1], ALU.mult, ALU.add), "scaled_ready" if f else None)
                    if b % 2:
                        low_share(dve, own, b - 1, dst, hi, lo, hi_name, hi_base, lo_name)

            def masked(i):
                b, g = i // 2, i % 2
                dve.wait_ge(*due("seg_exp", i + 1))
                dve.wait_ge(*due("cb_read", 1))
                own(dve.tensor_tensor(seg[:, i % 2], seg[:, i % 2], cb[:, b, g:g + 1, :].to_broadcast([P, 8, P]), ALU.mult), "m_ready")

            def finish(i):
                b, g = i // 2, i % 2
                dve.wait_ge(*due("y_near", i + 1))
                y = y_ssd[:, b, 8 * g:8 * g + 8, :].rearrange("p h n -> p (h n)")
                own(dve.tensor_tensor(y, y, aux[:, 2 + g, :], ALU.add), "y_read")
                own.wait()
                own(dve.tensor_tensor(y, y, zb[:, i * 512:(i + 1) * 512], ALU.mult))
                own.wait()
                own(dve.bn_stats(stats[:, 8 + 6 * i:14 + 6 * i], y))

            for s in steps:
                kind, i = s
                if kind == "piece":
                    last_piece = i.n
                    if i.n + 2 < len(pieces) and i.n not in late:
                        low_prep(i.n + 2)
                elif kind == "turn_x":
                    for b in range(4):
                        dve.wait_ge(*due("x_hi_ready", b + 1))
                        dve.wait_ge(*due("x_turned", b + 1))
                        ks = slice(2 * b, 2 * b + 2)
                        ins = dve.tensor_tensor(x_lo[:, ks, :], aux[:, b, :].rearrange("p (f s) -> p f s", f=2),
                                                x_hi[:, ks, :].bitcast(F32), ALU.subtract)
                        own(ins, "x_lo_ready" if b % 2 == 0 else "x_lo_odd")
                    low_prep(0)
                    low_prep(1)
                    angles()
                elif kind == "epi":
                    c = i
                    a2 = acc[:, c.pair, :, :]
                    if c.epilogue == "rotate":
                        n = rot_n[c.n]
                        dve.wait_ge(*due("piece_used", c.pieces[-1].n + 1))
                        dve.wait_ge(*due("trig_ready", 2))
                        if n >= 2:
                            dve.wait_ge(*due("rot_ready", n if n in (4, 5) else n - 1))
                        if n == 6:
                            dve.wait_ge(*due("res_ready", 1))
                        m = 1 if c.width == 2 * P else 2
                        pr = rot_products(n)
                        sin = trig[:, c.info["table"], 0:1, :].to_broadcast([P, m, S])
                        cos = trig[:, c.info["table"], 1:2, :].to_broadcast([P, m, S])
                        first, second = a2[:, 0:m, 0:S], a2[:, 0:m, S:2 * S]
                        for q, (part, f) in enumerate(((first, cos), (second, sin), (second, cos), (first, sin))):
                            ins = dve.tensor_tensor(pr[:, q, 0:m, :], part, f, ALU.mult)
                            if q < 3:
                                own(ins)
                        own(ins, "acc_read_dve")
                    elif c.epilogue.startswith("silu"):
                        dve.wait_ge(*due("piece_used", c.pieces[-1].n + 1))
                        dve.wait_ge(*due("tanh_ready", tanh_n[c.n]))
                        o = epi_dst(c)
                        own(dve.scalar_tensor_tensor(o, o, 1.0, a2, ALU.add, ALU.mult), "acc_read_dve")
                    elif c.epilogue in ("residual", "add"):
                        dve.wait_ge(*due("piece_used", c.pieces[-1].n + 1))
                        r = res[:, :, c.info["n"] * NCOL:(c.info["n"] + 1) * NCOL]
                        if c.acts == "cat2" and c.epilogue == "residual":
                            dve.wait_ge(*due("res_ready", 1))
                        scale = DN_ALPHA if c.epilogue == "residual" else 1.0
                        own(dve.scalar_tensor_tensor(r, r, scale, a2, ALU.mult, ALU.add), "acc_read_dve")
                        own.wait()
                        half_stats(c.info["n"])
                    elif c.epilogue == "copy_dt":
                        dve.wait_ge(*due("piece_used", c.pieces[-1].n + 1))
                        dve.wait_ge(*due("dt_landed", 48))
                        v = ssd_c[:, 0, :].rearrange("p (t n) -> p t n", t=T)
                        own(dve.tensor_tensor(v, a2[:, :, 0:16], ssd_c[:, 9, 0:16].rearrange("p (a n) -> p a n", a=1).to_broadcast([P, T, 16]),
                                          ALU.add), "acc_read_dve")
                        dve.wait_ge(*due("acc_read_dve", c.read_count))
                        own(dve.scalar_tensor_tensor(ssd_c[:, 3, :], ssd_c[:, 0, :], -1.0, ssd_c[:, 0, :], ALU.mult, ALU.min), "dt_exp_in")
                    elif c.epilogue == "relu2":
                        n = c.info["dst"]
                        dve.wait_ge(*due("piece_used", c.pieces[-1].n + 1))
                        dve.wait_ge(*due("relu_ready", n + 1))
                        if n:
                            dve.wait_ge(*due("ff_hi", n))
                            dve.wait_ge(*due("ff_lo", n))
                        own(dve.scalar_tensor_tensor(tmp[:, 1024:2048].rearrange("p (b n) -> p b n", b=2), a2, 0.0,
                                                 tmp[:, 0:1024].rearrange("p (b n) -> p b n", b=2), ALU.max, ALU.mult), "acc_read_dve")
                        dve.wait_ge(*due("ff_hi", n + 1))
                        ks = slice(4 * (n % 4), 4 * (n % 4) + 4)
                        own(dve.tensor_tensor(cat2_lo[:, ks, :].rearrange("p k s -> p (k s)"), tmp[:, 1024:2048],
                                          cat2_hi[:, ks, :].rearrange("p k s -> p (k s)").bitcast(F32), ALU.subtract), "ff_lo")
                elif kind == "rank_sums":
                    dve.wait_ge(*due("squares_summed", 1))
                    own(dve.tensor_scalar(stats[:, 46:50], aux[:, 0, 0:4], 1.0 / 256, RMS_EPS, ALU.mult, ALU.add), "mean_square")
                    dve.wait_ge(*due("rank_rstd", 1))
                    own(dve.tensor_tensor(R3[:, 1024:1536].rearrange("p (n l) -> p n l", n=4),
                                          ident.rearrange("p (a l) -> p a l", a=1).to_broadcast([P, 4, P]),
                                          stats[:, 50:54].rearrange("p (n l) -> p n l", l=1).to_broadcast([P, 4, P]), ALU.mult), "diag_ready")
                elif kind == "rank_spread":
                    dve.wait_ge(*due("ranks_spread", 1))
                    dve.wait_ge(*due("cols_landed", 16 * 9))
                    dve.wait_ge(*due("acc_read_act", 5))
                    for k in range(4):
                        v = R3[:, 2048 + k * S:2048 + (k + 1) * S]
                        own(dve.scalar_tensor_tensor(v, v, cols[:, k:k + 1], aux[:, 3, (k // 2) * S:(k // 2 + 1) * S],
                                                     ALU.mult, ALU.mult), "ranks_scaled" if k == 3 else None)
                    dve.wait_ge(*due("ranks_hi", 1))
                    own(dve.tensor_tensor(cat_lo[:, 20:24, :].rearrange("p k s -> p (k s)"), R3[:, 2048:3072],
                                          cat_hi[:, 20:24, :].rearrange("p k s -> p (k s)").bitcast(F32), ALU.subtract), "ranks_lo")
                elif kind == "ret_scores":
                    h = i
                    dve.wait_ge(*due("ret_scored", h + 1))
                    dve.wait_ge(*due("decay_landed", 16))
                    if h >= 2:
                        dve.wait_ge(*due("ret_summed", h - 1))
                    own(dve.tensor_tensor(probs[:, h % 2, :], aux[:, 0, 0:3 * P], decay[:, h, :], ALU.mult), "ret_decayed")
                elif kind == "ret_values":
                    h = i
                    gate = R2[:, :].rearrange("p (t n) -> p t n", t=T)
                    dve.wait_ge(*due("ret_summed", h + 1))
                    mv = stats[:, 32:36].rearrange("p (t n) -> p t n", t=T)
                    for t in range(T):
                        row_stats(aux[:, 2 + t, :], 1, 8 + 6 * t, mv[:, t, :])
                    own.wait()
                    own(dve.tensor_scalar(stats[:, 36 + 2 * (h % 2):38 + 2 * (h % 2)], mv[:, :, 1], LN_EPS, 4.0, ALU.add, ALU.mult), "ret_var")
                    for t in range(T):
                        v = gate[:, t, h * RET_DV:(h + 1) * RET_DV]
                        ins = dve.scalar_tensor_tensor(v, aux[:, 2 + t, :], mv[:, t, 0:1], v, ALU.subtract, ALU.mult)
                        if t == 0:
                            own(ins)
                    own(ins, "ret_centred")
                    dve.wait_ge(*due("ret_centred", h + 1))
                elif kind == "ret_turn":
                    for half in range(2):
                        n = 2 * i + half
                        dve.wait_ge(*due("ret_hi", n + 1))
                        dve.wait_ge(*due("ret_turned", n + 1))
                        own(dve.tensor_tensor(cat_lo[:, 2 * n:2 * n + 2, :], aux[:, 1 - half, :].rearrange("p (f s) -> p f s", f=2),
                                          cat_hi[:, 2 * n:2 * n + 2, :].bitcast(F32), ALU.subtract), "ret_lo")
                elif kind == "scores":
                    a = i
                    pr = probs[:, a % PROBS, :]
                    dve.wait_ge(*due("scores_ready", a + 1))
                    if a >= PROBS:
                        dve.wait_ge(*due("probs_turned", a - PROBS + 1))
                    nm = soft[:, a % PROBS, 0, :]
                    scale = (NOPE + ROPE) ** -0.5 if a < 8 else DH ** -0.5
                    bank = aux[:, 3 * (a % 2), 0:3 * P]
                    if a < 24:
                        own(dve.scalar_tensor_tensor(pr, bank, scale, causal, ALU.mult, ALU.add), "scores_read")
                    else:
                        dve.wait_ge(*due("bias_landed", 16 * BAND_HEADS))
                        dve.wait_ge(*due("half_ready", 1))
                        own(dve.scalar_tensor_tensor(pr[:, 0:P], bank[:, 0:P], scale, backwards(a - 24, P), ALU.mult, ALU.add))
                        own.wait()
                        own(dve.scalar_tensor_tensor(pr[:, P:], bank[:, P:], scale, backwards(a - 24, S), ALU.mult, ALU.add), "scores_read")
                    dve.wait_ge(*due("scores_read", a + 1))
                    own(dve.tensor_reduce(nm[:, 0:1], pr[:, 0:P], AX, ALU.max, negate=True))
                    own(dve.tensor_reduce(nm[:, 1:2], pr[:, P:], AX, ALU.max, negate=True), "negmax_ready")
                elif kind == "normalise":
                    a = i
                    pr = probs[:, a % PROBS, :]
                    sm = soft[:, a % PROBS, 1, :]
                    dve.wait_ge(*due("exp_ready", a + 1))
                    own(dve.reciprocal(sm, sm))
                    own.wait()
                    own(dve.tensor_scalar(pr[:, 0:P], pr[:, 0:P], sm[:, 0:1], None, ALU.mult))
                    own(dve.tensor_scalar(pr[:, P:], pr[:, P:], sm[:, 1:2], None, ALU.mult), "probs_ready")
                elif kind == "gate":
                    u = i
                    dve.wait_ge(*due("values_ready", LAST_OF_UNIT[u] + 1))
                    if u >= 2:
                        dve.wait_ge(*due("cat_hi_ready", u - 1))
                        dve.wait_ge(*due("cat_lo_ready", u - 1))
                    o = aux[:, 2, (u % 2) * S:(u % 2 + 1) * S]
                    if u < 16:
                        g = R1[:, u * S:(u + 1) * S] if u < 8 else R1[:, 2048 + (u - 8) * S:2048 + (u - 7) * S]
                        if u == 0 or u == 8:
                            dve.wait_ge(*due("acc_read_dve", GATE_READS[u // 8]))
                        if u == 8 + 4:
                            dve.wait_ge(*due("acc_read_dve", GATE_READS[2]))
                        own(dve.scalar_tensor_tensor(gated[:, u % 2, :], o, 0.5, g, ALU.mult, ALU.mult), "out_read")
                    else:
                        own(dve.tensor_copy(gated[:, u % 2, :], o), "out_read")
                elif kind == "low":
                    u = i
                    b, tile = cat_place(u)
                    dve.wait_ge(*due("cat_hi_ready", u + 1))
                    dve.wait_ge(*due("out_read", u + 1))
                    own(dve.tensor_tensor(acts[b][1][:, tile, :], gated[:, u % 2, :], acts[b][0][:, tile, :].bitcast(F32),
                                      ALU.subtract), "cat_lo_ready")
                elif kind == "layer_norm" and i == 0:
                    dve.wait_ge(*due("acc_read_dve", Y_READS[0]))
                    full_norm(kind, i)
                    scaled_split(0, ln_g_col[:, 0:8], ln_b_col[:, 0:8], R1, x_hi, x_lo, "x_hi_ready", 4, "x_lo_ready")
                    low_prep(last_piece + 2)
                elif kind == "layer_norm":
                    dve.wait_ge(*due("acc_read_dve", Y_READS[1]))
                    full_norm(kind, i)
                    dve.wait_ge(*due("gb_landed", 64))
                    for op, at in ((ALU.mult, 0), (ALU.add, 1024)):
                        g = R2[:, at:at + 1024].rearrange("p (a n) -> p a n", a=1).to_broadcast([P, T, D])
                        own.wait()
                        if op == ALU.mult:
                            own(dve.tensor_tensor(tmp[:, :].rearrange("p (t n) -> p t n", t=T), tmp[:, :].rearrange("p (t n) -> p t n", t=T), g, op))
                        else:
                            own(dve.tensor_tensor(res[:, :, :], tmp[:, :].rearrange("p (t n) -> p t n", t=T), g, op))
                elif kind == "rms_norm":
                    dve.wait_ge(*due("acc_read_dve", Y_READS[1] if i == 0 else SSD_READS))
                    full_norm(kind, i)
                    scaled_split(TURNS[kind, i], mix_col if i == 0 else mlp_col, None, R1, x_hi, x_lo, "x_hi_ready",
                                 4 * (1 + NORM[kind, i]), "x_lo_ready")
                    low_prep(last_piece + 2)
                    if i == 0:
                        own(dve.memset(conv_in[:, :, 0:3], 0.0))
                        dve.wait_ge(*due("conv_landed", 16 * 5))
                        own(dve.tensor_scalar(conv_c[:, :, :], conv_c[:, :, :], 0.5, None, ALU.mult), "pad_ready")
                        dve.wait_ge(*due("bias_landed", 16 * BAND_HEADS))
                        own(dve.memset(bias[0:64, :, 0:64], NEG), "half_ready")
                    else:
                        own.wait()
                elif kind == "conv":
                    n = i
                    dve.wait_ge(*due("acc_read_act", CONV_READS[n]))
                    for f in range(4 * n, 4 * n + 4):
                        own(dve.tensor_scalar(conv_out[:, f, :], conv_in[:, f, 0:S], conv_c[:, 0, f:f + 1], conv_c[:, 4, f:f + 1],
                                              ALU.mult, ALU.add))
                    for tap in range(1, TAPS):
                        own.wait()
                        for f in range(4 * n, 4 * n + 4):
                            own(dve.scalar_tensor_tensor(conv_out[:, f, :], conv_in[:, f, tap:tap + S], conv_c[:, tap, f:f + 1],
                                                         conv_out[:, f, :], ALU.mult, ALU.add), "conv_read" if tap == TAPS - 1 and f == 4 * n + 3 else None)
                    dve.wait_ge(*due("conv_tanh", n + 1))
                    own(dve.scalar_tensor_tensor(conv_out[:, 4 * n:4 * n + 4, :], conv_in[:, 4 * n:4 * n + 4, 0:S], 1.0,
                                                 conv_out[:, 4 * n:4 * n + 4, :], ALU.add, ALU.mult), "silu_ready")
                elif kind == "softplus":
                    e, u, t, z = ssd_c[:, 3, :], ssd_c[:, 4, :], ssd_c[:, 1, :], ssd_c[:, 7, :]
                    dve.wait_ge(*due("dt_exp", 1))
                    own(dve.tensor_scalar(u, e, 1.0, None, ALU.add), "dt_ln_in")
                    own.wait()
                    own(dve.tensor_scalar(t, u, 1.0, None, ALU.subtract))
                    own.wait()
                    own(dve.tensor_scalar(z, t, 0.0, None, ALU.is_equal))
                    own.wait()
                    own(dve.tensor_tensor(t, t, z, ALU.add))
                    own.wait()
                    own(dve.reciprocal(t, t))
                    own.wait()
                    own(dve.tensor_tensor(t, t, e, ALU.mult))
                    own(dve.tensor_tensor(z, z, e, ALU.mult))
                    dve.wait_ge(*due("dt_ln", 1))
                    own.wait()
                    own(dve.tensor_tensor(t, t, ssd_c[:, 6, :], ALU.mult))
                    own.wait()
                    own(dve.tensor_tensor(t, t, z, ALU.add))
                    own.wait()
                    own(dve.scalar_tensor_tensor(t, ssd_c[:, 0, :], 0.0, t, ALU.max, ALU.add))
                    own.wait()
                    a_row = ssd_c[:, 5, 0:16].rearrange("p (a n) -> p a n", a=1).to_broadcast([P, T, 16])
                    own(dve.scalar_tensor_tensor(ssd_c[:, 2, :].rearrange("p (t n) -> p t n", t=T), t.rearrange("p (t n) -> p t n", t=T),
                                             -1.0, a_row, ALU.mult, ALU.mult), "a_ready")
                elif kind == "ssd_cums":
                    cum, edge, far = ssd_c[:, 6, :], ssd_c[:, 7, :], ssd_c[:, 8, :]
                    dve.wait_ge(*due("cums_ready", 1))
                    own.wait()
                    own(dve.tensor_copy(cum, aux[:, 0, 0:32]))
                    own.wait()
                    own(dve.tensor_copy(edge, cum))
                    own(dve.tensor_tensor(far, aux[:, 0, 32:64], cum, ALU.subtract), "edge_ready")
                elif kind == "ssd_cb":
                    dve.wait_ge(*due("cb_ready", 1))
                    own(dve.tensor_tensor(R1[:, 3072:3584].rearrange("p (n l) -> p n l", n=4), aux[:, 2, :].rearrange("p (n l) -> p n l", n=4),
                                          tri.rearrange("p (a l) -> p a l", a=1).to_broadcast([P, 4, P]), ALU.mult))
                    own(dve.tensor_copy(R1[:, 3584:3840], aux[:, 3, 0:256]), "cb_read")
                elif kind == "ssd_xs":
                    b = i
                    dve.wait_ge(*due("xs_turned", b + 1))
                    xs = aux[:, 2 * b:2 * b + 2, :].rearrange("p c (h n) -> p (c h) n", n=SSD_P)
                    dt = ssd_c[:, 1, 16 * b:16 * b + 16].rearrange("p (h n) -> p h n", n=1).to_broadcast([P, 16, SSD_P])
                    skip = ssd_c[:, 5, 16:32].rearrange("p (h n) -> p h n", n=1).to_broadcast([P, 16, SSD_P])
                    own(dve.tensor_tensor(x_dt[:, b], xs, dt, ALU.mult))
                    own(dve.tensor_tensor(y_ssd[:, b], xs, skip, ALU.mult), "xs_read")
                    if b:
                        dve.wait_ge(*due("edge_exp", 1))
                        own.wait()
                        own(dve.tensor_tensor(x_far, x_dt[:, 0], ssd_c[:, 8, 0:16].rearrange("p (h n) -> p h n", n=1).to_broadcast([P, 16, SSD_P]),
                                              ALU.mult), "far_ready")
                elif kind == "ssd_rows":
                    b, g = i // 2, i % 2
                    cum = ssd_c[:, 6, 16 * b + 8 * g:16 * b + 8 * g + 8]
                    if i >= 2:
                        dve.wait_ge(*due("y_near", i - 1))
                    for q in range(2):
                        dve.wait_ge(*due("cums_ready", 2 + 2 * i + q))
                        own(dve.tensor_tensor(seg[:, i % 2, 4 * q:4 * q + 4, :], aux[:, q, :].rearrange("p (h n) -> p h n", h=4),
                                              cum[:, 4 * q:4 * q + 4].rearrange("p (h n) -> p h n", n=1).to_broadcast([P, 4, P]),
                                              ALU.subtract), "seg_rows")
                    own.wait()
                    own(dve.tensor_scalar(seg[:, i % 2], seg[:, i % 2], 0.0, None, ALU.min), "seg_ready")
                    if i:
                        finish(i - 1)
                    else:
                        dve.wait_ge(*due("y_far_ready", 1))
                        own(dve.tensor_tensor(y_far, aux[:, 2:4, :].rearrange("p c (h n) -> p (c h) n", n=SSD_P),
                                              ssd_c[:, 7, 16:32].rearrange("p (h n) -> p h n", n=1).to_broadcast([P, 16, SSD_P]), ALU.mult),
                            "far_read")
                        own.wait()
                        own(dve.tensor_tensor(y_ssd[:, 1], y_ssd[:, 1], y_far, ALU.add))
                    masked(i)
                elif kind == "ssd_last":
                    finish(3)
                elif kind == "ssd_gate":
                    y2 = R2[:, 2048:4096]
                    own.wait()
                    ag = ssd_c[:, 3, 0:8].rearrange("p (n v) -> p n v", v=2)
                    for n in range(4):
                        own(dve.bn_aggr(ag[:, n, :], stats[:, 8 + 6 * n:14 + 6 * n]))
                    own.wait()
                    ms = ssd_c[:, 3, 8:12]
                    own(dve.tensor_tensor(ms, ag[:, :, 0], ag[:, :, 0], ALU.mult))
                    own.wait()
                    own(dve.scalar_tensor_tensor(ms, ms, 4.0 * LN_EPS, ag[:, :, 1], ALU.add, ALU.add), "y_sq")
                    dve.wait_ge(*due("y_rstd", 1))
                    for n in range(4):
                        v = y2[:, n * 512:(n + 1) * 512]
                        own(dve.tensor_scalar(v, v, ssd_c[:, 3, 12 + n:13 + n], None, ALU.mult), "y_gated" if n == 3 else None)
                elif kind == "ssd_turn":
                    scaled_split(TURNS["ssd", 0], ssdn_col, None, tmp, cat2_hi[:, 4:12, :], cat2_lo[:, 4:12, :], "normed_hi", 0, "normed_lo")
                elif kind == "final":
                    dve.wait_ge(*due("acc_read_dve", FINAL_READS))
                    dve.wait_ge(*due("gb_landed", 80))
                    mv = row_rstd("final", 0)
                    for t in range(T):
                        own(dve.scalar_tensor_tensor(tmp[:, t * D:(t + 1) * D], res[:, t, :], stats[:, 44 + t:45 + t], R2[:, 0:D], ALU.mult, ALU.mult),
                            "final_ready")

        @block.gpsimd
        def _(pool):
            own = Own(pool, "pool_own")

            def low_prep(n):
                if pool_share(pieces[n]):
                    lo_prep(pool, own, n, 3, 4, "lo_ready_pool")

            def inverse_root(o, i, signal):
                n = i.shape[1]
                own(pool.tensor_tensor(o, i, half_neg.to_broadcast([P, n]), ALU.pow), signal)

            own(pool.memset(half_neg, -0.5))
            pool.dma_start(R1[:, 0:256].bitcast(I32), w["positions"].to_broadcast([P, S])).then_inc(sems["pos_landed"], 16)
            pool.dma_start(tmp[:, 0:RET_HEADS * 3 * P], w["decay"]).then_inc(sems["decay_landed"], 16)
            for j, name in ((9, "dt_bias_2"), (5, "a_log_2")):
                pool.dma_start(ssd_c[:, j, 0:16], w[name].to_broadcast([P, 16])).then_inc(sems["dt_landed"], 16)
            pool.dma_start(ssd_c[:, 5, 16:32], w["d_skip_2"].to_broadcast([P, 16])).then_inc(sems["dt_landed"], 16)
            for tap in range(TAPS):
                pool.dma_start(conv_c[:, tap, :], w["conv_w_2"][tap:tap + 1, :].rearrange("a (k p) -> p (a k)", p=P), allow_slow_non_contiguous=True).then_inc(sems["conv_landed"], 16)
            pool.dma_start(conv_c[:, 4, :], w["conv_b_2"].rearrange("a (k p) -> p (a k)", p=P), allow_slow_non_contiguous=True).then_inc(sems["conv_landed"], 16)
            own.wait()
            low_prep(0)
            low_prep(1)

            def gains(l):
                pool.dma_start(R2[:, 0:1024], w["ln_g"][l:l + 1].to_broadcast([P, D])).then_inc(sems["gb_landed"], 16)
                pool.dma_start(R2[:, 1024:2048], w["ln_b"][l:l + 1].to_broadcast([P, D])).then_inc(sems["gb_landed"], 16)

            def cum_rows(i):
                if i:
                    pool.wait_ge(*due("cums_ready", 1 + 2 * i))
                else:
                    pool.wait_ge(*due("a_ready", 1))
                    pool.wait_ge(*due("normed_turned", 8))
                a = ssd_c[:, 2, 8 * i:8 * i + 8].rearrange("p (h n) -> p h n", n=1).to_broadcast([P, 8, P])
                own(pool.tensor_tensor(row_a, tri.rearrange("p (a n) -> p a n", a=1).to_broadcast([P, 8, P]), a, ALU.mult), "rows_ready")

            for s in steps:
                kind, i = s
                if kind == "piece":
                    if i.n + 2 < len(pieces):
                        low_prep(i.n + 2)
                elif kind == "epi" and i.epilogue == "rotate":
                    c = i
                    n = rot_n[c.n]
                    m = 1 if c.width == 2 * P else 2
                    pool.wait_ge(*due("acc_read_dve", c.read_count))
                    if n >= 4 and c.info["dst"] is None:
                        pool.wait_ge(*due("ret_turned", 8))
                    pr, o = rot_products(n), rot_dst(c, n)
                    own(pool.tensor_tensor(o[:, :, 0, :], pr[:, 0, 0:m, :], pr[:, 1, 0:m, :], ALU.subtract))
                    own.wait()
                    own(pool.tensor_tensor(o[:, :, 1, :], pr[:, 2, 0:m, :], pr[:, 3, 0:m, :], ALU.add), "rot_ready")
                elif kind == "ret_values":
                    h = i
                    pool.wait_ge(*due("ret_var", h + 1))
                    inverse_root(stats[:, 40 + 2 * (h % 2):42 + 2 * (h % 2)], stats[:, 36 + 2 * (h % 2):38 + 2 * (h % 2)], "ret_rstd")
                elif kind == "rank_sums":
                    pool.wait_ge(*due("mean_square", 1))
                    inverse_root(stats[:, 50:54], stats[:, 46:50], "rank_rstd")
                elif kind == "layer_norm" or kind == "rms_norm":
                    n = {("layer_norm", 0): 0, ("layer_norm", 1): 1, ("rms_norm", 0): 2, ("rms_norm", 1): 3}[kind, i]
                    pool.wait_ge(*due("var_ready", n + 1))
                    inverse_root(stats[:, 44:46], stats[:, 36:38], "rstd_ready")
                    if (kind, i) in NORM:
                        for b in (1, 3):
                            low_share(pool, own, b, R1, x_hi, x_lo, "x_hi_ready", 4 * (1 + NORM[kind, i]), "x_lo_pool")
                    if kind == "layer_norm" and i == 0:
                        pool.wait_ge(*due("normed_ready", 1))
                        pool.wait_ge(*due("gb_landed", 32))
                        v = tmp[:, :].rearrange("p (t n) -> p t n", t=T)
                        own(pool.tensor_tensor(res[:, :, :], v, R2[:, 0:1024].rearrange("p (a n) -> p a n", a=1).to_broadcast([P, T, D]), ALU.mult))
                        own.wait()
                        own(pool.tensor_tensor(res[:, :, :], res[:, :, :], R2[:, 1024:2048].rearrange("p (a n) -> p a n", a=1).to_broadcast([P, T, D]), ALU.add), "res_ready")
                    if kind == "rms_norm" and i == 1:
                        pool.wait_ge(*due("normed_turned", 16))
                        pool.dma_start(R2[:, 0:1024], w["norm_final_w_2"].to_broadcast([P, D])).then_inc(sems["gb_landed"], 16)
                elif kind == "low" and i == MLA_HEADS - 1:
                    pool.wait_ge(*due("scores_ready", MLA_HEADS))
                    gains(0)
                elif kind == "gate" and i == 10:
                    pool.wait_ge(*due("rot_ready", 10))
                    gains(1)
                elif kind == "low" and i == 8:
                    pool.wait_ge(*due("acc_read_dve", Y_READS[0]))
                    table = w["rel_bias_2"]
                    for h in range(BAND_HEADS):
                        src = bass.AP(table.tensor, h * (2 * REL_CLIP + 1) + REL_CLIP + 1 - P, [[1, P], [1, S]])
                        pool.dma_start(bias[:, h, :], src).then_inc(sems["bias_landed"], 16)
                elif kind == "ssd_cums":
                    cum_rows(0)
                elif kind == "ssd_rows" and i < 3:
                    cum_rows(i + 1)
                elif kind == "ssd_gate":
                    pool.wait_ge(*due("y_sq", 1))
                    inverse_root(ssd_c[:, 3, 12:16], ssd_c[:, 3, 8:12], "y_rstd")
                elif kind == "ssd_turn":
                    for b in (1, 3):
                        low_share(pool, own, b, tmp, cat2_hi[:, 4:12, :], cat2_lo[:, 4:12, :], "normed_hi", 0, "normed_lo_pool")
                elif kind == "final":
                    pool.wait_ge(*due("var_ready", 5))
                    inverse_root(stats[:, 44:46], stats[:, 36:38], "rstd_ready")


_NAMES = ("w_in_even", "w_uq_even", "w_ukv_even", "w_out_even", "w_in_odd", "w_out_odd", "w_in_2", "w_out_2", "w_ff1_2", "w_ff2_2")
_ROWS = ("q_norm_even", "kv_norm_even", "ln_g", "ln_b", "norm_mix_w_2", "norm_mlp_w_2", "ssd_norm_w_2", "norm_final_w_2",
         "conv_b_2", "dt_bias_2", "a_log_2", "d_skip_2", "positions")


def kernel(**inputs):
    import concourse.bacc as _bacc
    from concourse.bass_utils import run_bass_kernel_spmd as _run

    arrays = {}
    arrays["x"] = np.ascontiguousarray(inputs["x"]).reshape(S, D)
    for name in _NAMES:
        a = np.ascontiguousarray(inputs[name])
        arrays[name] = a.reshape(a.shape[-2:])
    for name in _ROWS:
        a = np.ascontiguousarray(inputs[name])
        arrays[name] = a.reshape(-1, a.shape[-1])
    arrays["conv_w_2"] = np.ascontiguousarray(inputs["conv_w_2"]).reshape(TAPS, CONV_DIM)
    arrays["rel_bias_2"] = np.ascontiguousarray(np.asarray(inputs["rel_bias_2"])[0].T)
    arrays["tables"], arrays["decay"] = shape_tables()
    nc = _bacc.Bacc("TRN2", target_bir_lowering=False, num_devices=1)
    feed, w = {}, {}
    for name, a in arrays.items():
        feed[f"in_{name}"] = a
        w[name] = nc.dram_tensor(f"in_{name}", a.shape, mybir.dt.from_np(a.dtype), kind="ExternalInput").ap()
    out = nc.dram_tensor("out", (S, D), F32, kind="ExternalOutput").ap()
    build(nc, w, out)
    r = _run(nc, [feed], core_ids=[0])
    return r.results[0]["out"].reshape(1, S, D)
```

```python
from contextlib import ExitStack

import numpy as np

import concourse.bass as bass
from concourse import mybir

F32 = mybir.dt.float32
F32R = mybir.dt.float32r
I32 = mybir.dt.int32
ALU = mybir.AluOpType
ACT = mybir.ActivationFunctionType
AX = mybir.AxisListType.X

P = 128
S = 256
D = 1024
T = S // P
KD = D // P
NCOL = 512
NEG = -1e30
LN_EPS = 1e-5
RMS_EPS = 1e-6
DN_ALPHA = 4.0 ** 0.25

RET_HEADS, RET_DK, RET_DV = 4, 256, 512
MLA_HEADS, NOPE, ROPE = 8, 128, 64
MOBA_HEADS, DH = 16, 64
BAND_HEADS = 8
SSD_HEADS, SSD_P, SSD_N, SSD_G = 16, 64, 128, 2
CONV_DIM = 1536
CONV_TILES = CONV_DIM // P
TAPS = 4
REL_CLIP = 256
D_FF = 4096
FF_CHUNKS = D_FF // NCOL

RQ, RK, RV, RG, MQ, MKR, MG = 0, 1024, 2048, 4096, 6144, 6656, 6720
SQ, SK, SV, SZ, SX, SDT = 0, 512, 1024, 1536, 2560, 4096

C_ID, C_TRI, C_ONES, C_MASK, C_FRET, C_FROPE, C_SIGN = 0, 128, 256, 384, 768, 769, 770
C_END = 771
RAW_SLOTS = 3
LAG = 3
PROBS = LAG + 2
TWO_PI = 2.0 * np.pi
PI_SAFE = 3.1415925


def shape_tables():
    i = np.arange(P)
    table = np.zeros((P, C_END), np.float32)
    table[:, C_ID:C_ID + P] = np.eye(P)
    table[:, C_TRI:C_TRI + P] = i[:, None] <= i[None, :]
    table[:, C_ONES:C_ONES + P] = 1.0
    causal = np.where(i[None, :] <= i[:, None], 0.0, NEG)
    table[:, C_MASK:C_MASK + P] = causal
    table[:, C_MASK + 2 * P:C_MASK + 3 * P] = causal
    line = np.linspace(0.0, 1.0, P, dtype=np.float32)
    table[:, C_FRET] = np.float32(1.0) / np.power(np.float32(10000.0), line)
    half = np.arange(0, ROPE, 2, dtype=np.float32) / np.float32(ROPE)
    table[:, C_FROPE] = np.tile(np.float32(1.0) / np.power(np.float32(10000.0), half), P // (ROPE // 2))
    table[:, C_SIGN] = np.where(i % ROPE < ROPE // 2, -1.0, 1.0)
    decay = np.zeros((P, RET_HEADS, 3, P), np.float32)
    for h in range(RET_HEADS):
        log_g = np.log(1.0 - 2.0 ** (-5.0 - h))
        rel = i[None, :] - i[:, None]
        diag = np.where(rel >= 0, np.exp(log_g * np.maximum(rel, 0)), 0.0)
        decay[:, h, 0] = diag
        decay[:, h, 1] = np.exp(log_g * (rel + P))
        decay[:, h, 2] = diag
    decay *= RET_DK ** -0.5
    return table, decay.reshape(P, -1)


class Piece:

    def __init__(self, chunk, src, nk, k0, cols, order=None, rows=0):
        self.chunk, self.src, self.nk, self.k0, self.cols = chunk, src, nk, k0, cols
        self.order = order
        self.raw = nk * (rows or cols)
        self.size = nk * cols


class Chunk:

    def __init__(self, number, layout, acts, width, epilogue, **info):
        self.n, self.layout, self.acts, self.width, self.epilogue = number, layout, acts, width, epilogue
        self.info = info
        self.pieces = []
        self.banks = None


def plan(w):
    chunks, pieces, steps = [], [], []

    def chunk(layout, acts, width, epilogue, **info):
        c = Chunk(len(chunks), layout, acts, width, epilogue, **info)
        chunks.append(c)
        return c

    def rows(ap, k0, nk, c0, cols):
        return ap[k0 * P:(k0 + nk) * P, c0:c0 + cols].rearrange("(k p) n -> p k n", p=P)

    def load(c, ap, k0, nk, c0, cols=NCOL, order=None, acts_k0=None, src=None, width=None):
        p = Piece(c, src if src is not None else rows(ap, k0, nk, c0, cols), nk,
                  k0 if acts_k0 is None else acts_k0, width or cols, order, cols)
        p.n = len(pieces)
        pieces.append(p)
        c.pieces.append(p)
        steps.append(("piece", p))

    def whole(c, ap, c0, order=None):
        for k0 in range(0, KD, 4):
            load(c, ap, k0, 4, c0, order=order)

    def step(*s):
        steps.append(s)

    step("turn_x", 0)
    for n, c0 in enumerate((RQ, RQ + NCOL, RK, RK + NCOL)):
        c = chunk("feat", "x", NCOL, "rotate", rot=n, table=0, dst=4 * n)
        load(c, w["w_in_even"], 0, 4, c0, order="pairs")
        if n < 2:
            step("trig", n)
        load(c, w["w_in_even"], 4, 4, c0, order="pairs")
        step("epi", c)
    for n in range(4):
        c = chunk("tok", "x", NCOL, "copy_tok", dst=("R1", 2048, n * NCOL))
        whole(c, w["w_in_even"], RV + n * NCOL)
        step("epi", c)
    for h in range(RET_HEADS):
        c = chunk("tok", "x", NCOL, "silu_tok", dst=("R2", 2048, h * NCOL))
        load(c, w["w_in_even"], 0, 4, RG + h * NCOL)
        step("ret_scores", h)
        load(c, w["w_in_even"], 4, 4, RG + h * NCOL)
        step("epi", c)
        if h:
            step("ret_turn", h - 1)
        step("ret_values", h)
    c = chunk("feat", "x", NCOL, "keep_ranks")
    load(c, w["w_in_even"], 0, 4, MQ)
    load(c, w["w_in_even"], 4, 4, MQ)
    step("epi", c)
    step("ret_turn", RET_HEADS - 1)
    ck = chunk("feat", "x", NCOL, "rotate", rot=None, table=1, dst=None)
    load(ck, w["w_in_even"], 0, 8, MKR, ROPE, order="twice", width=P)
    ck.width = P
    step("rank_sums", 0)
    step("epi", ck)
    for n in range(2):
        c = chunk("feat", "x", NCOL, "silu_feat", dst=("R1", n * 1024))
        load(c, w["w_in_even"], 0, 4, MG + n * NCOL)
        if n == 0:
            step("rank_spread", 0)
        load(c, w["w_in_even"], 4, 4, MG + n * NCOL)
        step("epi", c)
    uq = w["w_uq_even"].rearrange("(k p) (h n) -> p k h n", p=P, n=NOPE + ROPE)
    ukv = w["w_ukv_even"].rearrange("(k p) (h n) -> p k h n", p=P, n=2 * NOPE)
    for n in range(2):
        c = chunk("feat", "ranks", NCOL, "copy_feat", dst=("R3", n * 1024))
        load(c, None, 0, 2, 0, src=[uq[:, k, 4 * n:4 * n + 4, 0:NOPE] for k in range(2)], acts_k0=0)
        step("epi", c)
    c = chunk("feat", "ranks", NCOL, "rotate", rot=None, table=1, dst=None)
    load(c, None, 0, 2, 0, src=[uq[:, k, :, NOPE:NOPE + ROPE] for k in range(2)], acts_k0=0)
    step("epi", c)
    for n in range(2):
        c = chunk("feat", "ranks", NCOL, "copy_feat", dst=("R3", 2048 + n * 1024))
        load(c, None, 0, 2, 0, src=[ukv[:, k, 4 * n:4 * n + 4, 0:NOPE] for k in range(2)], acts_k0=2)
        step("epi", c)

    def mla_values(n):
        c = chunk("tok", "ranks", NCOL, "copy_tok", dst=("R1", 1024, 2048 + n * NCOL))
        load(c, None, 0, 2, 0, src=[ukv[:, k, 4 * n:4 * n + 4, NOPE:] for k in range(2)], acts_k0=2)
        step("epi", c)

    def pipeline(first, count, per_unit, between):
        assert max(between) <= count + LAG + 1
        after = []
        for n in range(count + LAG + 2):
            if n < count:
                step("scores", first + n)
            steps.extend(after)
            after = []
            if 0 <= n - LAG < count:
                step("turn", first + n - LAG)
            m = n - LAG - 1
            if 0 <= m < count:
                step("values", first + m)
                if m % per_unit == per_unit - 1:
                    step("gate", UNIT[first + m])
            m = n - LAG - 2
            if m >= 0 and m % per_unit == per_unit - 1:
                step("low", UNIT[first + m])
            if n < count:
                step("normalise", first + n)
            for f in between.get(n, ()):
                f()
                if n < count and steps[-1][0] == "epi":
                    after.append(steps.pop())

    ys = [chunk("tok", "cat", NCOL, "residual", n=n) for n in range(2)]
    order = [(k0, n) for k0 in range(0, 24, 4) for n in range(2)]
    out_piece = [lambda k0=k0, n=n: load(ys[n], w["w_out_even"], k0, 4, n * NCOL) for k0, n in order]
    between = {n: [lambda n=n: mla_values(n)] for n in range(2)}
    between.update({n: [out_piece[i]] for i, n in enumerate((2, 3, 4, 5, 6, 7, 8, 9, 10, 12))})
    pipeline(0, MLA_HEADS, 1, between)
    out_piece[10]()
    step("epi", ys[0])
    out_piece[11]()
    step("epi", ys[1])
    step("layer_norm", 0)
    def halves_of(make, ap, c0, order=None):
        made = []

        def half(k0):
            if k0 == 0:
                made.append(make())
            load(made[0], ap, k0, 4, c0, order=order)
            if k0:
                step("epi", made[0])
        return [lambda: half(0), lambda: half(4)]

    def moba_part(part, n):
        c0 = 1024 * part + n * NCOL
        if part < 2:
            return halves_of(lambda: chunk("feat", "x", NCOL, "rotate", rot=part, table=1, dst=8 * part + 4 * n),
                             w["w_in_odd"], c0)
        if part == 2:
            return halves_of(lambda: chunk("tok", "x", NCOL, "copy_tok", dst=("R1", 1024, n * NCOL)), w["w_in_odd"], c0)
        return halves_of(lambda: chunk("feat", "x", NCOL, "silu_feat", dst=("R1", 2048 + n * 1024)), w["w_in_odd"], c0)

    for part in range(3):
        for f in moba_part(part, 0):
            f()

    ys2 = []

    def moba_out(k0, n, nk):
        if len(ys2) <= n:
            ys2.append(chunk("tok", "cat2", NCOL, "residual", n=n))
        load(ys2[n], w["w_out_odd"], k0, nk, n * NCOL)

    rest = moba_part(3, 0) + moba_part(0, 1) + moba_part(1, 1) + moba_part(2, 1) + moba_part(3, 1)
    between = {n: [f] for n, f in zip((0, 1, 2, 3, 4, 5, 7, 9, 10, 12), rest)}
    for n, k0, m, nk in ((13, 0, 0, 4), (15, 0, 1, 4), (18, 4, 0, 2), (18, 4, 1, 2)):
        between.setdefault(n, []).append(lambda k0=k0, m=m, nk=nk: moba_out(k0, m, nk))
    pipeline(8, MOBA_HEADS, 2, between)
    moba_out(6, 0, 2)
    step("epi", ys2[0])
    moba_out(6, 1, 2)
    step("epi", ys2[1])
    step("layer_norm", 1)
    step("rms_norm", 0)
    for n in range(3):
        c = chunk("feat", "x", NCOL, "conv_in", dst=4 * n)
        load(c, w["w_in_2"], 0, 4, SX + n * NCOL)
        if n:
            step("conv", 2 * (n - 1))
        else:
            c_dt = chunk("tok", "x", SSD_HEADS, "copy_dt")
            load(c_dt, w["w_in_2"], 0, 8, SDT, SSD_HEADS)
            step("epi", c_dt)
            step("softplus", 0)
        load(c, w["w_in_2"], 4, 4, SX + n * NCOL)
        step("epi", c)
        if n:
            step("conv", 2 * (n - 1) + 1)
        if n == 2:
            step("conv_end", 0)
    between = [[("conv", 4)], [("conv_end", 1), ("conv", 5), ("ssd_cums", 0)], [("conv_end", 2)], [("ssd_cb", 0), ("ssd_xs", 0), ("ssd_xs", 1)], [("ssd_rows", 0)], [("ssd_rows", 1)],
               [("ssd_rows", 2)], [("ssd_rows", 3)], [("ssd_last", 0), ("ssd_gate", 0)], [("ssd_turn", 0)]]
    parts = []
    for n in range(2):
        parts += halves_of(lambda n=n: chunk("tok", "x", NCOL, "silu_tok", dst=("zb", 1024, n * NCOL)), w["w_in_2"], SZ + n * NCOL)
    for n in range(2):
        parts += halves_of(lambda n=n: chunk("feat", "x", NCOL, "copy_feat", dst=("R3", n * 1024)), w["w_in_2"], SQ + n * NCOL)
    parts += halves_of(lambda: chunk("tok", "x", NCOL, "copy_tok", dst=("R3", NCOL, 2048)), w["w_in_2"], SV)
    for f, sts in zip(parts, between):
        f()
        for st in sts:
            step(*st)
    ys3 = []

    def second_out(k0, n, nk=4):
        if len(ys3) <= n:
            ys3.append(chunk("tok", "cat2", NCOL, "add", n=n))
        load(ys3[n], w["w_out_2"], k0, nk, n * NCOL)

    between = {}
    for n, k0, m, nk in ((1, 4, 0, 4), (3, 4, 1, 4), (5, 8, 0, 4), (7, 8, 1, 4), (12, 0, 0, 2), (12, 0, 1, 2)):
        between.setdefault(n, []).append(lambda k0=k0, m=m, nk=nk: second_out(k0, m, nk))
    pipeline(24, BAND_HEADS, 2, between)
    second_out(2, 0, 2)
    step("epi", ys3[0])
    second_out(2, 1, 2)
    step("epi", ys3[1])
    step("rms_norm", 1)
    down = [chunk("tok", "ff", NCOL, "add", n=n) for n in range(2)]
    for c in range(FF_CHUNKS + 1):
        if c < FF_CHUNKS:
            u = chunk("feat", "x", NCOL, "relu2", dst=c)
            whole(u, w["w_ff1_2"], c * NCOL)
            step("epi", u)
        if c:
            for n in range(2):
                load(down[n], w["w_ff2_2"], 4 * (c - 1), 4, n * NCOL)
                if c == FF_CHUNKS:
                    step("epi", down[n])
    step("final", 0)
    return chunks, pieces, steps


UNIT = {a: a if a < 8 else (8 + (a - 8) // 2 if a < 24 else 16 + (a - 24) // 2) for a in range(32)}
LAST_OF_UNIT = {u: max(a for a in UNIT if UNIT[a] == u) for u in range(20)}


def cat_place(u):
    return ("cat", 16 + u) if u < 8 else ("cat2", u - 8 if u < 16 else u - 16)


def build(nc, w, out):
    chunks, pieces, steps = plan(w)
    order = {}
    for s in steps:
        if s[0] == "piece" and s[1].chunk.n not in order:
            order[s[1].chunk.n] = len(order)
    down = [c for c in chunks if c.acts == "ff"]
    turn = 0
    for c in sorted(chunks, key=lambda c: order[c.n]):
        if c in down:
            c.pair, c.turn = 2 + down.index(c), None
        else:
            c.pair, c.turn = turn % 2, turn
            turn += 1
    by_turn = {c.turn: c for c in chunks if c.turn is not None}
    READER = {"keep_ranks": "act", "copy_tok": "act", "copy_feat": "act", "conv_in": "act", "copy_dt": "dve"}
    reads = {"act": 0, "dve": 0}
    for s in steps:
        if s[0] == "epi":
            c = s[1]
            c.reader = READER.get(c.epilogue, "dve")
            reads[c.reader] += 1
            c.read_count = reads[c.reader]

    with ExitStack() as ctx:
        def sb(name, shape, dt=F32):
            return ctx.enter_context(nc.sbuf_tensor(name, shape, dt))

        def sem(name):
            return ctx.enter_context(nc.semaphore(name))

        cst = sb("cst", [P, C_END])
        raw = sb("raw", [P, RAW_SLOTS, 2048])
        w_hi = sb("w_hi", [P, 2, 2048], F32R)
        w_lo = sb("w_lo", [P, 2, 2048], F32R)
        res = sb("res", [P, T, D])
        x_hi = sb("x_hi", [P, KD, S], F32R)
        x_lo = sb("x_lo", [P, KD, S], F32R)
        R1 = sb("R1", [P, 4096])
        R2 = sb("R2", [P, 4096])
        R3 = sb("R3", [P, 4096])
        tmp = sb("tmp", [P, 2048])
        trig = sb("trig", [P, 2, 2, S])
        probs = sb("probs", [P, PROBS, 3 * P])
        turned = sb("turned", [P, 2, 3 * P])
        gated = sb("gated", [P, 2, S])
        cols = sb("cols", [P, 64])
        ssd_c = sb("ssd_c", [P, 10, 2 * SSD_HEADS])
        conv_c = sb("conv_c", [P, 5, CONV_TILES])
        stats = sb("stats", [P, 64])
        soft = sb("soft", [P, PROBS, 2, 2])
        with nc.sbuf_tensor("cat_hi", [P, 24, S], F32R) as cat_hi, nc.sbuf_tensor("cat_lo", [P, 24, S], F32R) as cat_lo:
            pass
        cat2_hi = sb("cat2_hi", [P, 16, S], F32R)
        cat2_lo = sb("cat2_lo", [P, 16, S], F32R)
        zb = sb("zb", [P, 4096])
        acc = ctx.enter_context(nc.psum_tensor("acc", [P, 4, 2, 512], F32))
        aux = acc[:, 2:4].rearrange("p a b n -> p (a b) n")

        ident = cst[:, C_ID:C_ID + P]
        tri = cst[:, C_TRI:C_TRI + P]
        ones = cst[:, C_ONES:C_ONES + P]
        causal = cst[:, C_MASK:C_MASK + 3 * P]
        decay = tmp[:, 0:RET_HEADS * 3 * P].rearrange("p (h n) -> p h n", h=RET_HEADS)
        region = {"R1": R1, "R2": R2, "R3": R3, "zb": zb}
        qn_col, kvn_col = cols[:, 0:2], cols[:, 2:4]
        ln_g_col, ln_b_col = cols[:, 4:20], cols[:, 20:36]
        mix_col, mlp_col = cols[:, 36:44], cols[:, 44:52]
        ssdn_col = cols[:, 52:60]
        half_neg = cols[:, 60:61]
        acts = {"x": (x_hi, x_lo), "ranks": (cat_hi[:, 20:24], cat_lo[:, 20:24]), "cat": (cat_hi, cat_lo),
                "cat2": (cat2_hi, cat2_lo), "ff": (cat2_hi, cat2_lo)}
        q_pe = R2[:, 0:1024].rearrange("p (g s) -> p g s", g=4)
        k_pe = R2[:, 1024:1280].rearrange("p (g s) -> p g s", g=1)
        bias = zb[:, 2048:4096].rearrange("p (h n) -> p h n", h=BAND_HEADS)
        conv_in = R2[:, 0:CONV_TILES * (S + 3)].rearrange("p (c s) -> p c s", c=CONV_TILES)
        conv_out = R1[:, 0:CONV_TILES * S].rearrange("p (c s) -> p c s", c=CONV_TILES)
        b_T, c_T = conv_out[:, 8:10], conv_out[:, 10:12]
        x_dt = R2[:, 0:2048].rearrange("p (b h n) -> p b h n", b=2, h=SSD_HEADS)
        y_ssd = R2[:, 2048:4096].rearrange("p (b h n) -> p b h n", b=2, h=SSD_HEADS)
        x_far = R3[:, 3072:4096].rearrange("p (h n) -> p h n", h=SSD_HEADS)
        y_far = tmp[:, 1024:2048].rearrange("p (h n) -> p h n", h=SSD_HEADS)
        cb = R1[:, 3072:3840].rearrange("p (b g n) -> p b g n", b=3, g=2)
        seg = R1[:, 0:2048].rearrange("p (i h n) -> p i h n", i=2, h=8)
        row_a = tmp[:, 0:1024].rearrange("p (h n) -> p h n", h=8)

        raw_landed = [sem(f"raw_landed{i}") for i in range(RAW_SLOTS)]
        names = ("tables_landed", "decay_landed", "x_landed", "x_landed2", "pos_landed", "cols_landed", "dt_landed", "conv_landed", "gb_landed", "bias_landed",
                 "out_landed", "hi_half", "hi_ready", "lo_ready", "lo_ready_pool", "piece_used", "acc_read_act",
                 "acc_read_dve", "angles_ready", "trig_ready", "x_turned", "x_hi_ready", "x_lo_ready", "x_lo_odd", "x_lo_pool", "normed_lo_pool", "rot_swapped",
                 "rot_ready", "tanh_ready", "ret_scored", "ret_decayed", "ret_summed", "ret_centred", "ret_var",
                 "ret_rstd", "ret_scaled", "ret_turned", "ret_hi", "ret_lo", "squares_ready", "squares_summed",
                 "mean_square", "rank_rstd", "diag_ready", "ranks_spread", "ranks_scaled", "ranks_hi", "ranks_lo", "scores_ready", "scores_read",
                 "negmax_ready", "exp_ready", "probs_ready", "probs_turned", "turned_copied", "values_ready",
                 "out_read", "cat_hi_ready", "cat_lo_ready", "var_ready", "rstd_ready", "normed_ready", "normed_act", "centred", "row_added", "fresh_squared", "normed_turned",
                 "scaled_ready", "normed_hi", "normed_lo", "res_ready", "pool_own", "dve_own", "act_own", "pe_own",
                 "conv_read", "conv_tanh", "dt_exp_in", "dt_exp", "dt_ln_in", "dt_ln", "a_ready", "rows_ready", "cums_ready",
                 "seg_rows", "seg_ready", "seg_exp", "m_ready", "silu_ready", "far_ready", "far_read", "cb_ready", "cb_read", "xs_turned", "xs_read", "y_near",
                 "y_far_ready", "y_read", "edge_ready", "edge_exp", "y_gated", "y_sq", "y_rstd", "relu_ready", "ff_hi", "ff_lo",
                 "half_ready", "cols_set", "pad_ready", "final_ready")
        sems = {n: sem(n) for n in names}

        def due(name, value):
            return sems[name], value

        block = ctx.enter_context(nc.Block())

        class Own:

            def __init__(self, eng, name):
                self.eng, self.name, self.counts, self.last = eng, name, {}, None

            def __call__(self, ins, name=None):
                name = name or self.name
                self.counts[name] = self.counts.get(name, 0) + 1
                self.last = (name, self.counts[name])
                ins.then_inc(sems[name], 1)

            def wait(self):
                self.eng.wait_ge(sems[self.last[0]], self.last[1])

        def backwards(h, n):
            return bass.AP(zb, 2048 + h * S + n - 1, [[4096, P], [-1, n]])

        def split_views(p, k0, k1):
            slot = p.n % 2
            r = raw[:, p.n % RAW_SLOTS, k0 * p.raw // p.nk:k1 * p.raw // p.nk]
            parts = [b[:, slot, k0 * p.cols:k1 * p.cols] for b in (w_hi, w_lo)]
            if p.order == "pairs":
                return [(r.rearrange("p (k f t) -> p k t f", t=2, f=P),
                         *[v.rearrange("p (k t f) -> p k t f", t=2, f=P) for v in parts])]
            if p.order == "twice":
                r = r.rearrange("p (k s) -> p k s", k=p.nk)
                parts = [v.rearrange("p (k c s) -> p k c s", k=p.nk, c=2) for v in parts]
                return [(r, parts[0][:, :, c, :], parts[1][:, :, c, :]) for c in range(2)]
            return [(r, *parts)]

        def pool_share(p):
            return 0 if p.nk != 4 else 2 if p.chunk.epilogue == "conv_in" or p.chunk.epilogue == "silu_tok" and p.chunk.info["dst"][0] == "zb" else 1

        n_pool = {}
        count = 0
        for p in pieces:
            count += pool_share(p) > 0
            n_pool[p.n] = count
        n_spread = [p.n for p in pieces if p.order == "spread"]

        def hi_prep(eng, own, n):
            p = pieces[n]
            eng.wait_ge(raw_landed[n % RAW_SLOTS], 16 * p.loads)
            if n >= 2:
                eng.wait_ge(*due("piece_used", n - 1))
            if p.nk == 4:
                for r, hi, _ in split_views(p, 0, 2):
                    ins = eng.activation(hi, r, ACT.Copy)
                own(ins, "hi_half")
            for r, hi, _ in split_views(p, 2 if p.nk == 4 else 0, p.nk):
                ins = eng.activation(hi, r, ACT.Copy)
            own(ins, "hi_ready")

        def lo_prep(eng, own, n, k0, k1, signal):
            p = pieces[n]
            if p.nk == 4 and k1 <= 2:
                eng.wait_ge(*due("hi_half", n_pool[n]))
            else:
                eng.wait_ge(*due("hi_ready", n + 1))
            eng.wait_ge(raw_landed[n % RAW_SLOTS], 16 * p.loads)
            if n >= 2:
                eng.wait_ge(*due("piece_used", n - 1))
            for r, hi, lo in split_views(p, k0, k1):
                ins = eng.tensor_tensor(lo, r, hi.bitcast(F32), ALU.subtract)
            own(ins, signal)

        loads = [0] * RAW_SLOTS
        for p in pieces:
            srcs = p.src if isinstance(p.src, list) else [p.src]
            loads[p.n % RAW_SLOTS] += len(srcs)
            p.loads = loads[p.n % RAW_SLOTS]
            p.srcs = srcs

        MLA_COPIES = 4 + 1 + 2 + 2 + 2
        late = set()
        for s0, s1, s2 in zip(steps, steps[1:], steps[2:]):
            if s0[0] == "piece" and s1[0] == "epi" and s2[0] in ("layer_norm", "rms_norm"):
                late |= {s0[1].n - 1, s0[1].n}
        waiting = {s0[1].n for s0, s1 in zip(steps, steps[1:]) if s0[0] == "piece" and s1[0] == "scores"}
        NORM = {("layer_norm", 0): 0, ("rms_norm", 0): 1, ("rms_norm", 1): 2}
        TURNS = {("layer_norm", 0): 0, ("rms_norm", 0): 4, ("ssd", 0): 8, ("rms_norm", 1): 12}
        Z_READS = max(c.read_count for c in chunks if c.epilogue == "silu_tok")
        tanh_n = {}
        for s in steps:
            if s[0] == "epi" and s[1].epilogue.startswith("silu"):
                tanh_n[s[1].n] = len(tanh_n) + 1
        rot_n = {}
        for s in steps:
            if s[0] == "epi" and s[1].epilogue == "rotate":
                rot_n[s[1].n] = len(rot_n)

        Y_READS = [max(c.read_count for c in chunks if c.epilogue == "residual" and c.acts == a) for a in ("cat", "cat2")]
        ff2_used = {c: max(p.n for p in pieces if p.chunk.acts == "ff" and p.k0 == 4 * c) + 1 for c in range(FF_CHUNKS)}

        def rot_products(n):
            base = 2048 * (n % 2)
            r = tmp[:, :] if 4 <= n < 6 else R2[:, base:base + 2048]
            if n < 4:
                return r.rearrange("p (q m s) -> p q m s", q=4, m=2)
            return r.rearrange("p (q g s) -> p q g s", q=2, g=4)

        def rot_dst(c, n):
            if c.info["dst"] is not None:
                i = c.info["dst"]
                r = R3[:, i * S:(i + 4) * S]
                return r.rearrange("p (m t s) -> p m t s", m=2, t=2) if n < 4 else r.rearrange("p (g s) -> p g s", g=4)
            return k_pe if c.width == P else q_pe

        by = lambda e, f=None: [c.read_count for c in chunks if c.epilogue == e and (f is None or f(c))]
        GATE_READS = by("silu_feat", lambda c: True)
        GATE_READS = [GATE_READS[1], GATE_READS[2], GATE_READS[3]]
        SSD_READS = max(by("add", lambda c: c.acts == "cat2"))
        FINAL_READS = max(by("add", lambda c: c.acts == "ff"))
        CONV_READS = by("conv_in")

        def epi_dst(c):
            i = c.info["dst"]
            if c.layout == "tok":
                r, width, c0 = i
                if r == "R1" and width == 2048:
                    return R1[:, :].rearrange("p (t n) -> p t n", t=T)[:, :, c0:c0 + NCOL]
                if width == 2048:
                    return region[r][:, :].rearrange("p (t n) -> p t n", t=T)[:, :, c0:c0 + NCOL]
                base = (c0 // 2048) * 2048 if width == 1024 else 2048
                v = region[r][:, base:base + T * width].rearrange("p (t n) -> p t n", t=T)
                return v[:, :, c0 - base:c0 - base + NCOL]
            r, c0 = i
            return region[r][:, c0:c0 + 1024].rearrange("p (b n) -> p b n", b=2)

        @block.sync
        def _(sp):
            sp.dma_start(cst[:, :], w["tables"]).then_inc(sems["tables_landed"], 16)
            for half in range(2):
                c = slice(half * 512, (half + 1) * 512)
                sp.dma_start(res[:, :, c], w["x"].rearrange("(t p) n -> p t n", p=P)[:, :, c]).then_inc(sems[("x_landed", "x_landed2")[half]], 16)
            for p in pieces:
                n = p.n
                if n >= RAW_SLOTS:
                    sp.wait_ge(*due("hi_ready", n - RAW_SLOTS + 1))
                    sp.wait_ge(*due("lo_ready", n - RAW_SLOTS + 1))
                    if n_pool[n - RAW_SLOTS]:
                        sp.wait_ge(*due("lo_ready_pool", n_pool[n - RAW_SLOTS]))
                per = p.raw // len(p.srcs)
                for i, src in enumerate(p.srcs):
                    dst = raw[:, n % RAW_SLOTS, i * per:(i + 1) * per]
                    if len(src.shape) == 3:
                        dst = dst.rearrange("p (a b) -> p a b", a=src.shape[1])
                    sp.dma_start(dst, src).then_inc(raw_landed[n % RAW_SLOTS], 16)
            for t in range(T):
                sp.wait_ge(*due("final_ready", t + 1))
                sp.dma_start(out[t * P:(t + 1) * P, :], tmp[:, t * D:(t + 1) * D]).then_inc(sems["out_landed"], 16)
            sp.wait_ge(*due("out_landed", 32))

        @block.tensor
        def _(pe):
            own = Own(pe, "pe_own")

            def ready_acts(c):
                if c.acts == "ranks":
                    pe.wait_ge(*due("ranks_hi", 1))
                    pe.wait_ge(*due("ranks_lo", 1))

            state = {"x": 0}

            def x_ready(tiles):
                n = state["x"]
                if n == 0:
                    pe.wait_ge(*due("x_hi_ready", tiles // 2))
                    pe.wait_ge(*due("x_lo_ready", tiles // 4))
                    pe.wait_ge(*due("x_lo_odd", tiles // 4))
                    return
                pe.wait_ge(*due("x_hi_ready", 4 * n + tiles // 2))
                pe.wait_ge(*due("x_lo_ready", 2 * n + tiles // 4))
                pe.wait_ge(*due("x_lo_pool", 2 * (n - 1) + tiles // 4))

            def product(p):
                c = p.chunk
                slot = p.n % 2
                hi, lo = acts[c.acts]
                if p is c.pieces[0]:
                    ready_acts(c)
                    if c.turn is not None and c.turn >= 2:
                        before = by_turn[c.turn - 2]
                        pe.wait_ge(*due("acc_read_" + before.reader, before.read_count))
                k_last = p.k0 + p.nk
                if c.acts == "x":
                    x_ready(k_last)
                if c.acts == "cat":
                    if p.k0 < 16:
                        pe.wait_ge(*due("ret_hi", 8))
                        pe.wait_ge(*due("ret_lo", 8))
                    else:
                        pe.wait_ge(*due("cat_hi_ready", k_last - 16))
                        pe.wait_ge(*due("cat_lo_ready", k_last - 16))
                if c.acts == "cat2":
                    if c.epilogue == "residual":
                        pe.wait_ge(*due("cat_hi_ready", 8 + k_last))
                        pe.wait_ge(*due("cat_lo_ready", 8 + k_last))
                    elif p.k0 < 4:
                        pe.wait_ge(*due("cat_hi_ready", 16 + k_last))
                        pe.wait_ge(*due("cat_lo_ready", 16 + k_last))
                    else:
                        pe.wait_ge(*due("normed_hi", 4))
                        pe.wait_ge(*due("normed_lo", 2))
                        pe.wait_ge(*due("normed_lo_pool", 2))
                k_acts = p.k0
                if c.acts == "ff":
                    pe.wait_ge(*due("ff_hi", p.k0 // 4 + 1))
                    pe.wait_ge(*due("ff_lo", p.k0 // 4 + 1))
                    k_acts = p.k0 % 16
                pe.wait_ge(*due("hi_ready", p.n + 1))
                pe.wait_ge(*due("lo_ready", p.n + 1))
                if n_pool[p.n]:
                    pe.wait_ge(*due("lo_ready_pool", n_pool[p.n]))
                wh = w_hi[:, slot, 0:p.size].rearrange("p (k n) -> p k n", k=p.nk)
                wl = w_lo[:, slot, 0:p.size].rearrange("p (k n) -> p k n", k=p.nk)
                first, last = p is c.pieces[0], p is c.pieces[-1]
                for k in range(p.nk):
                    start, stop = first and k == 0, last and k == p.nk - 1
                    ka = k_acts + k
                    if c.layout == "tok":
                        for t in range(T):
                            o = acc[:, c.pair, t, 0:p.cols]
                            xh, xl = hi[:, ka, t * P:(t + 1) * P], lo[:, ka, t * P:(t + 1) * P]
                            pe.matmul(o, xh, wh[:, k, :], start=start, stop=False)
                            pe.matmul(o, xh, wl[:, k, :], start=False, stop=False)
                            ins = pe.matmul(o, xl, wh[:, k, :], start=False, stop=stop)
                    else:
                        for f in range(p.cols // P):
                            o = acc[:, c.pair, f // 2, (f % 2) * S:(f % 2 + 1) * S]
                            fs = slice(f * P, (f + 1) * P)
                            pe.matmul(o, wh[:, k, fs], hi[:, ka, :], start=start and f % 2 == 0, stop=False, skip_group_check=True)
                            pe.matmul(o, wh[:, k, fs], lo[:, ka, :], start=False, stop=False, skip_group_check=True)
                            ins = pe.matmul(o, wl[:, k, fs], hi[:, ka, :], start=False, stop=stop, skip_group_check=True)
                own(ins, "piece_used")

            def turn_tokens(src, per_bank_signal, tiles=range(KD)):
                for f in tiles:
                    for t in range(T):
                        ins = pe.transpose(aux[:, f // 2, (f % 2) * S + t * P:(f % 2) * S + (t + 1) * P],
                                           src[:, t, f * P:(f + 1) * P], ident)
                    if f % 2:
                        ins.then_inc(sems[per_bank_signal], 1)

            def near(i):
                b, g = i // 2, i % 2
                pe.wait_ge(*due("m_ready", i + 1))
                if i >= 2:
                    pe.wait_ge(*due("y_read", i - 1))
                if i == 0:
                    pe.wait_ge(*due("far_read", 1))
                for h in range(8):
                    ins = pe.matmul(aux[:, 2 + g, h * SSD_P:(h + 1) * SSD_P], seg[:, i % 2, h, :],
                                    x_dt[:, b, 8 * g + h, :], start=True, stop=True)
                own(ins, "y_near")

            normed = tmp[:, :].rearrange("p (t n) -> p t n", t=T)
            v_ret = R1[:, :].rearrange("p (t n) -> p t n", t=T)
            norms = [0]
            for s in steps:
                kind, i = s
                if kind == "piece":
                    product(i)
                elif kind == "turn_x":
                    pe.wait_ge(*due("tables_landed", 16))
                    for half in range(2):
                        pe.wait_ge(*due(("x_landed", "x_landed2")[half], 16))
                        turn_tokens(res, "x_turned", range(4 * half, 4 * half + 4))
                elif kind == "ret_scores":
                    h = i
                    if h == 0:
                        pe.wait_ge(*due("rot_ready", 4))
                        x_ready(8)
                    else:
                        pe.wait_ge(*due("ret_decayed", h))
                    if h >= 2:
                        pe.wait_ge(*due("ret_lo", 2 * h - 2))
                    q = R3[:, 0:2048].rearrange("p (f s) -> p f s", f=8)
                    k = R3[:, 2048:4096].rearrange("p (f s) -> p f s", f=8)
                    for j, (o0, i0, n) in enumerate(((0, 0, S), (S, P, P))):
                        for t in range(2):
                            ins = pe.matmul(aux[:, 0, o0:o0 + n], k[:, 2 * h + t, j * P:(j + 1) * P],
                                            q[:, 2 * h + t, i0:i0 + n], start=(t == 0), stop=(t == 1))
                    own(ins, "ret_scored")
                elif kind == "ret_values":
                    h = i
                    pe.wait_ge(*due("ret_decayed", h + 1))
                    pe.wait_ge(*due("acc_read_act", 4))
                    if h:
                        pe.wait_ge(*due("ret_centred", h))
                    pr = probs[:, h % 2, :]
                    vs = slice(h * RET_DV, (h + 1) * RET_DV)
                    pe.matmul(aux[:, 2, :], pr[:, 0:P], v_ret[:, 0, vs], start=True, stop=True)
                    pe.matmul(aux[:, 3, :], pr[:, P:2 * P], v_ret[:, 0, vs], start=True, stop=False)
                    pe.matmul(aux[:, 3, :], pr[:, 2 * P:3 * P], v_ret[:, 1, vs], start=False, stop=True).then_inc(sems["ret_summed"], 1)
                elif kind == "ret_turn":
                    h = i
                    gate = R2[:, :].rearrange("p (t n) -> p t n", t=T)
                    pe.wait_ge(*due("ret_scaled", h + 1))
                    for half in range(2):
                        n = 2 * h + half
                        if n >= 2:
                            pe.wait_ge(*due("ret_lo", n - 1))
                        if half:
                            pe.wait_ge(*due("ret_decayed", min(h + 2, RET_HEADS)))
                        for f in range(2):
                            for t in range(T):
                                c0 = h * RET_DV + (2 * half + f) * P
                                ins = pe.transpose(aux[:, 1 - half, f * S + t * P:f * S + (t + 1) * P], gate[:, t, c0:c0 + P], ident)
                        own(ins, "ret_turned")
                elif kind == "scores":
                    a = i
                    if a == 0:
                        pe.wait_ge(*due("ret_lo", 8))
                        pe.wait_ge(*due("acc_read_act", MLA_COPIES - 2))
                        pe.wait_ge(*due("rot_ready", 6))
                    if a == 8:
                        pe.wait_ge(*due("rot_ready", 8))
                    if a == 16:
                        pe.wait_ge(*due("rot_ready", 10))
                    if a == 24:
                        pe.wait_ge(*due("acc_read_act", MLA_COPIES + 2 + 3 + 2))
                        pe.wait_ge(*due("normed_lo", 2))
                    if a >= 2:
                        pe.wait_ge(*due("scores_read", a - 1))
                    bank = aux[:, 3 * (a % 2), :]
                    for o0, q0, n in ((0, 0, P), (P, P, S)):
                        o = bank[:, o0:o0 + n]
                        if a < 8:
                            g, r = a // 2, 64 * (a % 2)
                            qn = R3[:, a * S:(a + 1) * S]
                            kn = R3[:, 2048 + a * S:2048 + (a + 1) * S]
                            pe.matmul(o, qn[:, q0:q0 + P], kn[:, 0:n], start=True, stop=False)
                            ins = pe.matmul(o, q_pe[r:r + 64, g, q0:q0 + P], k_pe[r:r + 64, 0, 0:n],
                                            start=False, stop=True, tile_position=(r, 0))
                        elif a < 24:
                            g, r = (a - 8) // 2, 64 * (a % 2)
                            qk = R3[:, :].rearrange("p (q g s) -> p q g s", q=2, g=8)
                            ins = pe.matmul(o, qk[r:r + 64, 0, g, q0:q0 + P], qk[r:r + 64, 1, g, 0:n],
                                            start=True, stop=True, tile_position=(r, 0))
                        else:
                            g, r = (a - 24) // 2, 64 * (a % 2)
                            qk = R3[:, 0:2048].rearrange("p (q g s) -> p q g s", q=2, g=4)
                            ins = pe.matmul(o, qk[r:r + 64, 0, g, q0:q0 + P], qk[r:r + 64, 1, g, 0:n],
                                            start=True, stop=True, tile_position=(r, 0))
                    own(ins, "scores_ready")
                elif kind == "turn":
                    a = i
                    pe.wait_ge(*due("probs_ready", a + 1))
                    if a:
                        pe.wait_ge(*due("turned_copied", a))
                    pr = probs[:, a % PROBS, :]
                    for o0, c0 in ((0, 0), (P, P), (2 * P, 2 * P)):
                        ins = pe.transpose(aux[:, 1, o0:o0 + P], pr[:, c0:c0 + P], ident)
                    own(ins, "probs_turned")
                elif kind == "values":
                    a = i
                    u = UNIT[a]
                    pe.wait_ge(*due("turned_copied", a + 1))
                    if u:
                        pe.wait_ge(*due("out_read", u))
                    if a % 8 == 0:
                        pe.wait_ge(*due("acc_read_act", MLA_COPIES + (a // 8 if a < 24 else 2 + 3 + 3)))
                    tp = turned[:, a % 2, :]
                    if a < 8:
                        v, vs, rows = R1[:, 2048:4096].rearrange("p (t n) -> p t n", t=T), slice(a * P, (a + 1) * P), slice(0, P)
                    elif a < 24:
                        h, r = a - 8, 64 * (a % 2)
                        v, vs, rows = R1[:, 0:2048].rearrange("p (t n) -> p t n", t=T), slice(h * DH, (h + 1) * DH), slice(r, r + 64)
                    else:
                        h, r = a - 24, 64 * (a % 2)
                        v, vs, rows = R3[:, 2048:3072].rearrange("p (t n) -> p t n", t=T), slice(h * DH, (h + 1) * DH), slice(r, r + 64)
                    o = aux[rows, 2, (u % 2) * S:(u % 2 + 1) * S]
                    pe.matmul(o, v[:, 0, vs], tp[:, 0:S], start=True, stop=False, skip_group_check=True)
                    pe.matmul(o[:, P:S], v[:, 1, vs], tp[:, S:3 * P], start=False, stop=True,
                              skip_group_check=True).then_inc(sems["values_ready"], 1)
                elif kind == "layer_norm" or kind == "rms_norm":
                    if kind == "layer_norm" and i == 1:
                        continue
                    pe.wait_ge(*due("normed_ready", NORM[kind, i] + 1))
                    pe.wait_ge(*due("normed_act", NORM[kind, i] + 1))
                    turn_tokens(normed, "normed_turned")
                    state["x"] += 1
                elif kind == "rank_sums":
                    pe.wait_ge(*due("squares_ready", 1))
                    pe.wait_ge(*due("ret_lo", 8))
                    sq = R3[:, 0:1024].rearrange("p (k s) -> p k s", k=4)
                    for r in range(2):
                        for t in range(T):
                            for k in range(2):
                                ins = pe.matmul(aux[:, 0, 2 * r + t:2 * r + t + 1], sq[:, 2 * r + k, t * P:(t + 1) * P],
                                                ones[:, 0:1], start=(k == 0), stop=(k == 1))
                    own(ins, "squares_summed")
                elif kind == "rank_spread":
                    pe.wait_ge(*due("diag_ready", 1))
                    own(pe.matmul(aux[:, 3, :], ones, R3[:, 1024:1536], start=True, stop=True), "ranks_spread")
                elif kind == "ssd_cums":
                    pe.wait_ge(*due("a_ready", 1))
                    a = ssd_c[:, 2, :]
                    pe.matmul(aux[:, 0, 0:32], tri, a, start=True, stop=True)
                    own(pe.matmul(aux[:, 0, 32:64], ones, a, start=True, stop=True), "cums_ready")
                elif kind == "ssd_cb":
                    pe.wait_ge(*due("silu_ready", 3))
                    for b, (s0, l0) in enumerate(((0, 0), (P, P), (0, P))):
                        for g in range(2):
                            n = 2 * b + g
                            ins = pe.matmul(aux[:, 2 + n // 4, (n % 4) * P:(n % 4 + 1) * P], b_T[:, g, s0:s0 + P],
                                            c_T[:, g, l0:l0 + P], start=True, stop=True)
                    own(ins, "cb_ready")
                elif kind == "ssd_xs":
                    pe.wait_ge(*due("edge_ready", 1) if i == 0 else due("cb_read", 1))
                    for f in range(8):
                        ins = pe.transpose(aux[:, 2 * i + f // 4, (f % 4) * P:(f % 4 + 1) * P], conv_out[:, f, i * P:(i + 1) * P], ident)
                    own(ins, "xs_turned")
                elif kind == "ssd_rows":
                    if i:
                        near(i - 1)
                    pe.wait_ge(*due("rows_ready", i + 1))
                    if i == 0:
                        pe.wait_ge(*due("xs_read", 1))
                    for q in range(2):
                        n = 2 * i + q
                        if n >= 2:
                            pe.wait_ge(*due("seg_rows", n - 1))
                        own(pe.matmul(aux[:, q, :], ones, tmp[:, q * 512:(q + 1) * 512], start=True, stop=True), "cums_ready")
                    if i == 0:
                        pe.wait_ge(*due("far_ready", 1))
                        for g in range(2):
                            ins = pe.matmul(aux[:, 2 + g, :], cb[:, 2, g, :],
                                            x_far[:, 8 * g:8 * g + 8, :].rearrange("p h n -> p (h n)"), start=True, stop=True)
                        own(ins, "y_far_ready")
                elif kind == "ssd_last":
                    near(3)
                elif kind == "ssd_turn":
                    pe.wait_ge(*due("y_gated", 1))
                    turn_tokens(R2[:, 2048:4096].rearrange("p (t n) -> p t n", t=T), "normed_turned")
                elif kind == "final":
                    pass

        def low_share(eng, own, b, src, hi, lo, hi_name, hi_base, lo_name):
            eng.wait_ge(*due(hi_name, hi_base + b + 1))
            ks = slice(2 * b, 2 * b + 2)
            own(eng.tensor_tensor(lo[:, ks, :], src[:, b * 512:(b + 1) * 512].rearrange("p (f s) -> p f s", f=2),
                                  hi[:, ks, :].bitcast(F32), ALU.subtract), lo_name)

        @block.scalar
        def _(act):
            own = Own(act, "act_own")
            act.dma_start(cols[:, 0:2], w["q_norm_even"].rearrange("a (k p) -> p (a k)", p=P), allow_slow_non_contiguous=True).then_inc(sems["cols_landed"], 16)
            act.dma_start(cols[:, 2:4], w["kv_norm_even"].rearrange("a (k p) -> p (a k)", p=P), allow_slow_non_contiguous=True).then_inc(sems["cols_landed"], 16)
            for l in range(2):
                act.dma_start(cols[:, 4 + 8 * l:12 + 8 * l], w["ln_g"][l:l + 1].rearrange("a (k p) -> p (a k)", p=P), allow_slow_non_contiguous=True).then_inc(sems["cols_landed"], 16)
                act.dma_start(cols[:, 20 + 8 * l:28 + 8 * l], w["ln_b"][l:l + 1].rearrange("a (k p) -> p (a k)", p=P), allow_slow_non_contiguous=True).then_inc(sems["cols_landed"], 16)
            for c0, name in ((36, "norm_mix_w_2"), (44, "norm_mlp_w_2"), (52, "ssd_norm_w_2")):
                act.dma_start(cols[:, c0:c0 + 8], w[name].rearrange("a (k p) -> p (a k)", p=P), allow_slow_non_contiguous=True).then_inc(sems["cols_landed"], 16)
            for s in steps:
                kind, i = s
                if kind == "piece":
                    if i.n + 2 < len(pieces):
                        hi_prep(act, own, i.n + 2)
                elif kind == "turn_x":
                    for b in range(4):
                        act.wait_ge(*due("x_turned", b + 1))
                        own(act.activation(x_hi[:, 2 * b:2 * b + 2, :], aux[:, b, :].rearrange("p (f s) -> p f s", f=2),
                                       ACT.Copy), "x_hi_ready")
                    for n in range(2):
                        hi_prep(act, own, n)
                elif kind == "trig":
                    act.wait_ge(*due("angles_ready", i + 1))
                    own(act.activation(trig[:, i, :, :], trig[:, i, :, :], ACT.Sin), "trig_ready")
                elif kind == "epi":
                    c = i
                    a2 = acc[:, c.pair, :, :]
                    if c.epilogue in ("copy_tok", "copy_feat"):
                        act.wait_ge(*due("piece_used", c.pieces[-1].n + 1))
                        own(act.activation(epi_dst(c), a2, ACT.Copy), "acc_read_act")
                    elif c.epilogue.startswith("silu"):
                        act.wait_ge(*due("piece_used", c.pieces[-1].n + 1))
                        own(act.activation(epi_dst(c), a2, ACT.Tanh, scale=0.5), "tanh_ready")
                    elif c.epilogue == "rotate" and rot_n[c.n] >= 4:
                        n = rot_n[c.n]
                        act.wait_ge(*due("piece_used", c.pieces[-1].n + 1))
                        act.wait_ge(*due("rot_ready", n if n == 5 else n - 1))
                        if n == 4:
                            act.wait_ge(*due("ret_decayed", RET_HEADS))
                        if n == 6:
                            act.wait_ge(*due("res_ready", 1))
                        m = 1 if c.width == P else 4
                        a4 = a2.rearrange("p b (f s) -> p (b f) s", s=S)
                        sw = rot_products(n)[:, 1, 0:m, :]
                        for q in range(4):
                            ins = act.activation(sw[32 * (q ^ 1):32 * (q ^ 1) + 32], a4[32 * q:32 * q + 32, 0:m, :], ACT.Copy)
                        own(ins, "rot_swapped")
                    elif c.epilogue == "keep_ranks":
                        act.wait_ge(*due("piece_used", c.pieces[-1].n + 1))
                        own(act.activation(R3[:, 0:1024].rearrange("p (b n) -> p b n", b=2), a2, ACT.Square), "squares_ready")
                        own(act.activation(R3[:, 2048:3072].rearrange("p (b n) -> p b n", b=2), a2, ACT.Copy), "acc_read_act")
                    elif c.epilogue == "conv_in":
                        act.wait_ge(*due("piece_used", c.pieces[-1].n + 1))
                        act.wait_ge(*due("pad_ready", 1))
                        for b in range(2):
                            f = c.info["dst"] + 2 * b
                            ins = act.activation(conv_in[:, f:f + 2, 3:], a2[:, b, :].rearrange("p (f s) -> p f s", f=2), ACT.Copy)
                        own(ins, "acc_read_act")
                    elif c.epilogue == "relu2":
                        n = c.info["dst"]
                        act.wait_ge(*due("piece_used", c.pieces[-1].n + 1))
                        if n:
                            act.wait_ge(*due("acc_read_dve", c.read_count - 1))
                        own(act.activation(tmp[:, 0:1024].rearrange("p (b n) -> p b n", b=2), a2, ACT.Relu), "relu_ready")
                        act.wait_ge(*due("acc_read_dve", c.read_count))
                        if n >= 4:
                            act.wait_ge(*due("piece_used", ff2_used[n - 4]))
                        own(act.activation(cat2_hi[:, 4 * (n % 4):4 * (n % 4) + 4, :].rearrange("p k s -> p (k s)"), tmp[:, 1024:2048],
                                       ACT.Copy), "ff_hi")
                elif kind == "rank_spread":
                    act.wait_ge(*due("ranks_scaled", 1))
                    own(act.activation(cat_hi[:, 20:24, :].rearrange("p k s -> p (k s)"), R3[:, 2048:3072], ACT.Copy), "ranks_hi")
                elif kind == "ret_values":
                    h = i
                    gate = R2[:, :].rearrange("p (t n) -> p t n", t=T)
                    act.wait_ge(*due("ret_centred", h + 1))
                    act.wait_ge(*due("ret_rstd", h + 1))
                    for t in range(T):
                        v = gate[:, t, h * RET_DV:(h + 1) * RET_DV]
                        ins = act.activation(v, v, ACT.Copy, scale=stats[:, 40 + 2 * (h % 2) + t:41 + 2 * (h % 2) + t])
                    own(ins, "ret_scaled")
                elif kind == "ret_turn":
                    for half in range(2):
                        n = 2 * i + half
                        act.wait_ge(*due("ret_turned", n + 1))
                        own(act.activation(cat_hi[:, 2 * n:2 * n + 2, :], aux[:, 1 - half, :].rearrange("p (f s) -> p f s", f=2),
                                       ACT.Copy), "ret_hi")
                elif kind == "scores":
                    a = i
                    act.wait_ge(*due("negmax_ready", a + 1))
                    pr = probs[:, a % PROBS, :]
                    nm, sm = soft[:, a % PROBS, 0, :], soft[:, a % PROBS, 1, :]
                    act.activation(pr[:, 0:P], pr[:, 0:P], ACT.Exp, bias=nm[:, 0:1], accum_out=sm[:, 0:1])
                    own(act.activation(pr[:, P:], pr[:, P:], ACT.Exp, bias=nm[:, 1:2], accum_out=sm[:, 1:2]), "exp_ready")
                elif kind == "turn":
                    a = i
                    act.wait_ge(*due("probs_turned", a + 1))
                    if a >= 2:
                        act.wait_ge(*due("values_ready", a - 1))
                    own(act.activation(turned[:, a % 2, :], aux[:, 1, 0:3 * P], ACT.Copy), "turned_copied")
                elif kind == "gate":
                    u = i
                    act.wait_ge(*due("out_read", u + 1))
                    b, tile = cat_place(u)
                    if u == 8:
                        act.wait_ge(*due("acc_read_dve", Y_READS[0]))
                    if u == 16:
                        act.wait_ge(*due("acc_read_dve", Y_READS[1]))
                    own(act.activation(acts[b][0][:, tile, :], gated[:, u % 2, :], ACT.Copy), "cat_hi_ready")
                elif (kind, i) == ("layer_norm", 1):
                    scratch = probs.rearrange("p a n -> p (a n)")[:, 0:D]
                    for t in range(T):
                        act.wait_ge(*due("row_added", t + 1))
                        if t:
                            own.wait()
                        own(act.activation(scratch, res[:, t, :], ACT.Square, accum_out=stats[:, 38 + t:39 + t]), "fresh_squared")
                elif kind in ("layer_norm", "rms_norm") and (kind, i) in NORM:
                    t0 = TURNS[kind, i]
                    n = {("layer_norm", 0): 0, ("rms_norm", 0): 2, ("rms_norm", 1): 3}[kind, i]
                    act.wait_ge(*due("rstd_ready", n + 1))
                    if kind == "layer_norm":
                        act.wait_ge(*due("centred", 1))
                    own(act.activation(tmp[:, D:2 * D], tmp[:, D:2 * D] if kind == "layer_norm" else res[:, 1, :], ACT.Copy,
                                       scale=stats[:, 45:46]), "normed_act")
                    for b in range(4):
                        act.wait_ge(*due("scaled_ready", t0 + b + 1))
                        own(act.activation(x_hi[:, 2 * b:2 * b + 2, :], R1[:, b * 512:(b + 1) * 512].rearrange("p (f s) -> p f s", f=2),
                                       ACT.Copy), "x_hi_ready")
                elif kind == "conv_end":
                    n = i
                    act.wait_ge(*due("conv_read", n + 1))
                    own(act.activation(conv_in[:, 4 * n:4 * n + 4, 0:S], conv_out[:, 4 * n:4 * n + 4, :], ACT.Tanh), "conv_tanh")
                elif kind == "softplus":
                    act.wait_ge(*due("dt_exp_in", 1))
                    act.wait_ge(*due("dt_landed", 48))
                    act.activation(ssd_c[:, 3, :], ssd_c[:, 3, :], ACT.Exp)
                    own(act.activation(ssd_c[:, 5, 0:16], ssd_c[:, 5, 0:16], ACT.Exp), "dt_exp")
                    act.wait_ge(*due("dt_ln_in", 1))
                    own(act.activation(ssd_c[:, 6, :], ssd_c[:, 4, :], ACT.Ln), "dt_ln")
                elif kind == "ssd_cums":
                    act.wait_ge(*due("edge_ready", 1))
                    act.activation(ssd_c[:, 7, :], ssd_c[:, 7, :], ACT.Exp)
                    own(act.activation(ssd_c[:, 8, :], ssd_c[:, 8, :], ACT.Exp), "edge_exp")
                elif kind == "ssd_rows":
                    act.wait_ge(*due("seg_ready", i + 1))
                    own(act.activation(seg[:, i % 2], seg[:, i % 2], ACT.Exp), "seg_exp")
                elif kind == "ssd_turn":
                    t0 = TURNS["ssd", 0]
                    for b in range(4):
                        act.wait_ge(*due("scaled_ready", t0 + b + 1))
                        own(act.activation(cat2_hi[:, 4 + 2 * b:6 + 2 * b, :], tmp[:, b * 512:(b + 1) * 512].rearrange("p (f s) -> p f s", f=2),
                                       ACT.Copy), "normed_hi")

        @block.vector
        def _(dve):
            own = Own(dve, "dve_own")
            rot = [0]

            def low_prep(n):
                p = pieces[n]
                if pool_share(p) == 1:
                    lo_prep(dve, own, n, 0, 1, None)
                lo_prep(dve, own, n, 2 if pool_share(p) else 0, p.nk, "lo_ready")

            def angles(n):
                dve.wait_ge(*due("pos_landed", 16))
                dve.wait_ge(*due("tables_landed", 16))
                pos = R1[:, 256:512]
                if n == 0:
                    own(dve.tensor_copy(pos, R1[:, 0:256].bitcast(I32)))
                n_turn, ang = R1[:, 512:768], R1[:, 768:1024]
                c1 = 6.28125
                c2 = float(np.float32(np.floor((TWO_PI - c1) * 2 ** 20) / 2 ** 20))
                c3 = float(np.float32(TWO_PI - c1 - c2))
                magic = 1.5 * 2 ** 23
                col = (C_FRET, C_FROPE)[n]
                own.wait()
                own(dve.tensor_scalar(ang, pos, cst[:, col:col + 1], None, ALU.mult))
                own.wait()
                own(dve.tensor_scalar(n_turn, ang, 1.0 / TWO_PI, magic, ALU.mult, ALU.add))
                own.wait()
                own(dve.tensor_scalar(n_turn, n_turn, magic, None, ALU.subtract))
                for c in (c1, c2, c3):
                    own.wait()
                    own(dve.scalar_tensor_tensor(ang, n_turn, -c, ang, ALU.mult, ALU.add))
                own.wait()
                own(dve.tensor_scalar(trig[:, n, 0, :], ang, PI_SAFE, -PI_SAFE, ALU.min, ALU.max))
                if n == 1:
                    own.wait()
                    own(dve.tensor_scalar(trig[:, n, 0, :], trig[:, n, 0, :], cst[:, C_SIGN:C_SIGN + 1], None, ALU.mult))
                own(dve.tensor_scalar(ang, ang, 0.5 * np.pi, None, ALU.add))
                own.wait()
                own(dve.tensor_scalar(n_turn, ang, np.pi, -TWO_PI, ALU.is_gt, ALU.mult))
                own.wait()
                own(dve.tensor_tensor(ang, ang, n_turn, ALU.add))
                own.wait()
                own(dve.tensor_scalar(trig[:, n, 1, :], ang, PI_SAFE, -PI_SAFE, ALU.min, ALU.max), "angles_ready")

            def row_stats(src, count, at, slot):
                st = stats[:, at:at + 6 * count]
                for m in range(count):
                    own(dve.bn_stats(st[:, 6 * m:6 * m + 6], src[:, m * 512:(m + 1) * 512]))
                own.wait()
                own(dve.bn_aggr(slot, st))

            def half_stats(half):
                for t in range(T):
                    own(dve.bn_stats(stats[:, 8 + 12 * t + 6 * half:14 + 12 * t + 6 * half], res[:, t, half * 512:(half + 1) * 512]))

            def row_rstd(kind, i, centre=True):
                n = NORM_ALL[kind, i]
                mv = stats[:, 32:36].rearrange("p (t n) -> p t n", t=T)
                if kind == "rms_norm" and i == 0:
                    dve.wait_ge(*due("fresh_squared", 2))
                    own(dve.tensor_scalar(stats[:, 36:38], stats[:, 38:40], 1.0 / D, LN_EPS, ALU.mult, ALU.add), "var_ready")
                    dve.wait_ge(*due("rstd_ready", n + 1))
                    return mv
                own.wait()
                for t in range(T):
                    own(dve.bn_aggr(mv[:, t, :], stats[:, 8 + 12 * t:20 + 12 * t]))
                own.wait()
                if kind == "layer_norm":
                    own(dve.tensor_scalar(stats[:, 36:38], mv[:, :, 1], LN_EPS, None, ALU.add), "var_ready")
                else:
                    own(dve.tensor_tensor(stats[:, 38:40], mv[:, :, 0], mv[:, :, 0], ALU.mult))
                    own.wait()
                    own(dve.scalar_tensor_tensor(stats[:, 36:38], stats[:, 38:40], LN_EPS, mv[:, :, 1], ALU.add, ALU.add), "var_ready")
                if not centre:
                    return mv
                if kind == "layer_norm":
                    own(dve.tensor_scalar(tmp[:, D:2 * D], res[:, 1, :], mv[:, 1, 0:1], None, ALU.subtract), "centred")
                dve.wait_ge(*due("rstd_ready", n + 1))
                return mv

            def full_norm(kind, i):
                mv = row_rstd(kind, i)
                for t in range(1):
                    o = tmp[:, t * D:(t + 1) * D]
                    signal = "normed_ready"
                    if kind == "layer_norm":
                        own(dve.tensor_scalar(o, res[:, t, :], mv[:, t, 0:1], stats[:, 44 + t:45 + t], ALU.subtract, ALU.mult), signal)
                    else:
                        own(dve.tensor_scalar(o, res[:, t, :], stats[:, 44 + t:45 + t], None, ALU.mult), signal)

            NORM_ALL = {("layer_norm", 0): 0, ("layer_norm", 1): 1, ("rms_norm", 0): 2, ("rms_norm", 1): 3, ("final", 0): 4}

            def scaled_split(t0, gain, offset, dst, hi, lo, hi_name, hi_base, lo_name):
                for b in range(4):
                    dve.wait_ge(*due("normed_turned", t0 + b + 1))
                    for f in range(2):
                        k = 2 * b + f
                        src = aux[:, b, f * S:(f + 1) * S]
                        o = dst[:, k * S:(k + 1) * S]
                        if offset is None:
                            own(dve.tensor_scalar(o, src, gain[:, k:k + 1], None, ALU.mult), "scaled_ready" if f else None)
                        else:
                            own(dve.tensor_scalar(o, src, gain[:, k:k + 1], offset[:, k:k + 1], ALU.mult, ALU.add), "scaled_ready" if f else None)
                    if b % 2:
                        low_share(dve, own, b - 1, dst, hi, lo, hi_name, hi_base, lo_name)

            def masked(i):
                b, g = i // 2, i % 2
                dve.wait_ge(*due("seg_exp", i + 1))
                dve.wait_ge(*due("cb_read", 1))
                own(dve.tensor_tensor(seg[:, i % 2], seg[:, i % 2], cb[:, b, g:g + 1, :].to_broadcast([P, 8, P]), ALU.mult), "m_ready")

            def finish(i):
                b, g = i // 2, i % 2
                dve.wait_ge(*due("y_near", i + 1))
                y = y_ssd[:, b, 8 * g:8 * g + 8, :].rearrange("p h n -> p (h n)")
                own(dve.tensor_tensor(y, y, aux[:, 2 + g, :], ALU.add), "y_read")
                own.wait()
                own(dve.tensor_tensor(y, y, zb[:, i * 512:(i + 1) * 512], ALU.mult))
                own.wait()
                own(dve.bn_stats(stats[:, 8 + 6 * i:14 + 6 * i], y))

            for s in steps:
                kind, i = s
                if kind == "piece":
                    last_piece = i.n
                    if i.n in waiting:
                        continue
                    if i.n + 2 < len(pieces) and i.n not in late:
                        low_prep(i.n + 2)
                elif kind == "turn_x":
                    for b in range(4):
                        dve.wait_ge(*due("x_hi_ready", b + 1))
                        dve.wait_ge(*due("x_turned", b + 1))
                        ks = slice(2 * b, 2 * b + 2)
                        ins = dve.tensor_tensor(x_lo[:, ks, :], aux[:, b, :].rearrange("p (f s) -> p f s", f=2),
                                                x_hi[:, ks, :].bitcast(F32), ALU.subtract)
                        own(ins, "x_lo_ready" if b % 2 == 0 else "x_lo_odd")
                    low_prep(0)
                    low_prep(1)
                elif kind == "trig":
                    angles(i)
                elif kind == "epi":
                    c = i
                    a2 = acc[:, c.pair, :, :]
                    if c.epilogue == "rotate":
                        n = rot_n[c.n]
                        dve.wait_ge(*due("piece_used", c.pieces[-1].n + 1))
                        dve.wait_ge(*due("trig_ready", c.info["table"] + 1))
                        pr = rot_products(n)
                        if n < 4:
                            if n >= 2:
                                dve.wait_ge(*due("rot_ready", n - 1))
                            sin = trig[:, 0, 0:1, :].to_broadcast([P, 2, S])
                            cos = trig[:, 0, 1:2, :].to_broadcast([P, 2, S])
                            first, second = a2[:, :, 0:S], a2[:, :, S:2 * S]
                            for q, (part, f) in enumerate(((first, cos), (second, sin), (second, cos), (first, sin))):
                                ins = dve.tensor_tensor(pr[:, q], part, f, ALU.mult)
                                if q < 3:
                                    own(ins)
                        else:
                            m = 1 if c.width == P else 4
                            sin = trig[:, 1, 0:1, :].to_broadcast([P, m, S])
                            cos = trig[:, 1, 1:2, :].to_broadcast([P, m, S])
                            dve.wait_ge(*due("rot_swapped", n - 3))
                            sw = pr[:, 1, 0:m, :]
                            own(dve.tensor_tensor(sw, sw, sin, ALU.mult))
                            ins = dve.tensor_tensor(pr[:, 0, 0:m, :], a2.rearrange("p b (f s) -> p (b f) s", s=S)[:, 0:m, :], cos, ALU.mult)
                        own(ins, "acc_read_dve")
                    elif c.epilogue.startswith("silu"):
                        dve.wait_ge(*due("piece_used", c.pieces[-1].n + 1))
                        dve.wait_ge(*due("tanh_ready", tanh_n[c.n]))
                        o = epi_dst(c)
                        own(dve.scalar_tensor_tensor(o, o, 1.0, a2, ALU.add, ALU.mult), "acc_read_dve")
                    elif c.epilogue in ("residual", "add"):
                        dve.wait_ge(*due("piece_used", c.pieces[-1].n + 1))
                        r = res[:, :, c.info["n"] * NCOL:(c.info["n"] + 1) * NCOL]
                        if c.acts == "cat2" and c.epilogue == "residual":
                            dve.wait_ge(*due("res_ready", 1))
                        scale = DN_ALPHA if c.epilogue == "residual" else 1.0
                        own(dve.scalar_tensor_tensor(r, r, scale, a2, ALU.mult, ALU.add), "acc_read_dve")
                        own.wait()
                        half_stats(c.info["n"])
                    elif c.epilogue == "copy_dt":
                        dve.wait_ge(*due("piece_used", c.pieces[-1].n + 1))
                        dve.wait_ge(*due("dt_landed", 48))
                        v = ssd_c[:, 0, :].rearrange("p (t n) -> p t n", t=T)
                        own(dve.tensor_tensor(v, a2[:, :, 0:16], ssd_c[:, 9, 0:16].rearrange("p (a n) -> p a n", a=1).to_broadcast([P, T, 16]),
                                          ALU.add), "acc_read_dve")
                        dve.wait_ge(*due("acc_read_dve", c.read_count))
                        own(dve.scalar_tensor_tensor(ssd_c[:, 3, :], ssd_c[:, 0, :], -1.0, ssd_c[:, 0, :], ALU.mult, ALU.min), "dt_exp_in")
                    elif c.epilogue == "relu2":
                        n = c.info["dst"]
                        dve.wait_ge(*due("piece_used", c.pieces[-1].n + 1))
                        dve.wait_ge(*due("relu_ready", n + 1))
                        if n:
                            dve.wait_ge(*due("ff_hi", n))
                            dve.wait_ge(*due("ff_lo", n))
                        own(dve.scalar_tensor_tensor(tmp[:, 1024:2048].rearrange("p (b n) -> p b n", b=2), a2, 0.0,
                                                 tmp[:, 0:1024].rearrange("p (b n) -> p b n", b=2), ALU.max, ALU.mult), "acc_read_dve")
                        dve.wait_ge(*due("ff_hi", n + 1))
                        ks = slice(4 * (n % 4), 4 * (n % 4) + 4)
                        own(dve.tensor_tensor(cat2_lo[:, ks, :].rearrange("p k s -> p (k s)"), tmp[:, 1024:2048],
                                          cat2_hi[:, ks, :].rearrange("p k s -> p (k s)").bitcast(F32), ALU.subtract), "ff_lo")
                elif kind == "rank_sums":
                    dve.wait_ge(*due("squares_summed", 1))
                    own(dve.tensor_scalar(stats[:, 46:50], aux[:, 0, 0:4], 1.0 / 256, RMS_EPS, ALU.mult, ALU.add), "mean_square")
                    dve.wait_ge(*due("rank_rstd", 1))
                    own(dve.tensor_tensor(R3[:, 1024:1536].rearrange("p (n l) -> p n l", n=4),
                                          ident.rearrange("p (a l) -> p a l", a=1).to_broadcast([P, 4, P]),
                                          stats[:, 50:54].rearrange("p (n l) -> p n l", l=1).to_broadcast([P, 4, P]), ALU.mult), "diag_ready")
                elif kind == "rank_spread":
                    dve.wait_ge(*due("ranks_spread", 1))
                    dve.wait_ge(*due("cols_landed", 16 * 9))
                    dve.wait_ge(*due("acc_read_act", 5))
                    for k in range(4):
                        v = R3[:, 2048 + k * S:2048 + (k + 1) * S]
                        own(dve.scalar_tensor_tensor(v, v, cols[:, k:k + 1], aux[:, 3, (k // 2) * S:(k // 2 + 1) * S],
                                                     ALU.mult, ALU.mult), "ranks_scaled" if k == 3 else None)
                    dve.wait_ge(*due("ranks_hi", 1))
                    own(dve.tensor_tensor(cat_lo[:, 20:24, :].rearrange("p k s -> p (k s)"), R3[:, 2048:3072],
                                          cat_hi[:, 20:24, :].rearrange("p k s -> p (k s)").bitcast(F32), ALU.subtract), "ranks_lo")
                elif kind == "ret_scores":
                    h = i
                    dve.wait_ge(*due("ret_scored", h + 1))
                    dve.wait_ge(*due("decay_landed", 16))
                    if h >= 2:
                        dve.wait_ge(*due("ret_summed", h - 1))
                    own(dve.tensor_tensor(probs[:, h % 2, :], aux[:, 0, 0:3 * P], decay[:, h, :], ALU.mult), "ret_decayed")
                elif kind == "ret_values":
                    h = i
                    gate = R2[:, :].rearrange("p (t n) -> p t n", t=T)
                    dve.wait_ge(*due("ret_summed", h + 1))
                    mv = stats[:, 32:36].rearrange("p (t n) -> p t n", t=T)
                    for t in range(T):
                        row_stats(aux[:, 2 + t, :], 1, 8 + 6 * t, mv[:, t, :])
                    own.wait()
                    own(dve.tensor_scalar(stats[:, 36 + 2 * (h % 2):38 + 2 * (h % 2)], mv[:, :, 1], LN_EPS, 4.0, ALU.add, ALU.mult), "ret_var")
                    for t in range(T):
                        v = gate[:, t, h * RET_DV:(h + 1) * RET_DV]
                        ins = dve.scalar_tensor_tensor(v, aux[:, 2 + t, :], mv[:, t, 0:1], v, ALU.subtract, ALU.mult)
                        if t == 0:
                            own(ins)
                    own(ins, "ret_centred")
                    dve.wait_ge(*due("ret_centred", h + 1))
                elif kind == "ret_turn":
                    for half in range(2):
                        n = 2 * i + half
                        dve.wait_ge(*due("ret_hi", n + 1))
                        dve.wait_ge(*due("ret_turned", n + 1))
                        own(dve.tensor_tensor(cat_lo[:, 2 * n:2 * n + 2, :], aux[:, 1 - half, :].rearrange("p (f s) -> p f s", f=2),
                                          cat_hi[:, 2 * n:2 * n + 2, :].bitcast(F32), ALU.subtract), "ret_lo")
                elif kind == "scores":
                    a = i
                    pr = probs[:, a % PROBS, :]
                    dve.wait_ge(*due("scores_ready", a + 1))
                    if a >= PROBS:
                        dve.wait_ge(*due("probs_turned", a - PROBS + 1))
                    nm = soft[:, a % PROBS, 0, :]
                    scale = (NOPE + ROPE) ** -0.5 if a < 8 else DH ** -0.5
                    bank = aux[:, 3 * (a % 2), 0:3 * P]
                    if a < 24:
                        own(dve.scalar_tensor_tensor(pr, bank, scale, causal, ALU.mult, ALU.add), "scores_read")
                    else:
                        dve.wait_ge(*due("bias_landed", 16 * BAND_HEADS))
                        dve.wait_ge(*due("half_ready", 1))
                        own(dve.scalar_tensor_tensor(pr[:, 0:P], bank[:, 0:P], scale, backwards(a - 24, P), ALU.mult, ALU.add))
                        own.wait()
                        own(dve.scalar_tensor_tensor(pr[:, P:], bank[:, P:], scale, backwards(a - 24, S), ALU.mult, ALU.add), "scores_read")
                    dve.wait_ge(*due("scores_read", a + 1))
                    own(dve.tensor_reduce(nm[:, 0:1], pr[:, 0:P], AX, ALU.max, negate=True))
                    own(dve.tensor_reduce(nm[:, 1:2], pr[:, P:], AX, ALU.max, negate=True), "negmax_ready")
                    if last_piece in waiting:
                        low_prep(last_piece + 2)
                        waiting.discard(last_piece)
                elif kind == "normalise":
                    a = i
                    pr = probs[:, a % PROBS, :]
                    sm = soft[:, a % PROBS, 1, :]
                    dve.wait_ge(*due("exp_ready", a + 1))
                    own(dve.reciprocal(sm, sm))
                    own.wait()
                    own(dve.tensor_scalar(pr[:, 0:P], pr[:, 0:P], sm[:, 0:1], None, ALU.mult))
                    own(dve.tensor_scalar(pr[:, P:], pr[:, P:], sm[:, 1:2], None, ALU.mult), "probs_ready")
                elif kind == "gate":
                    u = i
                    dve.wait_ge(*due("values_ready", LAST_OF_UNIT[u] + 1))
                    if u >= 2:
                        dve.wait_ge(*due("cat_hi_ready", u - 1))
                        dve.wait_ge(*due("cat_lo_ready", u - 1))
                    o = aux[:, 2, (u % 2) * S:(u % 2 + 1) * S]
                    if u < 16:
                        g = R1[:, u * S:(u + 1) * S] if u < 8 else R1[:, 2048 + (u - 8) * S:2048 + (u - 7) * S]
                        if u == 0 or u == 8:
                            dve.wait_ge(*due("acc_read_dve", GATE_READS[u // 8]))
                        if u == 8 + 4:
                            dve.wait_ge(*due("acc_read_dve", GATE_READS[2]))
                        own(dve.scalar_tensor_tensor(gated[:, u % 2, :], o, 0.5, g, ALU.mult, ALU.mult), "out_read")
                    else:
                        own(dve.tensor_copy(gated[:, u % 2, :], o), "out_read")
                elif kind == "low":
                    u = i
                    b, tile = cat_place(u)
                    dve.wait_ge(*due("cat_hi_ready", u + 1))
                    dve.wait_ge(*due("out_read", u + 1))
                    own(dve.tensor_tensor(acts[b][1][:, tile, :], gated[:, u % 2, :], acts[b][0][:, tile, :].bitcast(F32),
                                      ALU.subtract), "cat_lo_ready")
                elif kind == "layer_norm" and i == 0:
                    dve.wait_ge(*due("acc_read_dve", Y_READS[0]))
                    full_norm(kind, i)
                    low_prep(last_piece + 1)
                    scaled_split(0, ln_g_col[:, 0:8], ln_b_col[:, 0:8], R1, x_hi, x_lo, "x_hi_ready", 4, "x_lo_ready")
                    low_prep(last_piece + 2)
                elif kind == "layer_norm":
                    dve.wait_ge(*due("acc_read_dve", Y_READS[1]))
                    mv = row_rstd(kind, i, centre=False)
                    dve.wait_ge(*due("gb_landed", 64))
                    for t in range(T):
                        own(dve.scalar_tensor_tensor(tmp[:, t * D:(t + 1) * D], res[:, t, :], mv[:, t, 0:1], R2[:, 0:D], ALU.subtract, ALU.mult))
                    dve.wait_ge(*due("rstd_ready", 2))
                    own.wait()
                    for t in range(T):
                        own(dve.scalar_tensor_tensor(res[:, t, :], tmp[:, t * D:(t + 1) * D], stats[:, 44 + t:45 + t], R2[:, D:2 * D], ALU.mult, ALU.add),
                            "row_added")
                elif kind == "rms_norm":
                    dve.wait_ge(*due("acc_read_dve", Y_READS[1] if i == 0 else SSD_READS))
                    full_norm(kind, i)
                    low_prep(last_piece + 1)
                    scaled_split(TURNS[kind, i], mix_col if i == 0 else mlp_col, None, R1, x_hi, x_lo, "x_hi_ready",
                                 4 * (1 + NORM[kind, i]), "x_lo_ready")
                    low_prep(last_piece + 2)
                    if i == 0:
                        own(dve.memset(conv_in[:, :, 0:3], 0.0))
                        dve.wait_ge(*due("conv_landed", 16 * 5))
                        own(dve.tensor_scalar(conv_c[:, :, :], conv_c[:, :, :], 0.5, None, ALU.mult), "pad_ready")
                        dve.wait_ge(*due("bias_landed", 16 * BAND_HEADS))
                        own(dve.memset(bias[0:64, :, 0:64], NEG), "half_ready")
                    else:
                        own.wait()
                elif kind == "conv":
                    n = i
                    tiles = range(2 * n, 2 * n + 2)
                    dve.wait_ge(*due("acc_read_act", CONV_READS[n // 2]))
                    for f in tiles:
                        own(dve.tensor_scalar(conv_out[:, f, :], conv_in[:, f, 0:S], conv_c[:, 0, f:f + 1], conv_c[:, 4, f:f + 1],
                                              ALU.mult, ALU.add))
                    for tap in range(1, TAPS):
                        own.wait()
                        for f in tiles:
                            own(dve.scalar_tensor_tensor(conv_out[:, f, :], conv_in[:, f, tap:tap + S], conv_c[:, tap, f:f + 1],
                                                         conv_out[:, f, :], ALU.mult, ALU.add), "conv_read" if tap == TAPS - 1 and n % 2 and f == tiles[-1] else None)
                elif kind == "conv_end":
                    n = i
                    dve.wait_ge(*due("conv_tanh", n + 1))
                    own(dve.scalar_tensor_tensor(conv_out[:, 4 * n:4 * n + 4, :], conv_in[:, 4 * n:4 * n + 4, 0:S], 1.0,
                                                 conv_out[:, 4 * n:4 * n + 4, :], ALU.add, ALU.mult), "silu_ready")
                elif kind == "softplus":
                    e, u, t, z = ssd_c[:, 3, :], ssd_c[:, 4, :], ssd_c[:, 1, :], ssd_c[:, 7, :]
                    dve.wait_ge(*due("dt_exp", 1))
                    own(dve.tensor_scalar(u, e, 1.0, None, ALU.add), "dt_ln_in")
                    own.wait()
                    own(dve.tensor_scalar(t, u, 1.0, None, ALU.subtract))
                    own.wait()
                    own(dve.tensor_scalar(z, t, 0.0, None, ALU.is_equal))
                    own.wait()
                    own(dve.tensor_tensor(t, t, z, ALU.add))
                    own.wait()
                    own(dve.reciprocal(t, t))
                    own.wait()
                    own(dve.tensor_tensor(t, t, e, ALU.mult))
                    own(dve.tensor_tensor(z, z, e, ALU.mult))
                    dve.wait_ge(*due("dt_ln", 1))
                    own.wait()
                    own(dve.tensor_tensor(t, t, ssd_c[:, 6, :], ALU.mult))
                    own.wait()
                    own(dve.tensor_tensor(t, t, z, ALU.add))
                    own.wait()
                    own(dve.scalar_tensor_tensor(t, ssd_c[:, 0, :], 0.0, t, ALU.max, ALU.add))
                    own.wait()
                    a_row = ssd_c[:, 5, 0:16].rearrange("p (a n) -> p a n", a=1).to_broadcast([P, T, 16])
                    own(dve.scalar_tensor_tensor(ssd_c[:, 2, :].rearrange("p (t n) -> p t n", t=T), t.rearrange("p (t n) -> p t n", t=T),
                                             -1.0, a_row, ALU.mult, ALU.mult), "a_ready")
                elif kind == "ssd_cums":
                    cum, edge, far = ssd_c[:, 6, :], ssd_c[:, 7, :], ssd_c[:, 8, :]
                    dve.wait_ge(*due("cums_ready", 1))
                    own.wait()
                    own(dve.tensor_copy(cum, aux[:, 0, 0:32]))
                    own.wait()
                    own(dve.tensor_copy(edge, cum))
                    own(dve.tensor_tensor(far, aux[:, 0, 32:64], cum, ALU.subtract), "edge_ready")
                elif kind == "ssd_cb":
                    dve.wait_ge(*due("cb_ready", 1))
                    own(dve.tensor_tensor(R1[:, 3072:3584].rearrange("p (n l) -> p n l", n=4), aux[:, 2, :].rearrange("p (n l) -> p n l", n=4),
                                          tri.rearrange("p (a l) -> p a l", a=1).to_broadcast([P, 4, P]), ALU.mult))
                    own(dve.tensor_copy(R1[:, 3584:3840], aux[:, 3, 0:256]), "cb_read")
                elif kind == "ssd_xs":
                    b = i
                    dve.wait_ge(*due("xs_turned", b + 1))
                    xs = aux[:, 2 * b:2 * b + 2, :].rearrange("p c (h n) -> p (c h) n", n=SSD_P)
                    dt = ssd_c[:, 1, 16 * b:16 * b + 16].rearrange("p (h n) -> p h n", n=1).to_broadcast([P, 16, SSD_P])
                    skip = ssd_c[:, 5, 16:32].rearrange("p (h n) -> p h n", n=1).to_broadcast([P, 16, SSD_P])
                    own(dve.tensor_tensor(x_dt[:, b], xs, dt, ALU.mult))
                    own(dve.tensor_tensor(y_ssd[:, b], xs, skip, ALU.mult), "xs_read")
                    if b:
                        dve.wait_ge(*due("edge_exp", 1))
                        own.wait()
                        own(dve.tensor_tensor(x_far, x_dt[:, 0], ssd_c[:, 8, 0:16].rearrange("p (h n) -> p h n", n=1).to_broadcast([P, 16, SSD_P]),
                                              ALU.mult), "far_ready")
                elif kind == "ssd_rows":
                    b, g = i // 2, i % 2
                    cum = ssd_c[:, 6, 16 * b + 8 * g:16 * b + 8 * g + 8]
                    if i >= 2:
                        dve.wait_ge(*due("y_near", i - 1))
                    for q in range(2):
                        dve.wait_ge(*due("cums_ready", 2 + 2 * i + q))
                        own(dve.tensor_tensor(seg[:, i % 2, 4 * q:4 * q + 4, :], aux[:, q, :].rearrange("p (h n) -> p h n", h=4),
                                              cum[:, 4 * q:4 * q + 4].rearrange("p (h n) -> p h n", n=1).to_broadcast([P, 4, P]),
                                              ALU.subtract), "seg_rows")
                    own.wait()
                    own(dve.tensor_scalar(seg[:, i % 2], seg[:, i % 2], 0.0, None, ALU.min), "seg_ready")
                    if i:
                        finish(i - 1)
                    else:
                        dve.wait_ge(*due("y_far_ready", 1))
                        own(dve.tensor_tensor(y_far, aux[:, 2:4, :].rearrange("p c (h n) -> p (c h) n", n=SSD_P),
                                              ssd_c[:, 7, 16:32].rearrange("p (h n) -> p h n", n=1).to_broadcast([P, 16, SSD_P]), ALU.mult),
                            "far_read")
                        own.wait()
                        own(dve.tensor_tensor(y_ssd[:, 1], y_ssd[:, 1], y_far, ALU.add))
                    masked(i)
                elif kind == "ssd_last":
                    finish(3)
                elif kind == "ssd_gate":
                    y2 = R2[:, 2048:4096]
                    own.wait()
                    ag = ssd_c[:, 3, 0:8].rearrange("p (n v) -> p n v", v=2)
                    for n in range(4):
                        own(dve.bn_aggr(ag[:, n, :], stats[:, 8 + 6 * n:14 + 6 * n]))
                    own.wait()
                    ms = ssd_c[:, 3, 8:12]
                    own(dve.tensor_tensor(ms, ag[:, :, 0], ag[:, :, 0], ALU.mult))
                    own.wait()
                    own(dve.scalar_tensor_tensor(ms, ms, 4.0 * LN_EPS, ag[:, :, 1], ALU.add, ALU.add), "y_sq")
                    dve.wait_ge(*due("y_rstd", 1))
                    for n in range(4):
                        v = y2[:, n * 512:(n + 1) * 512]
                        own(dve.tensor_scalar(v, v, ssd_c[:, 3, 12 + n:13 + n], None, ALU.mult), "y_gated" if n == 3 else None)
                elif kind == "ssd_turn":
                    scaled_split(TURNS["ssd", 0], ssdn_col, None, tmp, cat2_hi[:, 4:12, :], cat2_lo[:, 4:12, :], "normed_hi", 0, "normed_lo")
                elif kind == "final":
                    dve.wait_ge(*due("acc_read_dve", FINAL_READS))
                    dve.wait_ge(*due("gb_landed", 80))
                    mv = row_rstd("final", 0)
                    for t in range(T):
                        own(dve.scalar_tensor_tensor(tmp[:, t * D:(t + 1) * D], res[:, t, :], stats[:, 44 + t:45 + t], R2[:, 0:D], ALU.mult, ALU.mult),
                            "final_ready")

        @block.gpsimd
        def _(pool):
            own = Own(pool, "pool_own")

            def low_prep(n):
                if pool_share(pieces[n]):
                    lo_prep(pool, own, n, 2 - pool_share(pieces[n]), 2, "lo_ready_pool")

            def inverse_root(o, i, signal):
                n = i.shape[1]
                own(pool.tensor_tensor(o, i, half_neg.to_broadcast([P, n]), ALU.pow), signal)

            own(pool.memset(half_neg, -0.5))
            pool.dma_start(R1[:, 0:256].bitcast(I32), w["positions"].to_broadcast([P, S])).then_inc(sems["pos_landed"], 16)
            pool.dma_start(tmp[:, 0:RET_HEADS * 3 * P], w["decay"]).then_inc(sems["decay_landed"], 16)
            for j, name in ((9, "dt_bias_2"), (5, "a_log_2")):
                pool.dma_start(ssd_c[:, j, 0:16], w[name].to_broadcast([P, 16])).then_inc(sems["dt_landed"], 16)
            pool.dma_start(ssd_c[:, 5, 16:32], w["d_skip_2"].to_broadcast([P, 16])).then_inc(sems["dt_landed"], 16)
            for tap in range(TAPS):
                pool.dma_start(conv_c[:, tap, :], w["conv_w_2"][tap:tap + 1, :].rearrange("a (k p) -> p (a k)", p=P), allow_slow_non_contiguous=True).then_inc(sems["conv_landed"], 16)
            pool.dma_start(conv_c[:, 4, :], w["conv_b_2"].rearrange("a (k p) -> p (a k)", p=P), allow_slow_non_contiguous=True).then_inc(sems["conv_landed"], 16)
            own.wait()
            low_prep(0)
            low_prep(1)

            def gains(l):
                pool.dma_start(R2[:, 0:1024], w["ln_g"][l:l + 1].to_broadcast([P, D])).then_inc(sems["gb_landed"], 16)
                pool.dma_start(R2[:, 1024:2048], w["ln_b"][l:l + 1].to_broadcast([P, D])).then_inc(sems["gb_landed"], 16)

            def cum_rows(i):
                if i:
                    pool.wait_ge(*due("cums_ready", 1 + 2 * i))
                else:
                    pool.wait_ge(*due("a_ready", 1))
                    pool.wait_ge(*due("normed_turned", 8))
                a = ssd_c[:, 2, 8 * i:8 * i + 8].rearrange("p (h n) -> p h n", n=1).to_broadcast([P, 8, P])
                own(pool.tensor_tensor(row_a, tri.rearrange("p (a n) -> p a n", a=1).to_broadcast([P, 8, P]), a, ALU.mult), "rows_ready")

            for s in steps:
                kind, i = s
                if kind == "piece":
                    if i.n + 2 < len(pieces):
                        low_prep(i.n + 2)
                elif kind == "epi" and i.epilogue == "rotate":
                    c = i
                    n = rot_n[c.n]
                    pool.wait_ge(*due("acc_read_dve", c.read_count))
                    pr, o = rot_products(n), rot_dst(c, n)
                    if n < 4:
                        own(pool.tensor_tensor(o[:, :, 0, :], pr[:, 0], pr[:, 1], ALU.subtract))
                        own.wait()
                        own(pool.tensor_tensor(o[:, :, 1, :], pr[:, 2], pr[:, 3], ALU.add), "rot_ready")
                        continue
                    if c.info["dst"] is None:
                        pool.wait_ge(*due("ret_turned", 8))
                    m = 1 if c.width == P else 4
                    own(pool.tensor_tensor(o, pr[:, 0, 0:m, :], pr[:, 1, 0:m, :], ALU.add), "rot_ready")
                elif kind == "ret_values":
                    h = i
                    pool.wait_ge(*due("ret_var", h + 1))
                    inverse_root(stats[:, 40 + 2 * (h % 2):42 + 2 * (h % 2)], stats[:, 36 + 2 * (h % 2):38 + 2 * (h % 2)], "ret_rstd")
                elif kind == "rank_sums":
                    pool.wait_ge(*due("mean_square", 1))
                    inverse_root(stats[:, 50:54], stats[:, 46:50], "rank_rstd")
                elif kind == "layer_norm" or kind == "rms_norm":
                    n = {("layer_norm", 0): 0, ("layer_norm", 1): 1, ("rms_norm", 0): 2, ("rms_norm", 1): 3}[kind, i]
                    pool.wait_ge(*due("var_ready", n + 1))
                    inverse_root(stats[:, 44:46], stats[:, 36:38], "rstd_ready")
                    if (kind, i) in NORM:
                        for b in (1, 3):
                            low_share(pool, own, b, R1, x_hi, x_lo, "x_hi_ready", 4 * (1 + NORM[kind, i]), "x_lo_pool")
                    if kind == "layer_norm" and i == 0:
                        pool.wait_ge(*due("normed_ready", 1))
                        pool.wait_ge(*due("gb_landed", 32))
                        v = tmp[:, :].rearrange("p (t n) -> p t n", t=T)
                        own(pool.tensor_tensor(res[:, :, :], v, R2[:, 0:1024].rearrange("p (a n) -> p a n", a=1).to_broadcast([P, T, D]), ALU.mult))
                        own.wait()
                        own(pool.tensor_tensor(res[:, :, :], res[:, :, :], R2[:, 1024:2048].rearrange("p (a n) -> p a n", a=1).to_broadcast([P, T, D]), ALU.add), "res_ready")
                    if kind == "rms_norm" and i == 1:
                        pool.wait_ge(*due("normed_turned", 16))
                        pool.dma_start(R2[:, 0:1024], w["norm_final_w_2"].to_broadcast([P, D])).then_inc(sems["gb_landed"], 16)
                elif kind == "low" and i == MLA_HEADS - 1:
                    pool.wait_ge(*due("scores_ready", MLA_HEADS))
                    gains(0)
                elif kind == "gate" and i == 10:
                    pool.wait_ge(*due("rot_ready", 10))
                    gains(1)
                elif kind == "low" and i == 8:
                    pool.wait_ge(*due("acc_read_dve", Y_READS[0]))
                    table = w["rel_bias_2"]
                    for h in range(BAND_HEADS):
                        src = bass.AP(table.tensor, h * (2 * REL_CLIP + 1) + REL_CLIP + 1 - P, [[1, P], [1, S]])
                        pool.dma_start(bias[:, h, :], src).then_inc(sems["bias_landed"], 16)
                elif kind == "ssd_cums":
                    cum_rows(0)
                elif kind == "ssd_rows" and i < 3:
                    cum_rows(i + 1)
                elif kind == "ssd_gate":
                    pool.wait_ge(*due("y_sq", 1))
                    inverse_root(ssd_c[:, 3, 12:16], ssd_c[:, 3, 8:12], "y_rstd")
                elif kind == "ssd_turn":
                    for b in (1, 3):
                        low_share(pool, own, b, tmp, cat2_hi[:, 4:12, :], cat2_lo[:, 4:12, :], "normed_hi", 0, "normed_lo_pool")
                elif kind == "final":
                    pool.wait_ge(*due("var_ready", 5))
                    inverse_root(stats[:, 44:46], stats[:, 36:38], "rstd_ready")


_NAMES = ("w_in_even", "w_uq_even", "w_ukv_even", "w_out_even", "w_in_odd", "w_out_odd", "w_in_2", "w_out_2", "w_ff1_2", "w_ff2_2")
_ROWS = ("q_norm_even", "kv_norm_even", "ln_g", "ln_b", "norm_mix_w_2", "norm_mlp_w_2", "ssd_norm_w_2", "norm_final_w_2",
         "conv_b_2", "dt_bias_2", "a_log_2", "d_skip_2", "positions")


def kernel(**inputs):
    import concourse.bacc as _bacc
    from concourse.bass_utils import run_bass_kernel_spmd as _run

    arrays = {}
    arrays["x"] = np.ascontiguousarray(inputs["x"]).reshape(S, D)
    for name in _NAMES:
        a = np.ascontiguousarray(inputs[name])
        arrays[name] = a.reshape(a.shape[-2:])
    for name in _ROWS:
        a = np.ascontiguousarray(inputs[name])
        arrays[name] = a.reshape(-1, a.shape[-1])
    arrays["conv_w_2"] = np.ascontiguousarray(inputs["conv_w_2"]).reshape(TAPS, CONV_DIM)
    arrays["rel_bias_2"] = np.ascontiguousarray(np.asarray(inputs["rel_bias_2"])[0].T)
    arrays["tables"], arrays["decay"] = shape_tables()
    nc = _bacc.Bacc("TRN2", target_bir_lowering=False, num_devices=1)
    feed, w = {}, {}
    for name, a in arrays.items():
        feed[f"in_{name}"] = a
        w[name] = nc.dram_tensor(f"in_{name}", a.shape, mybir.dt.from_np(a.dtype), kind="ExternalInput").ap()
    out = nc.dram_tensor("out", (S, D), F32, kind="ExternalOutput").ap()
    build(nc, w, out)
    r = _run(nc, [feed], core_ids=[0])
    return r.results[0]["out"].reshape(1, S, D)
```
